# Optimizing a Trainium2 kernel written in Bass

```python
import math
import jax
import jax.numpy as jnp
from jax import lax
import numpy as np

D_MODEL = 1024
BATCH = 1
SEQ = 512
DEPTH = 4
DEC_BATCH = 8
DEC_SEQ = 1
PAST_LEN = 1024
PAGE_SIZE = 128

D_INNER = 2 * D_MODEL
EPS = 1e-6
MIXER_ORDER = ('retention', 'nsa', 'gated_deltanet')

R_HEADS = 8
R_DK = D_MODEL // R_HEADS
R_DV = D_INNER // R_HEADS
R_CHUNK = 128
ROPE_BASE = 10000.0
R_IN = 2 * R_HEADS * R_DK + 2 * D_INNER

N_HEADS = 16
KV_HEADS = 4
HEAD_DIM = D_INNER // N_HEADS
CMP_LEN = 32
CMP_STRIDE = 16
CMP_HID = HEAD_DIM
SLC_BLOCK = 64
N_SELECT = 16
WINDOW = 512
Q_BLOCK = 16
NSA_KV = 2 * KV_HEADS * HEAD_DIM
NSA_IN = 2 * D_INNER + 3 * NSA_KV + 3 * N_HEADS

G_HEADS = 16
G_DK = D_INNER // G_HEADS
G_DV = D_INNER // G_HEADS
CONV_W = 4
G_CHUNK = 64
G_IN = 4 * D_INNER + 2 * G_HEADS

kernel_name = 'hybrid_retention_nsa_gdn_step'

def rms_norm(x, g):
    xf = x.astype(jnp.float32)
    y = xf * lax.rsqrt(jnp.mean(xf * xf, axis=-1, keepdims=True) + EPS)
    return (y * g.astype(jnp.float32)).astype(x.dtype)

def l2_normalize(x):
    xf = x.astype(jnp.float32)
    return xf * lax.rsqrt(jnp.sum(xf * xf, axis=-1, keepdims=True) + EPS)

def rotary(x, pos):
    half = x.shape[-1] // 2
    inv = ROPE_BASE ** (-jnp.arange(half, dtype=jnp.float32) / half)
    ang = pos.astype(jnp.float32)[:, None] * inv[None, :]
    cos, sin = jnp.cos(ang), jnp.sin(ang)
    xf = x.astype(jnp.float32)
    x1, x2 = xf[..., :half], xf[..., half:]
    return jnp.concatenate([x1 * cos - x2 * sin, x1 * sin + x2 * cos], axis=-1)

def group_norm_heads(o, g):
    of = o.astype(jnp.float32)
    xc = of - jnp.mean(of, axis=-1, keepdims=True)
    y = xc * lax.rsqrt(jnp.mean(xc * xc, axis=-1, keepdims=True) + EPS)
    return y.reshape(o.shape[0], o.shape[1], -1) * g.astype(jnp.float32)

def masked_softmax(s, mask):
    s = jnp.where(mask, s.astype(jnp.float32), -jnp.inf)
    m = jnp.max(s, axis=-1, keepdims=True)
    m = jnp.where(jnp.isfinite(m), m, 0.0)
    e = jnp.exp(s - m)
    den = jnp.sum(e, axis=-1, keepdims=True)
    return e / jnp.where(den > 0, den, 1.0)

def to_chunks(x, c, n):
    return jnp.moveaxis(x.reshape(x.shape[0], x.shape[1], n, c, *x.shape[3:]), 2, 0)

def pad_time(x, tp):
    return jnp.pad(x.astype(jnp.float32), [(0, 0), (0, 0), (0, tp - x.shape[2])] + [(0, 0)] * (x.ndim - 3))

def retention_chunked(q, k, v, log_gamma, S0):
    B, H, T, _ = q.shape
    c = min(R_CHUNK, T)
    n = -(-T // c)
    tp = n * c
    ld = jnp.where(jnp.arange(tp)[None, :] < T, log_gamma[:, None], 0.0)
    qc, kc, vc = (to_chunks(pad_time(a, tp), c, n) for a in (q, k, v))
    lc = jnp.moveaxis(ld.reshape(H, n, c), 1, 0)
    tri = jnp.tril(jnp.ones((c, c), dtype=bool))

    def step(S, inp):
        qi, ki, vi, li = inp
        g = jnp.cumsum(li, axis=-1)
        dec = jnp.exp(jnp.where(tri, g[:, :, None] - g[:, None, :], -jnp.inf))
        att = jnp.einsum('bhid,bhjd->bhij', qi, ki) * dec
        o = (jnp.einsum('bhij,bhjv->bhiv', att, vi)
             + jnp.einsum('bhid,bhdv->bhiv', qi * jnp.exp(g)[:, :, None], S))
        gl = g[:, -1]
        S = (S * jnp.exp(gl)[:, None, None]
             + jnp.einsum('bhjd,bhjv->bhdv', ki * jnp.exp(gl[:, None] - g)[:, :, None], vi))
        return S, o

    S, o = lax.scan(step, S0.astype(jnp.float32), (qc, kc, vc, lc))
    o = jnp.moveaxis(o, 0, 2).reshape(B, H, tp, -1)[:, :, :T]
    return o, S

def gated_delta_chunked(q, k, v, log_alpha, beta, S0):
    B, H, T, _ = q.shape
    dv = v.shape[-1]
    c = min(G_CHUNK, T)
    n = -(-T // c)
    tp = n * c
    qc, kc, vc, lac, bc = (to_chunks(pad_time(a, tp), c, n) for a in (q, k, v, log_alpha, beta))
    tri = jnp.tril(jnp.ones((c, c), dtype=bool))
    strict = jnp.tril(jnp.ones((c, c), dtype=bool), k=-1)

    def step(S, inp):
        qi, ki, vi, li, bi = inp
        g = jnp.cumsum(li, axis=-1)
        dec = jnp.exp(jnp.where(tri, g[..., :, None] - g[..., None, :], -jnp.inf))
        kk = jnp.einsum('bhid,bhjd->bhij', ki, ki)
        L = jnp.where(strict, bi[..., :, None] * kk * dec, 0.0)
        rhs = jnp.concatenate([vi * bi[..., None], ki * (bi * jnp.exp(g))[..., None]], axis=-1)
        sol = lax.linalg.triangular_solve(L, rhs, left_side=True, lower=True, unit_diagonal=True)
        u = sol[..., :dv] - jnp.einsum('bhik,bhkv->bhiv', sol[..., dv:], S)
        att = jnp.einsum('bhid,bhjd->bhij', qi, ki) * dec
        o = (jnp.einsum('bhid,bhdv->bhiv', qi * jnp.exp(g)[..., None], S)
             + jnp.einsum('bhij,bhjv->bhiv', att, u))
        gl = g[..., -1:]
        S = (S * jnp.exp(gl)[..., None]
             + jnp.einsum('bhjd,bhjv->bhdv', ki * jnp.exp(gl - g)[..., None], u))
        return S, o

    S, o = lax.scan(step, S0.astype(jnp.float32), (qc, kc, vc, lac, bc))
    o = jnp.moveaxis(o, 0, 2).reshape(B, H, tp, dv)[:, :, :T]
    return o, S

def selection_map(n_cmp, n_slc):
    i = np.arange(n_cmp)[:, None]
    j = np.arange(n_slc)[None, :]
    lo = np.maximum(i * CMP_STRIDE, j * SLC_BLOCK)
    hi = np.minimum(i * CMP_STRIDE + CMP_LEN, (j + 1) * SLC_BLOCK)
    return jnp.asarray(np.maximum(hi - lo, 0) / CMP_STRIDE, dtype=jnp.float32)

def retention_mixer(h, w_in, gn, w_out, S0, q0):
    B, T, _ = h.shape
    z = h @ w_in
    qk = R_HEADS * R_DK
    q = z[..., :qk].reshape(B, T, R_HEADS, R_DK).transpose(0, 2, 1, 3)
    k = z[..., qk:2 * qk].reshape(B, T, R_HEADS, R_DK).transpose(0, 2, 1, 3)
    v = z[..., 2 * qk:2 * qk + D_INNER].reshape(B, T, R_HEADS, R_DV).transpose(0, 2, 1, 3)
    gate = z[..., 2 * qk + D_INNER:]
    pos = q0 + jnp.arange(T)
    q = rotary(q, pos)
    k = rotary(k, pos) * (R_DK ** -0.5)
    log_gamma = jnp.log1p(-jnp.exp2(-5.0 - jnp.arange(R_HEADS, dtype=jnp.float32)))
    o, S = retention_chunked(q, k, v, log_gamma, S0)
    o = group_norm_heads(o.transpose(0, 2, 1, 3), gn).astype(h.dtype)
    y = (o * jax.nn.silu(gate)) @ w_out
    return y, S.astype(h.dtype)

def nsa_mixer(h, w_in, qk_norm, cmp_pe, cmp_w1, cmp_w2, w_out, q0, past_cmp, past_slc, past_win):
    B, T, _ = h.shape
    G, R, d = KV_HEADS, N_HEADS // KV_HEADS, HEAD_DIM
    z = h @ w_in
    o1 = D_INNER
    o2 = o1 + NSA_KV
    o3 = o2 + NSA_KV
    o4 = o3 + NSA_KV
    o5 = o4 + D_INNER
    q = rms_norm(z[..., :o1].reshape(B, T, G, R, d), qk_norm[0]).transpose(0, 2, 3, 1, 4)
    kv_c = z[..., o1:o2].reshape(B, T, 2, G, d)
    kv_s = z[..., o2:o3].reshape(B, T, 2, G, d)
    kv_w = z[..., o3:o4].reshape(B, T, 2, G, d)
    gate = z[..., o4:o5]
    bgate = jax.nn.sigmoid(z[..., o5:]).reshape(B, T, G, R, 3).transpose(0, 2, 3, 1, 4)
    if past_cmp is None:
        rows_c, rows_s = kv_c, kv_s
        win_pre = jnp.zeros((B, WINDOW, 2, G, d), h.dtype)
    else:
        rows_c = jnp.concatenate([past_cmp, kv_c], axis=1)
        rows_s = jnp.concatenate([past_slc, kv_s], axis=1)
        win_pre = jnp.pad(past_win, ((0, 0), (WINDOW - past_win.shape[1], 0), (0, 0), (0, 0), (0, 0)))
    tk = q0 + T

    n_cmp = (tk - CMP_LEN) // CMP_STRIDE + 1
    r = CMP_LEN // CMP_STRIDE
    ch = rows_c[:, :(n_cmp + r - 1) * CMP_STRIDE].reshape(B, n_cmp + r - 1, CMP_STRIDE, 2, G, d)
    pre = sum(jnp.einsum('bnlcgd,cldh->bncgh',
                         ch[:, j:j + n_cmp] + cmp_pe[j * CMP_STRIDE:(j + 1) * CMP_STRIDE][None, None, :, :, None, :],
                         cmp_w1[:, j * CMP_STRIDE:(j + 1) * CMP_STRIDE]) for j in range(r))
    ckv = jnp.einsum('bncgh,chd->bncgd', jax.nn.silu(pre), cmp_w2)
    ck = rms_norm(ckv[:, :, 0], qk_norm[1]).transpose(0, 2, 1, 3)
    cv = ckv[:, :, 1].transpose(0, 2, 1, 3)
    cend = jnp.arange(n_cmp) * CMP_STRIDE + CMP_LEN - 1

    n_slc = -(-tk // SLC_BLOCK)
    rs = jnp.pad(rows_s, ((0, 0), (0, n_slc * SLC_BLOCK - tk), (0, 0), (0, 0), (0, 0)))
    rs = rs.reshape(B, n_slc, SLC_BLOCK, 2, G, d)
    sk = rms_norm(rs[:, :, :, 0], qk_norm[2]).transpose(0, 3, 1, 2, 4)
    sv = rs[:, :, :, 1].transpose(0, 3, 1, 2, 4)
    smap = selection_map(n_cmp, n_slc)
    sidx = jnp.arange(n_slc)
    n_sel = min(N_SELECT, n_slc)
    gather = jax.vmap(jax.vmap(lambda blk, ix: blk[ix]))

    we = jnp.concatenate([win_pre, kv_w], axis=1)
    wk = rms_norm(we[:, :, 0], qk_norm[3]).transpose(0, 2, 1, 3)
    wv = we[:, :, 1].transpose(0, 2, 1, 3)

    qb_len = math.gcd(T, Q_BLOCK)
    scale = d ** -0.5

    def block(i):
        s0 = i * qb_len
        qb = lax.dynamic_slice_in_dim(q, s0, qb_len, axis=3)
        gb = lax.dynamic_slice_in_dim(bgate, s0, qb_len, axis=3)
        pos = q0 + s0 + jnp.arange(qb_len)
        pc = masked_softmax(jnp.einsum('bgrqd,bgnd->bgrqn', qb, ck) * scale, cend[None, :] <= pos[:, None])
        oc = jnp.einsum('bgrqn,bgnd->bgrqd', pc.astype(cv.dtype), cv)
        imp = jnp.einsum('bgrqn,ns->bgqs', pc, smap)
        cur = pos // SLC_BLOCK
        vis = sidx[None, :] <= cur[:, None]
        forced = vis & ((sidx[None, :] == 0) | (sidx[None, :] >= cur[:, None] - 1))
        imp = jnp.where(forced, jnp.inf, jnp.where(vis, imp, -jnp.inf))
        top, idx = lax.top_k(imp, n_sel)
        ks = gather(sk, idx).reshape(B, G, qb_len, n_sel * SLC_BLOCK, d)
        vs = gather(sv, idx).reshape(B, G, qb_len, n_sel * SLC_BLOCK, d)
        kpos = idx[..., None] * SLC_BLOCK + jnp.arange(SLC_BLOCK)
        ms = (top[..., None] > -jnp.inf) & (kpos <= pos[None, None, :, None, None])
        ms = ms.reshape(B, G, qb_len, n_sel * SLC_BLOCK)[:, :, None]
        ps = masked_softmax(jnp.einsum('bgrqd,bgqkd->bgrqk', qb, ks) * scale, ms)
        os_ = jnp.einsum('bgrqk,bgqkd->bgrqd', ps.astype(vs.dtype), vs)
        kw = lax.dynamic_slice_in_dim(wk, s0, WINDOW + qb_len, axis=2)
        vw = lax.dynamic_slice_in_dim(wv, s0, WINDOW + qb_len, axis=2)
        wpos = q0 + s0 - WINDOW + jnp.arange(WINDOW + qb_len)
        mw = (wpos[None, :] >= 0) & (wpos[None, :] <= pos[:, None]) & (wpos[None, :] >= pos[:, None] - WINDOW)
        pw = masked_softmax(jnp.einsum('bgrqd,bgkd->bgrqk', qb, kw) * scale, mw)
        ow = jnp.einsum('bgrqk,bgkd->bgrqd', pw.astype(vw.dtype), vw)
        return gb[..., 0:1] * oc + gb[..., 1:2] * os_ + gb[..., 2:3] * ow

    o = lax.map(block, jnp.arange(T // qb_len))
    o = o.transpose(1, 0, 4, 2, 3, 5).reshape(B, T, D_INNER)
    y = (o * jax.nn.silu(gate)) @ w_out
    if past_win is None:
        win_state = kv_w[:, max(0, T - WINDOW):]
    else:
        win_state = we[:, we.shape[1] - past_win.shape[1]:]
    return y, kv_c, kv_s, win_state

def gdn_mixer(h, w_in, conv_w, A_log, dt_bias, onorm, w_out, conv0, S0):
    B, T, _ = h.shape
    z = h @ w_in
    c3 = 3 * D_INNER
    qkv = z[..., :c3]
    gate = z[..., c3:c3 + D_INNER]
    a = z[..., c3 + D_INNER:c3 + D_INNER + G_HEADS]
    b = z[..., c3 + D_INNER + G_HEADS:]
    ext = jnp.concatenate([conv0, qkv], axis=1)
    conv = sum(ext[:, j:j + T] * conv_w[j] for j in range(CONV_W))
    qkv = jax.nn.silu(conv)
    new_conv = ext[:, T:]
    q = l2_normalize(qkv[..., :D_INNER].reshape(B, T, G_HEADS, G_DK)) * (G_DK ** -0.5)
    k = l2_normalize(qkv[..., D_INNER:2 * D_INNER].reshape(B, T, G_HEADS, G_DK))
    v = qkv[..., 2 * D_INNER:].reshape(B, T, G_HEADS, G_DV)
    beta = jax.nn.sigmoid(b.astype(jnp.float32))
    log_alpha = -jnp.exp(A_log.astype(jnp.float32)) * jax.nn.softplus(a.astype(jnp.float32) + dt_bias.astype(jnp.float32))
    o, S = gated_delta_chunked(q.transpose(0, 2, 1, 3), k.transpose(0, 2, 1, 3), v.transpose(0, 2, 1, 3),
                               log_alpha.transpose(0, 2, 1), beta.transpose(0, 2, 1), S0)
    o = rms_norm(o.transpose(0, 2, 1, 3), onorm).reshape(B, T, D_INNER).astype(h.dtype)
    y = (o * jax.nn.silu(gate)) @ w_out
    return y, new_conv, S.astype(h.dtype)

def setup_inputs(seed: int = 0) -> dict:
    key = jax.random.key(seed)
    keys = iter(jax.random.split(key, 64))
    nk = lambda: next(keys)
    f32 = jnp.float32
    n_pages = PAST_LEN // PAGE_SIZE
    n_pool = (DEC_BATCH * n_pages * 5) // 4
    win_keep = min(WINDOW, PAST_LEN)

    def w(shape, fan_in):
        return jax.random.normal(nk(), shape, f32) * fan_in ** -0.5

    def gain(shape):
        return 1.0 + 0.02 * jax.random.normal(nk(), shape, f32)

    x_prompt = jax.random.normal(nk(), (BATCH, SEQ, D_MODEL), f32)
    x_sample = jax.random.normal(nk(), (DEC_BATCH, DEC_SEQ, D_MODEL), f32)
    state_l0_ret = 0.5 * jax.random.normal(nk(), (DEC_BATCH, R_HEADS, R_DK, R_DV), f32)
    cache_l1_cmp = jax.random.normal(nk(), (n_pool, PAGE_SIZE, 2, KV_HEADS, HEAD_DIM), f32)
    cache_l1_slc = jax.random.normal(nk(), (n_pool, PAGE_SIZE, 2, KV_HEADS, HEAD_DIM), f32)
    state_l1_win = jax.random.normal(nk(), (DEC_BATCH, win_keep, 2, KV_HEADS, HEAD_DIM), f32)
    state_l2_conv = jax.random.normal(nk(), (DEC_BATCH, CONV_W - 1, 3 * D_INNER), f32)
    state_l2_gdn = 0.1 * jax.random.normal(nk(), (DEC_BATCH, G_HEADS, G_DK, G_DV), f32)
    state_l3_ret = 0.5 * jax.random.normal(nk(), (DEC_BATCH, R_HEADS, R_DK, R_DV), f32)
    page_table = jax.random.permutation(nk(), n_pool)[:DEC_BATCH * n_pages].reshape(DEC_BATCH, n_pages).astype(jnp.int32)

    dt = jnp.exp(jax.random.uniform(nk(), (G_HEADS,), f32, math.log(1e-3), math.log(1e-1)))
    return {
        'x_prompt': x_prompt, 'x_sample': x_sample,
        'state_l0_ret': state_l0_ret, 'cache_l1_cmp': cache_l1_cmp, 'cache_l1_slc': cache_l1_slc,
        'state_l1_win': state_l1_win, 'state_l2_conv': state_l2_conv, 'state_l2_gdn': state_l2_gdn,
        'state_l3_ret': state_l3_ret, 'page_table': page_table,
        'l0_norm': gain((D_MODEL,)), 'l0_w_in': w((D_MODEL, R_IN), D_MODEL),
        'l0_gn': gain((D_INNER,)), 'l0_w_out': w((D_INNER, D_MODEL), D_INNER),
        'l1_norm': gain((D_MODEL,)), 'l1_w_in': w((D_MODEL, NSA_IN), D_MODEL),
        'l1_qk_norm': gain((4, HEAD_DIM)),
        'l1_cmp_pe': 0.02 * jax.random.normal(nk(), (CMP_LEN, 2, HEAD_DIM), f32),
        'l1_cmp_w1': w((2, CMP_LEN, HEAD_DIM, CMP_HID), CMP_LEN * HEAD_DIM),
        'l1_cmp_w2': w((2, CMP_HID, HEAD_DIM), CMP_HID),
        'l1_w_out': w((D_INNER, D_MODEL), D_INNER),
        'l2_norm': gain((D_MODEL,)), 'l2_w_in': w((D_MODEL, G_IN), D_MODEL),
        'l2_conv_w': w((CONV_W, 3 * D_INNER), CONV_W),
        'l2_A_log': jnp.log(jax.random.uniform(nk(), (G_HEADS,), f32, 1.0, 16.0)),
        'l2_dt_bias': dt + jnp.log(-jnp.expm1(-dt)),
        'l2_onorm': gain((G_DV,)), 'l2_w_out': w((D_INNER, D_MODEL), D_INNER),
        'l3_norm': gain((D_MODEL,)), 'l3_w_in': w((D_MODEL, R_IN), D_MODEL),
        'l3_gn': gain((D_INNER,)), 'l3_w_out': w((D_INNER, D_MODEL), D_INNER),
    }

def reference(x_prompt, x_sample, state_l0_ret, cache_l1_cmp, cache_l1_slc, state_l1_win, state_l2_conv,
              state_l2_gdn, state_l3_ret, page_table,
              l0_norm, l0_w_in, l0_gn, l0_w_out,
              l1_norm, l1_w_in, l1_qk_norm, l1_cmp_pe, l1_cmp_w1, l1_cmp_w2, l1_w_out,
              l2_norm, l2_w_in, l2_conv_w, l2_A_log, l2_dt_bias, l2_onorm, l2_w_out,
              l3_norm, l3_w_in, l3_gn, l3_w_out):
    B = x_prompt.shape[0]
    DB = x_sample.shape[0]
    layer_params = {
        0: (l0_norm, l0_w_in, l0_gn, l0_w_out),
        1: (l1_norm, l1_w_in, l1_qk_norm, l1_cmp_pe, l1_cmp_w1, l1_cmp_w2, l1_w_out),
        2: (l2_norm, l2_w_in, l2_conv_w, l2_A_log, l2_dt_bias, l2_onorm, l2_w_out),
        3: (l3_norm, l3_w_in, l3_gn, l3_w_out),
    }
    ret_state = {0: state_l0_ret, 3: state_l3_ret}
    new = {}
    xp, xs = x_prompt, x_sample
    for i in range(DEPTH):
        kind = MIXER_ORDER[i % len(MIXER_ORDER)]
        norm, *w = layer_params[i]
        hp, hs = rms_norm(xp, norm), rms_norm(xs, norm)
        if kind == 'retention':
            yp, sp = retention_mixer(hp, *w, jnp.zeros((B, R_HEADS, R_DK, R_DV), jnp.float32), 0)
            ys, ss = retention_mixer(hs, *w, ret_state[i], PAST_LEN)
            new[i] = (sp, ss)
        elif kind == 'nsa':
            past_c = cache_l1_cmp[page_table].reshape(DB, -1, 2, KV_HEADS, HEAD_DIM)
            past_s = cache_l1_slc[page_table].reshape(DB, -1, 2, KV_HEADS, HEAD_DIM)
            yp, cp, slp, wp = nsa_mixer(hp, *w, 0, None, None, None)
            ys, cs, sls, ws = nsa_mixer(hs, *w, PAST_LEN, past_c, past_s, state_l1_win)
            new[i] = (cp, cs, slp, sls, wp, ws)
        else:
            yp, cvp, gp = gdn_mixer(hp, *w, jnp.zeros((B, CONV_W - 1, 3 * D_INNER), x_prompt.dtype),
                                    jnp.zeros((B, G_HEADS, G_DK, G_DV), jnp.float32))
            ys, cvs, gs = gdn_mixer(hs, *w, state_l2_conv, state_l2_gdn)
            new[i] = (cvp, cvs, gp, gs)
        xp, xs = xp + yp, xs + ys
    return (xp, xs,
            new[0][0], new[0][1],
            new[1][0], new[1][1], new[1][2], new[1][3], new[1][4], new[1][5],
            new[2][0], new[2][1], new[2][2], new[2][3],
            new[3][0], new[3][1])


_drawn_inputs = setup_inputs


def setup_inputs(seed=0):
    import zlib

    import numpy as np

    out = dict(_drawn_inputs(seed))
    spreads = {}
    factors = {'cache_l1_slc': 3.378,
     'l0_gn': 3.425,
     'l1_norm': 2.835,
     'l1_qk_norm': 8.0,
     'l1_cmp_pe': 8.0,
     'l2_onorm': 23.794,
     'l3_gn': 30.773}
    for name, (base, spread) in spreads.items():
        noise = np.random.default_rng([zlib.crc32(name.encode()), seed]).standard_normal(out[name].shape)
        drawn = base * np.exp(spread * noise) if base else spread * noise
        out[name] = jnp.asarray(drawn.astype(out[name].dtype))
    for name, factor in factors.items():
        out[name] = (out[name] * factor).astype(out[name].dtype)
    return out
```

```python
from contextlib import ExitStack

import numpy as np
import concourse.bass as bass
from concourse import mybir

F32 = mybir.dt.float32
I32 = mybir.dt.int32
ALU = mybir.AluOpType
ACT = mybir.ActivationFunctionType
AX = mybir.AxisListType.X

P = 128
DM = 1024
KM = DM // P
DI = 2 * DM
KI = DI // P
SEQ = 512
NT = SEQ // P
DB = 8
TT = NT + 1
TOK = SEQ + DB
EPS = 1e-6
NEG = -1e30

RH, RK, RV = 8, 128, 256
NH, KVH, HD = 16, 4, 128
HPG = NH // KVH
CL, CS = 32, 16
GH = 16
LAYERS = 4


class Mem:
    pass


class Stage(ExitStack):

    def __init__(self, nc):
        super().__init__()
        self.nc, self.sems = nc, []
        self.callback(self.clear)

    def sem(self, name):
        self.sems.append(self.nc.alloc_semaphore(name))
        return self.sems[-1]

    def clear(self):
        self.nc.clear_and_free_semaphores(self.sems)
        self.nc.all_engine_barrier()


def row(ap):
    return ap.rearrange("a p n -> p (a n)")


def load_tokens(nc, m):
    with Stage(nc) as ctx:
        zeroed = ctx.sem("zeroed")
        loaded = ctx.sem("loaded")
        block = ctx.enter_context(nc.Block())

        @block.vector
        def _(dve):
            nc.vector.memset(m.xres[:, NT, :], 0.0).then_inc(zeroed, 1)

        @block.sync
        def _(sp):
            sp.dma_start(m.xres[:, 0:NT, :], m.x_prompt.rearrange("b (t p) d -> p (b t) d", p=P)).then_inc(loaded, 16)
            sp.dma_start(m.ident[:], m.c_ident).then_inc(loaded, 16)
            sp.wait_ge(zeroed, 1)
            sp.dma_start(m.xres[0:DB, NT, :], m.x_sample.rearrange("b s d -> (b s) d")).then_inc(loaded, 16)
            sp.wait_ge(loaded, 48)


def norm_and_transpose(nc, m, layer):
    with Stage(nc) as ctx:
        sb = lambda n, s: ctx.enter_context(nc.sbuf_tensor(f"n{layer}_{n}", s, F32))
        sem = lambda n: ctx.sem(f"n{layer}_{n}")
        gain = sb("gain", [P, DM])
        squares = sb("squares", [P, 2, DM])
        normed = sb("normed", [P, 2, DM])
        sumsq = sb("sumsq", [P, TT])
        ms = sb("ms", [P, TT])
        rms = sb("rms", [P, TT])
        rinv = sb("rinv", [P, TT])
        tp = ctx.enter_context(nc.psum_tensor(f"n{layer}_tp", [P, 2, KM, P], F32))
        gain_in, sums_ready, ms_ready, rms_ready = sem("gain_in"), sem("sums"), sem("ms"), sem("rms")
        normed_ready, tp_ready, tp_used = sem("normed"), sem("tp_ready"), sem("tp_used")
        block = ctx.enter_context(nc.Block())

        @block.sync
        def _(sp):
            g = m.norm[layer].rearrange("(o d) -> o d", o=1)
            sp.dma_start(gain[:], g.to_broadcast([P, DM])).then_inc(gain_in, 16)

        @block.scalar
        def _(act):
            for t in range(TT):
                if t >= 2:
                    act.wait_ge(sums_ready, t - 1)
                nc.scalar.activation(squares[:, t % 2], m.xres[:, t], ACT.Square,
                                     accum_out=sumsq[:, t:t + 1]).then_inc(sums_ready, 1)
            act.wait_ge(ms_ready, 1)
            nc.scalar.activation(rms[:], ms[:], ACT.Sqrt).then_inc(rms_ready, 1)
            for t in range(TT):
                act.wait_ge(tp_ready, t + 1)
                n = P if t < NT else DB
                nc.scalar.copy(m.hT[:, :, t * P:t * P + n], tp[:, t % 2, :, 0:n]).then_inc(tp_used, 1)

        @block.vector
        def _(dve):
            dve.wait_ge(sums_ready, TT)
            nc.vector.tensor_scalar(ms[:], sumsq[:], 1.0 / DM, EPS, ALU.mult, ALU.add).then_inc(ms_ready, 1)
            dve.wait_ge(rms_ready, 1)
            nc.vector.reciprocal(rinv[:], rms[:])
            dve.drain()
            dve.wait_ge(gain_in, 16)
            for t in range(TT):
                if t >= 2:
                    dve.wait_ge(tp_ready, t - 1)
                nc.vector.scalar_tensor_tensor(normed[:, t % 2], m.xres[:, t], rinv[:, t:t + 1], gain[:],
                                               ALU.mult, ALU.mult).then_inc(normed_ready, 1)

        @block.tensor
        def _(pe):
            for t in range(TT):
                pe.wait_ge(normed_ready, t + 1)
                if t >= 2:
                    pe.wait_ge(tp_used, t - 1)
                for k in range(KM):
                    last = nc.tensor.transpose(tp[:, t % 2, k], normed[:, t % 2, k * P:(k + 1) * P], m.ident[:])
                last.then_inc(tp_ready, 1)


def output_projection(nc, m, layer):
    HALF, QUARTER = DM // 2, DM // 4
    with Stage(nc) as ctx:
        sem = lambda n: ctx.sem(f"o{layer}_{n}")
        w = ctx.enter_context(nc.sbuf_tensor(f"o{layer}_w", [P, 2, KI, HALF], F32))
        acc = ctx.enter_context(nc.psum_tensor(f"o{layer}_acc", [P, 4, HALF], F32))
        accs = ctx.enter_context(nc.psum_tensor(f"o{layer}_accs", [P, QUARTER], F32))
        w_in = [sem(f"w_in{i}") for i in range(4)]
        y_ready, y_added = sem("y_ready"), sem("y_added")
        block = ctx.enter_context(nc.Block())
        wv = m.w_out[layer].rearrange("(k p) n -> p k n", p=P)

        @block.sync
        def _(sp):
            for i in range(4):
                half, kk = i // 2, (i % 2) * (KI // 2)
                sp.dma_start(w[:, half, kk:kk + KI // 2, :],
                             wv[:, kk:kk + KI // 2, half * HALF:(half + 1) * HALF]).then_inc(w_in[i], 16)

        @block.tensor
        def _(pe):
            for half in range(2):
                for t in range(NT):
                    n = half * NT + t
                    if n >= 4:
                        pe.wait_ge(y_added, n - 3)
                    for k in range(KI):
                        if t == 0 and k % (KI // 2) == 0:
                            pe.wait_ge(w_in[2 * half + k // (KI // 2)], 16)
                        last = nc.tensor.matmul(acc[:, n % 4, :], m.ogT[:, k, t * P:(t + 1) * P], w[:, half, k, :],
                                                start=(k == 0), stop=(k == KI - 1))
                    last.then_inc(y_ready, 1)
            for k in range(KI):
                for j in range(4):
                    last = nc.tensor.matmul(accs[32 * j:32 * j + DB], m.ogT[:, k, SEQ:TOK],
                                            w[:, j // 2, k, j % 2 * QUARTER:(j % 2 + 1) * QUARTER],
                                            start=(k == 0), stop=(k == KI - 1))
            last.then_inc(y_ready, 1)

        @block.vector
        def _(dve):
            for half in range(2):
                for t in range(NT):
                    n = half * NT + t
                    x = m.xres[:, t, half * HALF:(half + 1) * HALF]
                    dve.wait_ge(y_ready, n + 1)
                    nc.vector.tensor_tensor(x, x, acc[:, n % 4, :], ALU.add).then_inc(y_added, 1)
            dve.wait_ge(y_ready, 2 * NT + 1)
            for j in range(4):
                x = m.xres[0:DB, NT, j * QUARTER:(j + 1) * QUARTER]
                nc.vector.tensor_tensor(x, x, accs[32 * j:32 * j + DB], ALU.add)


def store_tokens(nc, m):
    with Stage(nc) as ctx:
        stored = ctx.sem("stored")
        block = ctx.enter_context(nc.Block())

        @block.sync
        def _(sp):
            sp.dma_start(m.y_prompt.rearrange("b (t p) d -> p (b t) d", p=P), m.xres[:, 0:NT, :]).then_inc(stored, 16)
            sp.dma_start(m.y_sample.rearrange("b s d -> (b s) d"), m.xres[0:DB, NT, :]).then_inc(stored, 16)
            sp.wait_ge(stored, 32)


RW = 2 * RK + 2 * RV
RC = 2 * P + 3 + 2


def retention(nc, m, layer, state_in, state_prompt, state_sample, w_heads, head_consts):
    with Stage(nc) as ctx:
        sb = lambda n, s: ctx.enter_context(nc.sbuf_tensor(f"r{layer}_{n}", s, F32))
        ps = lambda n: ctx.enter_context(nc.psum_tensor(f"r{layer}_{n}", [P, 512], F32))
        sem = lambda n: ctx.sem(f"r{layer}_{n}")
        w = sb("w", [P, 2, KM, RW])
        hc = sb("hc", [P, 2, RC])
        rope = sb("rope", [P, TT, 2, 2 * RK])
        d8 = sb("d8", [P, DB, DB])
        e8 = sb("e8", [DB, DB, P])
        state = sb("state", [P, 2, DB, RV])
        rot = sb("rot", [P, TT, 2 * RK])
        t1 = sb("t1", [P, 2, 2 * RK])
        t2 = sb("t2", [P, 2, 2 * RK])
        z = sb("z", [P, TT, 512])
        v = z[:, :, 2 * RK:512]
        sgT = sb("sgT", [P, 2, TOK])
        gs = sb("gs", [DB, 2, P])
        qT = sb("qT", [P, NT, P])
        kT = sb("kT", [P, NT, P])
        qgT = sb("qgT", [P, NT, P])
        kd = sb("kd", [P, NT, RK])
        km = sb("km", [DB, DB, RK])
        qm = sb("qm", [P, DB, DB])
        qs = sb("qs", [P, DB])
        att = sb("att", [P, NT, P])
        S = sb("S", [P, NT, RV])
        stats = sb("stats", [P, TT, 6])
        mv = sb("mv", [P, TT, 2])
        var = sb("var", [P, TT])
        sd = sb("sd", [P, TT])
        rs = sb("rs", [P, TT])
        y = sb("y", [P, TT, RV])
        Z = [ps("Z0"), ps("Z1")]
        G = [ps("G0"), ps("G1")]
        GS = ps("GS")
        T = [ps("T0"), ps("T1"), ps("T2")]
        OUT = [T[1], T[2], G[0], G[1]]
        w_in, hc_in = [sem("w_in0"), sem("w_in1")], [sem("hc_in0"), sem("hc_in1")]
        st_in, st_out = [sem("st_in0"), sem("st_in1")], [sem("st_out0"), sem("st_out1")]
        c_in, z_ready, z_v = sem("c_in"), sem("z_ready"), sem("z_v")
        gate_ready, gate_used, qk_ready, q_copied, k_copied = (sem("gate_ready"), sem("gate_used"), sem("qk_ready"),
                                                               sem("q_copied"), sem("k_copied"))
        rot_ready, kd_ready, qm_ready, qg_ready = sem("rot_ready"), sem("kd_ready"), sem("qm_ready"), sem("qg_ready")
        sup_ready, S_ready, att_ready, att_masked = sem("sup_ready"), sem("S_ready"), sem("att_ready"), sem("att_masked")
        outer_ready, state_new, o_ready, os_ready = sem("outer_ready"), sem("state_new"), sem("o_ready"), sem("os_ready")
        var_ready, sd_ready, y_ready, yT_ready, og_ready = (sem("var_ready"), sem("sd_ready"), sem("y_ready"),
                                                            sem("yT_ready"), sem("og_ready"))
        S_out = sem("S_out")
        block = ctx.enter_context(nc.Block())

        def heads(eng, body):
            with eng.Fori(0, RH // 2) as pair:
                for s in range(2):
                    body(pair, s, 2 * pair + s)

        @block.sync
        def _(sp):
            sp.dma_start(rope[:], m.c_rope).then_inc(c_in, 16)
            sp.dma_start(d8[:], m.c_d8).then_inc(c_in, 16)
            sp.dma_start(e8[:], m.c_e8).then_inc(c_in, 16)

            for s in range(2):
                sp.dma_start(w[:, s], w_heads[s]).then_inc(w_in[s], 16)
                sp.dma_start(hc[:, s], head_consts[s]).then_inc(hc_in[s], 16)
                sp.dma_start(state[:, s], state_in[:, s].rearrange("b k v -> k b v")).then_inc(st_in[s], 16)
            with sp.Fori(0, RH // 2 - 1) as pair:
                for s in range(2):
                    h = 2 * pair + s
                    sp.wait_ge(gate_ready, h + 1)
                    sp.dma_start(w[:, s], row4(w_heads[bass.ds(h + 2, 1)])).then_inc(w_in[s], 16)
                    sp.wait_ge(state_new, h + 1)
                    sp.dma_start(state_sample[:, bass.ds(h, 1)].rearrange("b a k v -> k (b a) v"),
                                 state[:, s]).then_inc(st_out[s], 16)
                    sp.wait_ge(S_ready, h + 1)
                    sp.dma_start(row(state_prompt[0, bass.ds(h, 1)]), S[:, NT - 1]).then_inc(S_out, 16)
                    sp.wait_ge(st_out[s], pair * 16 + 16)
                    sp.wait_ge(os_ready, h + 1)
                    sp.dma_start(state[:, s], state_in[:, bass.ds(h + 2, 1)].rearrange("b a k v -> k (b a) v")
                                 ).then_inc(st_in[s], 16)
                    sp.wait_ge(og_ready, h + 1)
                    sp.dma_start(hc[:, s], row(head_consts[bass.ds(h + 2, 1)])).then_inc(hc_in[s], 16)
            for s in range(2):
                h = RH - 2 + s
                sp.wait_ge(state_new, h + 1)
                sp.dma_start(state_sample[:, h].rearrange("b k v -> k b v"), state[:, s]).then_inc(st_out[s], 16)
                sp.wait_ge(S_ready, h + 1)
                sp.dma_start(state_prompt[0, h], S[:, NT - 1]).then_inc(S_out, 16)
                sp.wait_ge(st_out[s], 16 * (RH // 2))
            sp.wait_ge(S_out, 16 * RH)

        @block.tensor
        def _(pe):
            def head(pair, s, h):
                pe.wait_ge(w_in[s], pair * 16 + 16)
                pe.wait_ge(y_ready, h)
                for t in range(NT):
                    if t >= 2:
                        pe.wait_ge(z_v, h * TT + t - 1)
                    for k in range(KM):
                        last = nc.tensor.matmul(Z[t % 2][:], m.hT[:, k, t * P:(t + 1) * P], w[:, s, k, 0:512],
                                                start=(k == 0), stop=(k == KM - 1))
                    last.then_inc(z_ready, 1)
                for first, groups in ((0, 4), (4, 2)):
                    for k in range(KM):
                        for j in range(groups):
                            last = nc.tensor.matmul(GS[32 * j:32 * j + DB, first * 32:first * 32 + P],
                                                    m.hT[:, k, SEQ:TOK], w[:, s, k, (first + j) * P:(first + j + 1) * P],
                                                    start=(k == 0), stop=(k == KM - 1))
                last.then_inc(z_ready, 1)
                for f in range(2):
                    for k in range(KM):
                        nc.tensor.matmul(G[f][:], w[:, s, k, 512 + f * P:512 + (f + 1) * P], m.hT[:, k, 0:SEQ],
                                         start=(k == 0), stop=(k == KM - 1))
                pe.wait_ge(w_in[0], 16)
                pe.wait_ge(z_v, h * TT + TT)
                for f in range(2):
                    last = nc.tensor.matmul(GS[:, 2 * P + f * DB:2 * P + (f + 1) * DB], gs[:, f], m.ident[0:DB, 0:DB],
                                            start=True, stop=True)
                last.then_inc(gate_ready, 1)
                pe.wait_ge(rot_ready, h + 1)
                pe.wait_ge(og_ready, h)
                for c in range(NT):
                    nc.tensor.transpose(T[0][:, c * P:(c + 1) * P], rot[:, c, 0:RK], m.ident[:])
                    nc.tensor.transpose(T[1][:, c * P:(c + 1) * P], rot[:, c, RK:2 * RK], m.ident[:])
                nc.tensor.transpose(T[2][:, 0:DB], rot[0:DB, NT, 0:RK], m.ident[0:DB, 0:DB]).then_inc(qk_ready, 1)
                pe.wait_ge(kd_ready, h + 1)
                pe.wait_ge(k_copied, h + 1)
                pe.wait_ge(qg_ready, h + 1)
                pe.wait_ge(z_v, h * TT + TT)
                for c in range(NT):
                    last = nc.tensor.matmul(T[1 + c // 2][:, (c % 2) * RV:(c % 2 + 1) * RV], kd[:, c], v[:, c],
                                            start=True, stop=True)
                last.then_inc(sup_ready, 1)
                pe.wait_ge(q_copied, h + 1)
                for c in range(NT):
                    last = nc.tensor.matmul(T[0][:, c * P:(c + 1) * P], kT[:, c], qT[:, c], start=True, stop=True)
                last.then_inc(att_ready, 1)
                pe.wait_ge(S_ready, h + 1)
                pe.wait_ge(gate_used, h + 1)
                for b in range(DB):
                    last = nc.tensor.matmul(OUT[b // 2][:, (b % 2) * RV:(b % 2 + 1) * RV], km[:, b], v[0:DB, NT],
                                            start=True, stop=True)
                last.then_inc(outer_ready, 1)
                pe.wait_ge(att_masked, h + 1)
                pe.wait_ge(z_v, h * TT + TT)
                for c in range(NT):
                    o = Z[c // 2][:, (c % 2) * RV:(c % 2 + 1) * RV]
                    last = nc.tensor.matmul(o, att[:, c], v[:, c], start=True, stop=(c == 0))
                    if c > 0:
                        last = nc.tensor.matmul(o, qgT[:, c], S[:, c - 1], start=False, stop=True)
                last.then_inc(o_ready, 1)
                pe.wait_ge(state_new, h + 1)
                pe.wait_ge(qm_ready, h + 1)
                for b in range(DB):
                    last = nc.tensor.matmul(GS[0:DB, 0:RV], qm[:, b], state[:, s, b], start=(b == 0), stop=(b == DB - 1))
                last.then_inc(os_ready, 1)
                pe.wait_ge(y_ready, h + 1)
                for f in range(2):
                    for c in range(NT):
                        nc.tensor.transpose(T[f][:, c * P:(c + 1) * P], y[:, c, f * P:(f + 1) * P], m.ident[:])
                    last = nc.tensor.transpose(T[2][:, f * DB:(f + 1) * DB], y[0:DB, NT, f * P:(f + 1) * P],
                                               m.ident[0:DB, 0:DB])
                last.then_inc(yT_ready, 1)

            heads(pe, head)

        @block.scalar
        def _(act):
            def head(pair, s, h):
                for t in range(NT):
                    act.wait_ge(z_ready, h * TT + t + 1)
                    if t == 0:
                        act.wait_ge(os_ready, h)
                        act.wait_ge(rot_ready, h)
                    nc.scalar.copy(z[:, t], Z[t % 2][:]).then_inc(z_v, 1)
                act.wait_ge(z_ready, h * TT + TT)
                for j in range(4):
                    nc.scalar.copy(z[0:DB, NT, j * P:(j + 1) * P], GS[32 * j:32 * j + DB, 0:P])
                for f in range(2):
                    last = nc.scalar.copy(gs[:, f], GS[32 * f:32 * f + DB, P:2 * P])
                last.then_inc(z_v, 1)
                act.wait_ge(gate_ready, h + 1)
                act.wait_ge(og_ready, h)
                nc.scalar.activation(sgT[:, 0, 0:SEQ], G[0][:], ACT.Silu)
                nc.scalar.activation(sgT[:, 1, 0:SEQ], G[1][:], ACT.Silu)
                nc.scalar.activation(sgT[:, :, SEQ:TOK], GS[:, 2 * P:2 * P + 2 * DB].rearrange("p (f b) -> p f b", f=2),
                                     ACT.Silu).then_inc(gate_used, 1)
                act.wait_ge(qk_ready, h + 1)
                nc.scalar.copy(kT[:].rearrange("p c n -> p (c n)"), T[1][:]).then_inc(k_copied, 1)
                nc.scalar.copy(qT[:].rearrange("p c n -> p (c n)"), T[0][:]).then_inc(q_copied, 1)
                act.wait_ge(var_ready, h + 1)
                nc.scalar.activation(sd[:], var[:], ACT.Sqrt).then_inc(sd_ready, 1)

            heads(act, head)

        @block.vector
        def _(dve):
            dve.wait_ge(c_in, 48)
            nc.vector.memset(mv[:], 0.0)
            nc.vector.memset(rot[:], 0.0)
            dve.drain()

            def head(pair, s, h):
                for t in range(TT):
                    n = P if t < NT else DB
                    dve.wait_ge(z_v, h * TT + t + 1)
                    zh = z[0:n, t, 0:2 * RK].rearrange("p (a b n) -> p a b n", a=2, b=2)
                    u = t2[0:n, t % 2].rearrange("p (a b n) -> p a b n", a=2, b=2)
                    sn = rope[0:n, t, 1].rearrange("p (a b n) -> p a b n", a=2, b=2)
                    nc.vector.tensor_tensor(t1[0:n, t % 2], z[0:n, t, 0:2 * RK], rope[0:n, t, 0], ALU.mult)
                    nc.vector.tensor_tensor(u[:, :, 0], zh[:, :, 1], sn[:, :, 0], ALU.mult)
                    nc.vector.tensor_tensor(u[:, :, 1], zh[:, :, 0], sn[:, :, 1], ALU.mult)
                    dve.drain()
                    last = nc.vector.tensor_tensor(rot[0:n, t], t1[0:n, t % 2], t2[0:n, t % 2], ALU.add)
                last.then_inc(rot_ready, 1)
                dve.drain()
                dve.wait_ge(hc_in[s], pair * 16 + 16)
                last = nc.vector.tensor_scalar(kd[:], rot[:, 0:NT, RK:2 * RK], hc[:, s, 2 * P:2 * P + 1], None, ALU.mult)
                nc.vector.tensor_tensor(km[:], rot[0:DB, NT:TT, RK:2 * RK].to_broadcast([DB, DB, RK]), e8[:],
                                        ALU.mult).then_inc(kd_ready, 1)
                dve.wait_ge(q_copied, h + 1)
                nc.vector.tensor_tensor(qgT[:], qT[:],
                                        hc[:, s:s + 1, P:2 * P].to_broadcast([P, NT, P]), ALU.mult)
                nc.vector.tensor_copy(qs[:], T[2][:, 0:DB]).then_inc(qg_ready, 1)
                dve.drain()
                nc.vector.tensor_tensor(qm[:], qs[:].rearrange("p (a b) -> p a b", a=1).to_broadcast([P, DB, DB]), d8[:],
                                        ALU.mult).then_inc(qm_ready, 1)
                dve.wait_ge(sup_ready, h + 1)
                dve.wait_ge(S_out, h * 16)
                nc.vector.tensor_copy(S[:, 0], T[1][:, 0:RV])
                for c in range(1, NT):
                    dve.drain()
                    last = nc.vector.scalar_tensor_tensor(S[:, c], S[:, c - 1], hc[:, s, 2 * P + 1:2 * P + 2],
                                                          T[1 + c // 2][:, (c % 2) * RV:(c % 2 + 1) * RV],
                                                          ALU.mult, ALU.add)
                last.then_inc(S_ready, 1)
                dve.wait_ge(att_ready, h + 1)
                nc.vector.tensor_tensor(att[:], T[0][:].rearrange("p (c n) -> p c n", c=NT),
                                        hc[:, s:s + 1, 0:P].to_broadcast([P, NT, P]), ALU.mult).then_inc(att_masked, 1)
                dve.wait_ge(outer_ready, h + 1)
                dve.wait_ge(st_in[s], pair * 16 + 16)
                for q in range(4):
                    st = state[:, s, 2 * q:2 * q + 2].rearrange("p b v -> p (b v)")
                    last = nc.vector.scalar_tensor_tensor(st, st, hc[:, s, 2 * P + 2:2 * P + 3], OUT[q][:],
                                                          ALU.mult, ALU.add)
                last.then_inc(state_new, 1)
                o = [Z[c // 2][:, (c % 2) * RV:(c % 2 + 1) * RV] for c in range(NT)] + [GS[0:DB, 0:RV]]
                dve.wait_ge(o_ready, h + 1)
                dve.wait_ge(os_ready, h + 1)
                for t in range(TT):
                    n = P if t < NT else DB
                    nc.vector.bn_stats(stats[0:n, t], o[t])
                dve.drain()
                for t in range(TT):
                    n = P if t < NT else DB
                    nc.vector.bn_aggr(mv[0:n, t], stats[0:n, t])
                dve.drain()
                nc.vector.tensor_scalar(var[:], mv[:, :, 1], EPS, None, ALU.add).then_inc(var_ready, 1)
                dve.wait_ge(sd_ready, h + 1)
                nc.vector.reciprocal(rs[:], sd[:])
                dve.drain()
                for t in range(TT):
                    n = P if t < NT else DB
                    last = nc.vector.tensor_scalar(y[0:n, t], o[t], mv[0:n, t, 0:1], rs[0:n, t:t + 1],
                                                   ALU.subtract, ALU.mult)
                last.then_inc(y_ready, 1)
                dve.wait_ge(yT_ready, h + 1)
                dve.wait_ge(gate_used, h + 1)
                for f in range(2):
                    g = hc[:, s, 2 * P + 3 + f:2 * P + 4 + f]
                    nc.vector.scalar_tensor_tensor(m.ogT[:, bass.ds(2 * h + f, 1), 0:SEQ].rearrange("p a n -> p (a n)"),
                                                   T[f][:], g, sgT[:, f, 0:SEQ], ALU.mult, ALU.mult)
                    last = nc.vector.scalar_tensor_tensor(
                        m.ogT[:, bass.ds(2 * h + f, 1), SEQ:TOK].rearrange("p a n -> p (a n)"),
                        T[2][:, f * DB:(f + 1) * DB], g, sgT[:, f, SEQ:TOK], ALU.mult, ALU.mult)
                last.then_inc(og_ready, 1)

            heads(dve, head)


def row4(ap):
    return ap.rearrange("a p k n -> p (a k) n")


QP = NH // HPG
KVP = 6
GP = DI // 512
NP = QP + KVP + GP
NCP = (SEQ - CL) // CS + 1
PAST = 1024
NCS = (PAST + 1 - CL) // CS + 1
LOW = 1e25


def nsa_project(nc, m, a):
    with Stage(nc) as ctx:
        sb = lambda n, s: ctx.enter_context(nc.sbuf_tensor(f"np_{n}", s, F32))
        ps = lambda n, s: ctx.enter_context(nc.psum_tensor(f"np_{n}", s, F32))
        sem = lambda n: ctx.sem(f"np_{n}")
        w = sb("w", [P, 2, KM, 512])
        wb = sb("wb", [P, KM, 3 * NH])
        stage = sb("stage", [P, TT, 512])
        nrm = sb("nrm", [P, 2, 512])
        gs = sb("gs", [DB, 4, P])
        ss, ms, sd, rs = sb("ss", [P, 4]), sb("ms", [P, 4]), sb("sd", [P, 4]), sb("rs", [P, 4])
        Z = ps("Z", [P, 2, 512])
        TP = ps("TP", [P, 2, 512])
        B = ps("B", [P, 512])
        sq = ps("sq", [P, 512])
        G = ps("G", [P, 2, 512])
        w_in = [sem("w_in0"), sem("w_in1")]
        c_in, z_ready, z_copied, nrm_ready = sem("c_in"), sem("z_ready"), sem("z_copied"), sem("nrm_ready")
        tp_ready, tp_copied, sq_ready, ms_ready, sd_ready = (sem("tp_ready"), sem("tp_copied"), sem("sq_ready"),
                                                             sem("ms_ready"), sem("sd_ready"))
        gate_ready, gate_used, b_ready, b_used = (sem("gate_ready"), sem("gate_used"),
                                                              sem("b_ready"), sem("b_used"))
        sq_used = sem("sq_used")
        gs_ready, gs_copied, gst_ready, gs_used = sem("gs_ready"), sem("gs_copied"), sem("gst_ready"), sem("gs_used")
        stored, shifted = sem("stored"), sem("shifted")
        block = ctx.enter_context(nc.Block())

        ROWS = [(m.cmp_prompt, m.cmp_sample), (m.slc_prompt, m.slc_sample), (m.win_prompt, None)]
        KINDS = ["raw", "raw", "key", "value", "key", "value"]
        KT = [a.XT[:, 0:KVH], a.XT[:, KVH:2 * KVH], a.skT[:], None, a.wkT[:], None]
        GAIN = [None, None, 2, None, 3, None]
        TILE = [stage, stage, stage, a.sv, stage, a.wv]
        NB = [QP * TT + n for n in (0, 0, 0, TT, TT, 2 * TT)]
        UB = [QP * TT + n for n in (0, NT, 2 * NT, 2 * NT + TT, 2 * NT + TT, 2 * NT + 2 * TT)]

        @block.sync
        def _(sp):
            sp.dma_start(a.gain[:], m.c_gain).then_inc(c_in, 16)
            sp.dma_start(wb[:], m.w1_bgate).then_inc(c_in, 16)
            for s in range(2):
                sp.dma_start(w[:, s], m.w_in[1][s]).then_inc(w_in[s], 16)
            sp.dma_start(m.win_sample[:, 0:511], m.state_l1_win[:, 1:512]).then_inc(shifted, 16)
            with sp.Fori(1, (NP - 2) // 2) as pair:
                for s in range(2):
                    sp.wait_ge(z_ready, (2 * pair + s - 1) * TT)
                    sp.dma_start(w[:, s], row4(m.w_in[1][bass.ds(2 * pair + s, 1)])).then_inc(w_in[s], 16)
            for s in range(2):
                sp.wait_ge(gate_ready, 4 * (s + 1))
                sp.dma_start(w[:, s], m.w_in[1][NP - 2 + s]).then_inc(w_in[s], 16)
            sp.wait_ge(shifted, 16)

        @block.gpsimd
        def _(pool):
            for j in range(KVP):
                pool.wait_ge(z_copied, (QP + j + 1) * TT)
                prompt, sample = ROWS[j // 2]
                pool.dma_start(prompt[0, :, j % 2].rearrange("(t p) g d -> p t (g d)", p=P), TILE[j][:, 0:NT]
                               ).then_inc(stored, 16)
                dst = sample[:, 0, j % 2] if sample is not None else m.win_sample[:, 511, j % 2]
                pool.dma_start(dst.rearrange("b g d -> b (g d)"), TILE[j][0:DB, NT]).then_inc(stored, 16)
            pool.wait_ge(stored, 32 * KVP)

        @block.tensor
        def _(pe):
            def project_samples(out, s, k):
                for j in range(4):
                    last = nc.tensor.matmul(out[32 * j:32 * j + DB], m.hT[:, k, SEQ:TOK],
                                            w[:, s, k, j * P:(j + 1) * P], start=(k == 0), stop=(k == KM - 1))
                return last

            def project(n, s, t):
                if t > 0:
                    pe.wait_ge(z_copied, n - 1)
                else:
                    pe.wait_ge(z_copied, n)
                for k in range(KM):
                    if t < NT:
                        last = nc.tensor.matmul(Z[:, t % 2], m.hT[:, k, t * P:(t + 1) * P], w[:, s, k],
                                                start=(k == 0), stop=(k == KM - 1))
                    else:
                        last = project_samples(Z[:, t % 2, 0:P], s, k)
                last.then_inc(z_ready, 1)

            def turn(src, t, u):
                pe.wait_ge(tp_copied, u - 1 if t > 0 else u)
                for r in range(4):
                    last = nc.tensor.transpose(TP[:, t % 2, r * P:(r + 1) * P], src[:, r * P:(r + 1) * P], m.ident[:])
                last.then_inc(tp_ready, 1)

            with pe.Fori(0, QP // 2) as pair:
                for s in range(2):
                    piece = 2 * pair + s
                    pe.wait_ge(w_in[s], pair * 16 + 16)
                    for t in range(TT + 1):
                        if t < TT:
                            project(piece * TT + t, s, t)
                        if t > 0:
                            pe.wait_ge(nrm_ready, piece * TT + t)
                            turn(nrm[:, (t - 1) % 2], t - 1, piece * TT + t - 1)
            for j in range(KVP):
                piece, s = QP + j, (QP + j) % 2
                pe.wait_ge(w_in[s], 16 * (piece // 2 + 1))
                for t in range(TT + 1):
                    if t < TT:
                        project(piece * TT + t, s, t)
                    if t > 0 and KINDS[j] == "key":
                        pe.wait_ge(nrm_ready, NB[j] + t)
                        turn(nrm[:, (t - 1) % 2], t - 1, UB[j] + t - 1)
                    if 0 < t <= NT and KINDS[j] == "raw":
                        pe.wait_ge(z_copied, piece * TT + t)
                        turn(stage[:, t - 1], t - 1, UB[j] + t - 1)
            with pe.Fori(0, GP // 2) as pair:
                for s in range(2):
                    piece = QP + KVP + 2 * pair + s
                    pe.wait_ge(w_in[s], ((QP + KVP) // 2 + pair) * 16 + 16)
                    pe.wait_ge(gs_used, 2 * pair + s)
                    for k in range(KM):
                        last = project_samples(B[:, 0:P], s, k)
                    last.then_inc(gs_ready, 1)
                    for f in range(4):
                        n = (2 * pair + s) * 4 + f
                        pe.wait_ge(gate_used, n - 1 if s + f > 0 else n)
                        for k in range(KM):
                            last = nc.tensor.matmul(G[:, f % 2], w[:, s, k, f * P:(f + 1) * P], m.hT[:, k, 0:SEQ],
                                                    start=(k == 0), stop=(k == KM - 1))
                        last.then_inc(gate_ready, 1)
                        if f == 1:
                            pe.wait_ge(c_in, 32)
                            pe.wait_ge(gs_copied, 2 * pair + s + 1)
                            for j in range(4):
                                last = nc.tensor.matmul(B[:, P + j * DB:P + (j + 1) * DB], gs[:, j],
                                                        m.ident[0:DB, 0:DB], start=True, stop=True)
                            last.then_inc(gst_ready, 1)
            pe.wait_ge(c_in, 32)
            pe.wait_ge(gs_used, GP)
            for t in range(TT):
                mt = P if t < NT else DB
                pe.wait_ge(b_used, t)
                for k in range(KM):
                    last = nc.tensor.matmul(B[0:mt, 0:3 * NH], m.hT[:, k, t * P:t * P + mt], wb[:, k],
                                            start=(k == 0), stop=(k == KM - 1))
                last.then_inc(b_ready, 1)

        @block.scalar
        def _(act):
            def leave(dst, t):
                if t < NT:
                    return nc.scalar.copy(dst[:, t], Z[:, t % 2])
                for j in range(4):
                    last = nc.scalar.copy(dst[0:DB, t, j * P:(j + 1) * P], Z[32 * j:32 * j + DB, t % 2, 0:P])
                return last

            def norm(n, t):
                mt = P if t < NT else DB
                act.drain()
                act.wait_ge(sq_used, n)
                nc.scalar.activation(sq[0:mt], stage[0:mt, t], ACT.Square).then_inc(sq_ready, 1)
                act.wait_ge(ms_ready, n + 1)
                nc.scalar.activation(sd[0:mt], ms[0:mt], ACT.Sqrt).then_inc(sd_ready, 1)

            def out(u, t, dst, gain):
                mt = P if t < NT else DB
                act.wait_ge(tp_ready, u + 1)
                src = TP[:, t % 2].rearrange("p (r n) -> p r n", r=4)[:, :, 0:mt]
                at = dst[:, :, t * P:t * P + mt]
                if gain is None:
                    nc.scalar.copy(at, src).then_inc(tp_copied, 1)
                else:
                    nc.scalar.activation(at, src, ACT.Copy, scale=a.gain[:, gain:gain + 1]).then_inc(tp_copied, 1)

            act.wait_ge(c_in, 32)
            with act.Fori(0, QP) as piece:
                for t in range(TT):
                    act.wait_ge(z_ready, piece * TT + t + 1)
                    act.wait_ge(nrm_ready, piece * TT)
                    leave(stage, t).then_inc(z_copied, 1)
                    norm(piece * TT + t, t)
                    if t > 0:
                        out(piece * TT + t - 1, t - 1, a.qT[:, bass.ds(piece * HPG, HPG)], 0)
                out(piece * TT + TT - 1, TT - 1, a.qT[:, bass.ds(piece * HPG, HPG)], 0)
            for j in range(KVP):
                kind = KINDS[j]
                tiles = NT if kind == "raw" else TT
                act.wait_ge(nrm_ready, NB[j])
                act.wait_ge(stored, 32 * j)
                for t in range(TT + 1):
                    if t < TT:
                        act.wait_ge(z_ready, (QP + j) * TT + t + 1)
                        leave(TILE[j], t).then_inc(z_copied, 1)
                        if kind == "key":
                            norm(NB[j] + t, t)
                    if kind != "value" and 0 < t <= tiles:
                        out(UB[j] + t - 1, t - 1, KT[j], GAIN[j])
            with act.Fori(0, GP) as piece:
                act.wait_ge(gs_ready, piece + 1)
                for j in range(4):
                    last = nc.scalar.copy(gs[:, j], B[32 * j:32 * j + DB, 0:P])
                last.then_inc(gs_copied, 1)
                for f in range(4):
                    act.wait_ge(gate_ready, 4 * piece + f + 1)
                    nc.scalar.activation(m.ogT[:, bass.ds(4 * piece + f, 1), 0:SEQ].rearrange("p a n -> p (a n)"),
                                         G[:, f % 2], ACT.Silu).then_inc(gate_used, 1)
                act.wait_ge(gst_ready, piece + 1)
                nc.scalar.activation(m.ogT[:, bass.ds(4 * piece, 4), SEQ:TOK],
                                     B[:, P:P + 4 * DB].rearrange("p (j b) -> p j b", j=4), ACT.Silu).then_inc(gs_used, 1)
            for t in range(TT):
                mt = P if t < NT else DB
                act.wait_ge(b_ready, t + 1)
                nc.scalar.activation(a.bg[0:mt, t], B[0:mt, 0:3 * NH], ACT.Sigmoid).then_inc(b_used, 1)

        @block.vector
        def _(dve):
            def norm(u, t, scale):
                mt = P if t < NT else DB
                dve.wait_ge(sq_ready, u + 1)
                nc.vector.tensor_reduce(ss[0:mt], sq[0:mt].rearrange("p (r n) -> p r n", r=4), axis=AX,
                                        op=ALU.add).then_inc(sq_used, 1)
                dve.drain()
                nc.vector.tensor_scalar(ms[0:mt], ss[0:mt], 1.0 / HD, EPS, ALU.mult, ALU.add).then_inc(ms_ready, 1)
                dve.wait_ge(sd_ready, u + 1)
                nc.vector.reciprocal(rs[0:mt], sd[0:mt])
                dve.drain()
                if scale is not None:
                    nc.vector.tensor_scalar(rs[0:mt], rs[0:mt], scale, None, ALU.mult)
                    dve.drain()
                nc.vector.tensor_tensor(nrm[0:mt, t % 2].rearrange("p (r n) -> p r n", r=4),
                                        stage[0:mt, t].rearrange("p (r n) -> p r n", r=4),
                                        rs[0:mt].rearrange("p (r o) -> p r o", o=1).to_broadcast([mt, 4, P]),
                                        ALU.mult).then_inc(nrm_ready, 1)

            with dve.Fori(0, QP) as piece:
                for t in range(TT):
                    u = piece * TT + t
                    dve.wait_ge(tp_ready, u - 1 if t > 0 else u)
                    norm(u, t, HD ** -0.5)
            for j in range(KVP):
                if KINDS[j] == "key":
                    for t in range(TT):
                        dve.wait_ge(tp_ready, UB[j] + (t - 1 if t > 0 else 0))
                        norm(NB[j] + t, t, None)


def nsa_compress(nc, m, a):
    G4, N = KVH, NCP
    with Stage(nc) as ctx:
        sb = lambda n, s: ctx.enter_context(nc.sbuf_tensor(f"nc_{n}", s, F32))
        ps = lambda n, s: ctx.enter_context(nc.psum_tensor(f"nc_{n}", s, F32))
        sem = lambda n: ctx.sem(f"nc_{n}")
        pcs = sb("pcs", [P, 2, G4, N])
        ck = sb("ck", [N, G4, P])
        sq = sb("sq", [N, G4, P])
        ckn = sb("ckn", [N, G4, P])
        ss, ms, sd, rs = sb("ss", [N, 4]), sb("ms", [N, 4]), sb("sd", [N, 4]), sb("rs", [N, 4])
        BI = ps("BI", [P, 512])
        PRE = ps("PRE", [P, 512])
        CK = ps("CK", [P, 512])
        CV = ps("CV", [P, 512])
        TC = ps("TC", [P, 512])
        w_in, bias_ready, bias_copied, pre_ready, pcs_ready = (sem("w_in"), sem("bias_ready"), sem("bias_copied"),
                                                               sem("pre_ready"), sem("pcs_ready"))
        ck_ready, ck_copied, sq_ready, ms_ready, sd_ready = (sem("ck_ready"), sem("ck_copied"), sem("sq_ready"),
                                                             sem("ms_ready"), sem("sd_ready"))
        ckn_ready, tc_ready, done, cv_cleared = sem("ckn_ready"), sem("tc_ready"), sem("done"), sem("cv_cleared")
        block = ctx.enter_context(nc.Block())

        @block.sync
        def _(sp):
            sp.dma_start(a.w1[:], m.cmp_w1.rearrange("c l d h -> d (c l) h")).then_inc(w_in, 16)
            sp.dma_start(a.w2[:], m.cmp_w2.rearrange("c h d -> h c d")).then_inc(w_in, 16)
            sp.dma_start(a.peT[:], m.c_peT).then_inc(w_in, 16)

        @block.tensor
        def _(pe):
            pe.wait_ge(w_in, 48)
            for c in range(2):
                for l in range(CL):
                    last = nc.tensor.matmul(BI[:, c:c + 1], a.w1[:, c * CL + l], a.peT[:, c * CL + l:c * CL + l + 1],
                                            start=(l == 0), stop=(l == CL - 1))
            last.then_inc(bias_ready, 1)
            for c in range(2):
                for l in range(CL):
                    last = nc.tensor.matmul(PRE[:, c * G4 * N:(c + 1) * G4 * N], a.w1[:, c * CL + l],
                                            a.XT[:, c * G4:(c + 1) * G4, l:l + CS * (N - 1) + 1:CS],
                                            start=(l == 0), stop=(l == CL - 1))
            last.then_inc(pre_ready, 1)
            pe.wait_ge(pcs_ready, 1)
            for c, bank in ((0, CK), (1, CV)):
                for g in range(G4):
                    last = nc.tensor.matmul(bank[0:N, g * P:(g + 1) * P], pcs[:, c, g], a.w2[:, c], start=True, stop=True)
            last.then_inc(ck_ready, 1)
            pe.wait_ge(ckn_ready, 1)
            for g in range(G4):
                last = nc.tensor.transpose(TC[:, g * N:(g + 1) * N], ckn[:, g], m.ident[0:N, 0:N])
            last.then_inc(tc_ready, 1)

        @block.scalar
        def _(act):
            act.wait_ge(bias_ready, 1)
            nc.scalar.copy(a.bias[:], BI[:, 0:2])
            act.wait_ge(pre_ready, 1)
            act.drain()
            for c in range(2):
                last = nc.scalar.activation(pcs[:, c].rearrange("p g n -> p (g n)"), PRE[:, c * G4 * N:(c + 1) * G4 * N],
                                            ACT.Silu, bias=a.bias[:, c:c + 1])
            last.then_inc(pcs_ready, 1)
            act.wait_ge(ck_ready, 1)
            nc.scalar.copy(ck[:].rearrange("n g d -> n (g d)"), CK[0:N, :])
            act.wait_ge(cv_cleared, 1)
            nc.scalar.copy(a.cv[0:N], CV[0:N, :])
            act.drain()
            nc.scalar.activation(sq[:], ck[:], ACT.Square).then_inc(sq_ready, 1)
            act.wait_ge(ms_ready, 1)
            nc.scalar.activation(sd[:], ms[:], ACT.Sqrt).then_inc(sd_ready, 1)
            act.wait_ge(tc_ready, 1)
            nc.scalar.activation(a.ckT[:].rearrange("p g n -> p (g n)"), TC[:, 0:G4 * N], ACT.Copy,
                                 scale=a.gain[:, 1:2]).then_inc(done, 1)

        @block.vector
        def _(dve):
            nc.vector.memset(a.cv[:], 0.0).then_inc(cv_cleared, 1)
            dve.wait_ge(sq_ready, 1)
            nc.vector.tensor_reduce(ss[:], sq[:], axis=AX, op=ALU.add)
            dve.drain()
            nc.vector.tensor_scalar(ms[:], ss[:], 1.0 / HD, EPS, ALU.mult, ALU.add).then_inc(ms_ready, 1)
            dve.wait_ge(sd_ready, 1)
            nc.vector.reciprocal(rs[:], sd[:])
            dve.drain()
            nc.vector.tensor_tensor(ckn[:], ck[:], rs[:].rearrange("n (g o) -> n g o", o=1).to_broadcast([N, G4, P]),
                                    ALU.mult).then_inc(ckn_ready, 1)


def nsa_prompt(nc, m, a):
    R = HPG
    with Stage(nc) as ctx:
        sb = lambda n, s: ctx.enter_context(nc.sbuf_tensor(f"na_{n}", s, F32))
        ps = lambda n, s: ctx.enter_context(nc.psum_tensor(f"na_{n}", s, F32))
        sem = lambda n: ctx.sem(f"na_{n}")
        causal = sb("causal", [P, P])
        cmask = sb("cmask", [P, NT, NCP])
        qg = sb("qg", [P, R, SEQ])
        prob = sb("prob", [P, R, SEQ])
        pT = sb("pT", [P, 2, SEQ])
        mx, nmx, den, rden, coef = (sb(n, [P, R]) for n in ("mx", "nmx", "den", "rden", "coef"))
        o_sb = sb("o_sb", [P, R, P])
        S = ps("S", [P, R, 512])
        PT = ps("PT", [P, 2, 512])
        O = ps("O", [P, R, P])
        OT = ps("OT", [P, R, P])
        c_in, qg_ready, s_ready, max_ready, exp_ready, p_ready = (sem("c_in"), sem("qg_ready"), sem("s_ready"),
                                                                  sem("max_ready"), sem("exp_ready"), sem("p_ready"))
        pt_ready, pt_copied, pv_done, o_ready, o_copied, ot_ready, ot_used = (
            sem("pt_ready"), sem("pt_copied"), sem("pv_done"), sem("o_ready"), sem("o_copied"), sem("ot_ready"),
            sem("ot_used"))
        block = ctx.enter_context(nc.Block())
        BR = 3

        @block.gpsimd
        def _(pool):
            nc.gpsimd.tensor_copy(a.qs[:], a.qT[:, :, SEQ:TOK])
            nc.gpsimd.tensor_copy(a.ks[:, 0], a.skT[:, :, SEQ:TOK])
            nc.gpsimd.tensor_copy(a.ks[:, 1], a.wkT[:, :, SEQ:TOK])


        @block.sync
        def _(sp):
            sp.dma_start(causal[:], m.c_causal).then_inc(c_in, 16)
            sp.dma_start(cmask[:], m.c_cmask).then_inc(c_in, 16)

        def values(pe, g, it, br, r, q):
            gs = bass.ds(g * HD, HD)
            pe.wait_ge(pt_copied, q + 1)
            if br < 2:
                v = [a.sv, a.wv][br]
                for j in range(it + 1):
                    last = nc.tensor.matmul(O[:, r], pT[:, r % 2, j * P:(j + 1) * P], v[:, j, gs],
                                            start=(br == 0 and r == 0 and j == 0), stop=False, skip_group_check=True)
            else:
                last = nc.tensor.matmul(O[:, r], pT[:, r % 2, 0:P], a.cv[:, gs],
                                        start=False, stop=(r == R - 1), skip_group_check=True)
            last.then_inc(pv_done, 1)

        @block.tensor
        def _(pe):
            with pe.Fori(0, KVH) as g:
                pe.wait_ge(qg_ready, g + 1)
                gs = bass.ds(g, 1)
                for it in range(NT):
                    unit = g * NT + it
                    for br in range(BR):
                        step = unit * BR + br
                        nj = (it + 1) * P if br < 2 else NCP
                        keys = [a.skT, a.wkT, a.ckT][br]
                        pe.wait_ge(exp_ready, step)
                        for r in range(R):
                            last = nc.tensor.matmul(S[:, r, 0:nj], qg[:, r, it * P:(it + 1) * P],
                                                    keys[:, gs, 0:nj].rearrange("p a n -> p (a n)"),
                                                    start=True, stop=True)
                        last.then_inc(s_ready, 1)
                        pe.wait_ge(p_ready, step + 1)
                        if br == 0:
                            pe.wait_ge(o_copied, unit)
                        for r in range(R):
                            q = step * R + r
                            if r > 0:
                                pe.wait_ge(pt_copied, q - 1)
                            else:
                                pe.wait_ge(pt_copied, q)
                            if br < 2:
                                for j in range(it + 1):
                                    last = nc.tensor.transpose(PT[:, r % 2, j * P:(j + 1) * P],
                                                               prob[:, r, j * P:(j + 1) * P], m.ident[:])
                            else:
                                last = nc.tensor.transpose(PT[0:NCP, r % 2, 0:P], prob[:, r, 0:NCP], m.ident[:])
                            last.then_inc(pt_ready, 1)
                            if r > 0:
                                values(pe, g, it, br, r - 1, q - 1)
                        values(pe, g, it, br, R - 1, step * R + R - 1)
                    pe.wait_ge(o_copied, unit + 1)
                    pe.wait_ge(ot_used, unit)
                    for r in range(R):
                        last = nc.tensor.transpose(OT[:, r], o_sb[:, r], m.ident[:])
                    last.then_inc(ot_ready, 1)

        @block.scalar
        def _(act):
            with act.Fori(0, KVH) as g:
                act.wait_ge(s_ready, g * NT * BR)
                nc.scalar.copy(qg[:], a.qT[:, bass.ds(g * R, R), 0:SEQ]).then_inc(qg_ready, 1)
                for it in range(NT):
                    unit = g * NT + it
                    for br in range(BR):
                        step = unit * BR + br
                        nj = (it + 1) * P if br < 2 else NCP
                        act.wait_ge(max_ready, step + 1)
                        act.wait_ge(pt_ready, step * R)
                        for r in range(R):
                            last = nc.scalar.activation(prob[:, r, 0:nj], S[:, r, 0:nj], ACT.Exp, bias=nmx[:, r:r + 1],
                                                        accum_out=den[:, r:r + 1])
                        last.then_inc(exp_ready, 1)
                        for r in range(R):
                            q = step * R + r
                            act.wait_ge(pt_ready, q + 1)
                            act.wait_ge(pv_done, q - 1 if r > 0 else q)
                            if br < 2:
                                nc.scalar.copy(pT[:, r % 2, 0:nj], PT[:, r % 2, 0:nj]).then_inc(pt_copied, 1)
                            else:
                                nc.scalar.copy(pT[0:NCP, r % 2, 0:P], PT[0:NCP, r % 2, 0:P]).then_inc(pt_copied, 1)
                    act.wait_ge(pv_done, (unit + 1) * BR * R)
                    act.wait_ge(ot_ready, unit)
                    nc.scalar.copy(o_sb[:], O[:]).then_inc(o_copied, 1)

        @block.vector
        def _(dve):
            dve.wait_ge(c_in, 32)
            with dve.Fori(0, KVH) as g:
                for it in range(NT):
                    unit = g * NT + it
                    for br in range(BR):
                        step = unit * BR + br
                        nj = (it + 1) * P if br < 2 else NCP
                        lo = nj - P if br < 2 else 0
                        mask = causal[:] if br < 2 else cmask[:, it]
                        dve.wait_ge(s_ready, step + 1)
                        nc.vector.tensor_tensor(S[:, :, lo:nj], S[:, :, lo:nj],
                                                mask.rearrange("p (o n) -> p o n", o=1).to_broadcast([P, R, nj - lo]),
                                                ALU.add)
                        dve.drain()
                        nc.vector.tensor_reduce(mx[:], S[:, :, 0:nj], axis=AX, op=ALU.max)
                        dve.drain()
                        nc.vector.tensor_scalar(nmx[:], mx[:], -1.0, LOW, ALU.mult, ALU.min).then_inc(max_ready, 1)
                        dve.wait_ge(exp_ready, step + 1)
                        nc.vector.tensor_scalar(rden[:], den[:], 1e-30, None, ALU.max)
                        dve.drain()
                        nc.vector.reciprocal(rden[:], rden[:])
                        dve.drain()
                        gb = (1, 2, 0)[br]
                        nc.vector.tensor_tensor(coef[:], rden[:], a.bg[:, it, bass.ds(g * R + gb * NH, R)], ALU.mult)
                        dve.drain()
                        nc.vector.tensor_tensor(prob[:, :, 0:nj], prob[:, :, 0:nj],
                                                coef[:].rearrange("p (r o) -> p r o", o=1).to_broadcast([P, R, nj]),
                                                ALU.mult).then_inc(p_ready, 1)
                    dve.wait_ge(ot_ready, unit + 1)
                    og = m.ogT[:, bass.ds(g * R, R), it * P:(it + 1) * P]
                    nc.vector.tensor_tensor(og, OT[:], og, ALU.mult).then_inc(ot_used, 1)


NSL = (PAST + 1 + 63) // 64
PG = 8
WP = 4
KTP = PG + WP


def nsa_samples(nc, m, a):
    N, G4 = NCS, KVH
    with Stage(nc) as ctx:
        sb = lambda n, s: ctx.enter_context(nc.sbuf_tensor(f"s_{n}", s, F32))
        ps = lambda n, s: ctx.enter_context(nc.psum_tensor(f"s_{n}", s, F32))
        sem = lambda n: ctx.sem(f"s_{n}")
        pt = ctx.enter_context(nc.sbuf_tensor("s_pt", [1, DB * PG], I32))
        A, B, C = (sb(n, [P, 4, 2 * G4 * HD]) for n in "ABC")
        W = m.hT[:].rearrange("p k n -> p (k n)")[:, 0:4 * 2 * G4 * HD].rearrange("p (t n) -> p t n", t=4)
        XT = sb("XT", [P, 2 * G4, PAST])
        KT = XT[:, 0:G4]
        WT = XT[:, G4:2 * G4, 0:512]
        vs = sb("vs", [DB, 2, G4 * HD])
        gmask, hmask, group = sb("gmask", [P, G4, NH]), sb("hmask", [NH, G4]), sb("group", [NH, NH])
        smap, blocks, e16 = sb("smap", [N, NSL]), sb("blocks", [NH, NSL]), sb("e16", [NH, DB, DB])
        bgT, gb = sb("bgT", [NH, 3, DB]), sb("gb", [NH, 3])
        qz, kn = sb("qz", [P, G4, NH]), sb("kn", [P, 2, G4])
        pcs = sb("pcs", [P, 2, G4, N])
        ck, cv, ckn = sb("ck", [N, G4, P]), sb("cv", [N, G4 * HD]), sb("ckn", [N, G4, P])
        ckT = sb("ckT", [P, G4, N])
        css, cms, csd, crs = (sb(n, [N, 4]) for n in ("css", "cms", "csd", "crs"))
        ksq = B[:, 0].rearrange("p (s n) -> p s n", s=2)
        kss, kms, ksd, krs = (sb(n, [P, KTP, G4]) for n in ("kss", "kms", "ksd", "krs"))
        p = sb("p", [NH, PAST + 1])
        mx, nmx, den, rden, coef = (sb(n, [NH, 1]) for n in ("mx", "nmx", "den", "rden", "coef"))
        pcg, pcT, imp, imp2 = sb("pcg", [NH, N]), sb("pcT", [N, 2, NH]), sb("imp", [NH, NSL]), sb("imp2", [NH, NSL])
        least, at_least, drop, dmask = sb("least", [NH, 1]), sb("at_least", [NH, NSL]), sb("drop", [NH, 1]), sb("dmask", [NH, NSL])
        pn = sb("pn", [NH, DB])
        pT, pnT = sb("pT", [P, PG, NH]), sb("pnT", [DB, NH])
        od, o16 = ckn[0:NH], sb("o16", [NH, P])
        X = [ps(f"X{i}", [P, 512]) for i in range(4)]
        SA, SB, MI, OB = (ps(n, [P, 512]) for n in ("SA", "SB", "MI", "OB"))
        c_in, a_in, b_in, s0_in, s1_in, w_in = (sem(n) for n in ("c_in", "a_in", "b_in", "s0_in", "s1_in", "w_in"))
        turned, xk_copied, xv_copied, pre_ready, pcs_ready = (
            sem(n) for n in ("turned", "xk_copied", "xv_copied", "pre_ready", "pcs_ready"))
        ck_ready, ck_sq, ck_ms, ck_sd, ckn_ready, tc_ready, ckT_ready, qz_ready = (
            sem(n) for n in ("ck_ready", "ck_sq", "ck_ms", "ck_sd", "ckn_ready", "tc_ready", "ckT_ready", "qz_ready"))
        sc_ready, max_ready, exp_ready, pc_ready, pct_ready, pct_copied = (
            sem(n) for n in ("sc_ready", "max_ready", "exp_ready", "pc_ready", "pct_ready", "pct_copied"))
        imph_ready, imph_copied, impg_ready, dmask_ready = (
            sem(n) for n in ("imph_ready", "imph_copied", "impg_ready", "dmask_ready"))
        sq_ready, sq_used, kms_ready, ksd_ready, kn_ready, kt_ready, kt_copied = (
            sem(n) for n in ("sq_ready", "sq_used", "kms_ready", "ksd_ready", "kn_ready", "kt_ready", "kt_copied"))
        s_ready, p_ready, pst_ready, pst_copied, o_done, o16_ready, ot_ready, ob_used = (
            sem(n) for n in ("s_ready", "p_ready", "pst_ready", "pst_copied", "o_done", "o16_ready", "ot_ready", "ob_used"))
        bg_ready, bg_copied, ot_used = sem("bg_ready"), sem("bg_copied"), sem("ot_used")
        block = ctx.enter_context(nc.Block())
        ID = m.ident

        def pages(eng, cache, slot, b, first, sem_in):
            for i in range(4):
                page = eng.value_load(pt[0:1, bass.ds(b * PG + first + i, 1)], min_val=0, max_val=cache.shape[0] - 1)
                eng.dma_start(slot[:, i], cache[bass.ds(page, 1)].rearrange("a r c g d -> r (a c g d)")
                              ).then_inc(sem_in, 16)

        @block.sync
        def _(sp):
            sp.dma_start(pt[:], m.page_table.rearrange("(o b) n -> o (b n)", o=1)).then_inc(c_in, 16)
            for dst, src in ((gmask, m.c_gmask), (hmask, m.c_hmask), (group, m.c_group), (smap, m.c_smap),
                             (blocks, m.c_blocks), (e16, m.c_e16)):
                sp.dma_start(dst[:], src).then_inc(c_in, 16)
            sp.dma_start(a.w1[:], m.cmp_w1.rearrange("c l d h -> d (c l) h")).then_inc(c_in, 16)
            sp.dma_start(vs[:, 0], m.slc_sample[:, 0, 1].rearrange("b g d -> b (g d)")).then_inc(c_in, 16)
            sp.dma_start(vs[:, 1], m.win_sample[:, 511, 1].rearrange("b g d -> b (g d)")).then_inc(c_in, 16)
            sp.wait_ge(c_in, 160)
            with sp.Fori(0, DB) as b:
                sp.wait_ge(c_in, 160)
                sp.wait_ge(o_done, 3 * b)
                pages(sp, m.cache_cmp, A, b, 0, a_in)
                pages(sp, m.cache_cmp, B, b, 4, b_in)
                pages(sp, m.cache_slc, C, b, 0, s0_in)
                sp.dma_start(W, m.state_l1_win[bass.ds(b, 1)].rearrange("a (t r) c g d -> r (a t) (c g d)", r=P)
                             ).then_inc(w_in, 16)
                sp.wait_ge(c_in, 160)
                sp.wait_ge(turned, b * PG + 4)
                pages(sp, m.cache_slc, A, b, 4, s1_in)

        @block.tensor
        def _(pe):
            pe.wait_ge(c_in, 160)
            for br in range(3):
                last = nc.tensor.matmul(MI[0:NH, br * DB:(br + 1) * DB], a.bg[0:DB, NT, br * NH:(br + 1) * NH],
                                        ID[0:DB, 0:DB], start=True, stop=True)
            last.then_inc(bg_ready, 1)
            pe.wait_ge(bg_copied, 1)
            with pe.Fori(0, DB) as b:
                for i in range(PG):
                    if i == 0:
                        pe.wait_ge(a_in, b * 64 + 64)
                        pe.wait_ge(pst_copied, 2 * b)
                        pe.wait_ge(kt_copied, b * KTP)
                    if i == 4:
                        pe.wait_ge(b_in, b * 64 + 64)
                    if i >= 2:
                        pe.wait_ge(xk_copied, b * PG + i - 1)
                        pe.wait_ge(xv_copied, b * PG + i - 1)
                    src = (A, B)[i // 4][:, i % 4]
                    for cg in range(2 * G4):
                        last = nc.tensor.transpose(X[2 * (i % 2) + cg // G4][:, (cg % G4) * P:(cg % G4 + 1) * P],
                                                   src[:, cg * P:(cg + 1) * P], ID[:])
                    last.then_inc(turned, 1)
                pe.wait_ge(xk_copied, b * PG + PG)
                pe.wait_ge(xv_copied, b * PG + PG)
                pe.wait_ge(p_ready, 2 * b)
                for c in range(2):
                    for l in range(CL):
                        last = nc.tensor.matmul(SA[:, c * G4 * N:(c + 1) * G4 * N], a.w1[:, c * CL + l],
                                                XT[:, c * G4:(c + 1) * G4, l:l + CS * (N - 1) + 1:CS],
                                                start=(l == 0), stop=(l == CL - 1))
                last.then_inc(pre_ready, 1)
                pe.wait_ge(pcs_ready, b + 1)
                for c in range(2):
                    for g in range(G4):
                        last = nc.tensor.matmul(X[c][0:N, g * P:(g + 1) * P], pcs[:, c, g], a.w2[:, c],
                                                start=True, stop=True)
                last.then_inc(ck_ready, 1)
                pe.wait_ge(ckn_ready, b + 1)
                for g in range(G4):
                    last = nc.tensor.matmul(X[2][:, g * N:(g + 1) * N], ckn[:, g], ID[0:N, 0:N], start=True, stop=True)
                last.then_inc(tc_ready, 1)
                pe.wait_ge(ckT_ready, b + 1)
                pe.wait_ge(qz_ready, b + 1)
                pe.wait_ge(ot_used, b)
                for g in range(G4):
                    last = nc.tensor.matmul(MI[0:NH, 0:N], qz[:, g], ckT[:, g], start=(g == 0), stop=(g == G4 - 1))
                last.then_inc(sc_ready, 1)
                pe.wait_ge(pc_ready, b + 1)
                nc.tensor.matmul(MI[0:N, 0:NH], p[:, 0:N], ID[0:NH, 0:NH], start=True, stop=True)
                nc.tensor.matmul(MI[0:N, NH:2 * NH], pcg[:], ID[0:NH, 0:NH], start=True, stop=True).then_inc(pct_ready, 1)
                pe.wait_ge(c_in, 160)
                pe.wait_ge(pct_copied, b + 1)
                nc.tensor.matmul(MI[0:NH, 0:NSL], pcT[:, 0], smap[:], start=True, stop=True).then_inc(imph_ready, 1)
                pe.wait_ge(c_in, 160)
                pe.wait_ge(ob_used, b)
                nc.tensor.matmul(OB[0:NH, :], pcT[:, 1], cv[:], start=True, stop=False).then_inc(o_done, 1)
                pe.wait_ge(c_in, 160)
                pe.wait_ge(imph_copied, b + 1)
                nc.tensor.matmul(MI[0:NH, 0:NSL], group[:], imp[:], start=True, stop=True).then_inc(impg_ready, 1)
                for br, first, tiles, keys in ((0, 0, PG, KT), (1, PG, WP, WT)):
                    for i in range(tiles):
                        u = b * KTP + first + i
                        pe.wait_ge(kn_ready, u + 1)
                        if i >= 4:
                            pe.wait_ge(kt_copied, u - 3)
                        elif br == 1:
                            pe.wait_ge(pst_copied, 2 * b + 1)
                            pe.wait_ge(kt_copied, u - 3)
                        src = (C, A, W)[(first + i) // 4][:, i % 4]
                        for g in range(G4):
                            last = nc.tensor.transpose(X[i % 4][:, g * P:(g + 1) * P], src[:, g * P:(g + 1) * P], ID[:])
                        last.then_inc(kt_ready, 1)
                    pe.wait_ge(kt_copied, b * KTP + first + tiles)
                    pe.wait_ge(dmask_ready, b + 1)
                    if br == 1:
                        pe.wait_ge(p_ready, 2 * b + 1)
                    for h in range(tiles // 4):
                        for g in range(G4):
                            nc.tensor.matmul((SA, SB)[h][0:NH, :], qz[:, g], keys[:, g, h * 512:(h + 1) * 512],
                                             start=(g == 0), stop=(g == G4 - 1))
                    for g in range(G4):
                        last = nc.tensor.matmul(MI[0:NH, 0:1], qz[:, g], kn[:, br, g:g + 1], start=(g == 0),
                                                stop=(g == G4 - 1))
                    last.then_inc(s_ready, 1)
                    pe.wait_ge(p_ready, 2 * b + br + 1)
                    for i in range(tiles):
                        nc.tensor.matmul(X[0][:, i * NH:(i + 1) * NH], p[:, i * P:(i + 1) * P], ID[0:NH, 0:NH],
                                         start=True, stop=True)
                    nc.tensor.matmul(X[0][0:DB, PG * NH:(PG + 1) * NH], pn[:], ID[0:NH, 0:NH],
                                     start=True, stop=True).then_inc(pst_ready, 1)
                    pe.wait_ge(pst_copied, 2 * b + br + 1)
                    for i in range(tiles):
                        v = (C, A, W)[(first + i) // 4][:, i % 4, G4 * HD:]
                        nc.tensor.matmul(OB[0:NH, :], pT[:, i], v, start=False, stop=False)
                    nc.tensor.matmul(OB[0:NH, :], pnT[:], vs[:, br], start=False, stop=(br == 1)).then_inc(o_done, 1)
                pe.wait_ge(o16_ready, b + 1)
                nc.tensor.matmul(MI[:, 0:NH], o16[:], ID[0:NH, 0:NH], start=True, stop=True).then_inc(ot_ready, 1)

        @block.scalar
        def _(act):
            act.wait_ge(c_in, 160)
            with act.Fori(0, DB) as b:
                for i in range(PG):
                    act.wait_ge(turned, b * PG + i + 1)
                    if i == 0:
                        act.wait_ge(s_ready, 2 * b)
                    nc.scalar.copy(XT[:, 0:G4, i * P:(i + 1) * P], X[2 * (i % 2)][:].rearrange("p (g n) -> p g n", g=G4)
                                   ).then_inc(xk_copied, 1)
                act.wait_ge(pre_ready, b + 1)
                for c in range(2):
                    last = nc.scalar.activation(pcs[:, c].rearrange("p g n -> p (g n)"),
                                                SA[:, c * G4 * N:(c + 1) * G4 * N], ACT.Silu, bias=a.bias[:, c:c + 1])
                last.then_inc(pcs_ready, 1)
                act.wait_ge(ck_ready, b + 1)
                act.wait_ge(o_done, 3 * b)
                nc.scalar.copy(ck[:].rearrange("n g d -> n (g d)"), X[0][0:N, :])
                nc.scalar.copy(cv[:], X[1][0:N, :])
                act.drain()
                nc.scalar.activation(ckn[:], ck[:], ACT.Square).then_inc(ck_sq, 1)
                act.wait_ge(ck_ms, b + 1)
                nc.scalar.activation(csd[:], cms[:], ACT.Sqrt).then_inc(ck_sd, 1)
                act.wait_ge(tc_ready, b + 1)
                nc.scalar.activation(ckT[:].rearrange("p g n -> p (g n)"), X[2][:, 0:G4 * N], ACT.Copy,
                                     scale=a.gain[:, 1:2]).then_inc(ckT_ready, 1)
                act.wait_ge(max_ready, 3 * b + 1)
                nc.scalar.activation(p[:, 0:N], MI[0:NH, 0:N], ACT.Exp, bias=nmx[:], accum_out=den[:]).then_inc(exp_ready, 1)
                for br, first, tiles, keys in ((0, 0, PG, KT), (1, PG, WP, WT)):
                    for i in range(tiles):
                        u = b * KTP + first + i
                        if br == 1 and i == 0:
                            act.wait_ge(w_in, b * 16 + 16)
                        elif i == 0:
                            act.wait_ge(s0_in, b * 64 + 64)
                        elif i == 4:
                            act.wait_ge(s1_in, b * 64 + 64)
                        src = (C, A, W)[(first + i) // 4][:, i % 4, 0:G4 * HD]
                        act.wait_ge(sq_used, u - 1 if i > 0 else u)
                        nc.scalar.activation(ksq[:, i % 2], src, ACT.Square).then_inc(sq_ready, 1)
                    act.wait_ge(kms_ready, 2 * b + br + 1)
                    nc.scalar.activation(ksd[:, first:first + tiles], kms[:, first:first + tiles], ACT.Sqrt
                                         ).then_inc(ksd_ready, 1)
                    for i in range(tiles):
                        act.wait_ge(kt_ready, b * KTP + first + i + 1)
                        nc.scalar.activation(keys[:, :, i * P:(i + 1) * P],
                                             X[i % 4][:].rearrange("p (g n) -> p g n", g=G4), ACT.Copy,
                                             scale=a.gain[:, 2 + br:3 + br]).then_inc(kt_copied, 1)
                    act.wait_ge(max_ready, 3 * b + br + 2)
                    nc.scalar.activation(p[:, 0:tiles * P + 1], p[:, 0:tiles * P + 1], ACT.Exp, bias=nmx[:],
                                         accum_out=den[:]).then_inc(exp_ready, 1)

        @block.vector
        def _(dve):
            dve.wait_ge(c_in, 160)
            dve.wait_ge(bg_ready, 1)
            nc.vector.tensor_copy(bgT[:].rearrange("h r b -> h (r b)"), MI[0:NH, 0:3 * DB]).then_inc(bg_copied, 1)
            dve.drain()
            with dve.Fori(0, DB) as b:
                one = bass.ds(b, 1)
                nc.vector.tensor_tensor(qz[:], a.qs[:, :, one].rearrange("p h (g b) -> p (b g) h", g=1)
                                        .to_broadcast([P, G4, NH]), gmask[:], ALU.mult)
                nc.vector.tensor_copy(kn[:].rearrange("p r g -> p (r g)"),
                                      a.ks[:, :, :, one].rearrange("p r g b -> p (r g b)"))
                nc.vector.tensor_copy(gb[:], bgT[:, :, one].rearrange("h r b -> h (r b)")).then_inc(qz_ready, 1)
                for i in range(PG):
                    dve.wait_ge(turned, b * PG + i + 1)
                    nc.vector.tensor_copy(XT[:, G4:2 * G4, i * P:(i + 1) * P],
                                          X[2 * (i % 2) + 1][:].rearrange("p (g n) -> p g n", g=G4)).then_inc(xv_copied, 1)
                dve.wait_ge(ck_sq, b + 1)
                nc.vector.tensor_reduce(css[:], ckn[:], axis=AX, op=ALU.add)
                dve.drain()
                nc.vector.tensor_scalar(cms[:], css[:], 1.0 / HD, EPS, ALU.mult, ALU.add).then_inc(ck_ms, 1)
                dve.wait_ge(ck_sd, b + 1)
                nc.vector.reciprocal(crs[:], csd[:])
                dve.drain()
                nc.vector.tensor_tensor(ckn[:], ck[:], crs[:].rearrange("n (g o) -> n g o", o=1)
                                        .to_broadcast([N, G4, P]), ALU.mult).then_inc(ckn_ready, 1)

                def shares(k, gate):
                    dve.wait_ge(exp_ready, 3 * b + k + 1)
                    nc.vector.reciprocal(rden[:], den[:])
                    dve.drain()
                    nc.vector.tensor_tensor(coef[:], rden[:], gb[:, gate:gate + 1], ALU.mult)
                    dve.drain()

                def maximum(k, s):
                    nc.vector.tensor_reduce(mx[:], s, axis=AX, op=ALU.max)
                    dve.drain()
                    nc.vector.tensor_scalar(nmx[:], mx[:], -1.0, LOW, ALU.mult, ALU.min).then_inc(max_ready, 1)

                dve.wait_ge(sc_ready, b + 1)
                maximum(0, MI[0:NH, 0:N])
                shares(0, 0)
                nc.vector.tensor_scalar(pcg[:], p[:, 0:N], coef[:], None, ALU.mult)
                dve.drain()
                nc.vector.tensor_scalar(p[:, 0:N], p[:, 0:N], rden[:], None, ALU.mult).then_inc(pc_ready, 1)
                dve.wait_ge(pct_ready, b + 1)
                nc.vector.tensor_copy(pcT[:].rearrange("n r h -> n (r h)"), MI[0:N, 0:2 * NH]).then_inc(pct_copied, 1)
                dve.wait_ge(imph_ready, b + 1)
                nc.vector.tensor_copy(imp[:], MI[0:NH, 0:NSL]).then_inc(imph_copied, 1)
                dve.wait_ge(impg_ready, b + 1)
                nc.vector.tensor_copy(imp2[:], MI[0:NH, 0:NSL])
                dve.drain()
                nc.vector.tensor_reduce(least[:], imp2[:, 1:NSL - 2], axis=AX, op=ALU.min)
                dve.drain()
                nc.vector.scalar_tensor_tensor(at_least[:, 1:NSL - 2], imp2[:, 1:NSL - 2], least[:], blocks[:, 1:NSL - 2],
                                               ALU.is_le, ALU.mult)
                dve.drain()
                nc.vector.tensor_reduce(drop[:], at_least[:, 1:NSL - 2], axis=AX, op=ALU.max)
                dve.drain()
                nc.vector.tensor_scalar(dmask[:], blocks[:], drop[:], NEG, ALU.is_equal, ALU.mult).then_inc(dmask_ready, 1)
                for br, first, tiles, gate in ((0, 0, PG, 1), (1, PG, WP, 2)):
                    for i in range(tiles):
                        u = b * KTP + first + i
                        dve.wait_ge(sq_ready, u + 1)
                        nc.vector.tensor_reduce(kss[:, first + i], ksq[:, i % 2].rearrange("p (g n) -> p g n", g=G4),
                                                axis=AX, op=ALU.add).then_inc(sq_used, 1)
                    dve.drain()
                    nc.vector.tensor_scalar(kms[:, first:first + tiles], kss[:, first:first + tiles], 1.0 / HD, EPS,
                                            ALU.mult, ALU.add).then_inc(kms_ready, 1)
                    dve.wait_ge(ksd_ready, 2 * b + br + 1)
                    nc.vector.reciprocal(krs[:, first:first + tiles], ksd[:, first:first + tiles])
                    dve.drain()
                    for i in range(tiles):
                        k = (C, A, W)[(first + i) // 4][:, i % 4, 0:G4 * HD].rearrange("p (g n) -> p g n", g=G4)
                        nc.vector.tensor_tensor(k, k, krs[:, first + i].rearrange("p (g o) -> p g o", o=1)
                                                .to_broadcast([P, G4, P]), ALU.mult).then_inc(kn_ready, 1)
                    n = tiles * P
                    dve.wait_ge(s_ready, 2 * b + br + 1)
                    if br == 0:
                        for h in range(2):
                            nc.vector.tensor_tensor(p[:, h * 512:(h + 1) * 512].rearrange("h (j n) -> h j n", n=64),
                                                    (SA, SB)[h][0:NH, :].rearrange("h (j n) -> h j n", n=64),
                                                    dmask[:, 8 * h:8 * h + 8].rearrange("h (j o) -> h j o", o=1)
                                                    .to_broadcast([NH, 8, 64]), ALU.add)
                    else:
                        dve.wait_ge(pst_ready, 2 * b + 1)
                        nc.vector.tensor_copy(p[:, 0:512], SA[0:NH, :])
                    nc.vector.tensor_copy(p[:, n:n + 1], MI[0:NH, 0:1])
                    dve.drain()
                    maximum(br + 1, p[:, 0:n + 1])
                    shares(br + 1, gate)
                    nc.vector.tensor_scalar(pn[:], e16[:, one].rearrange("h a b -> h (a b)"), p[:, n:n + 1], coef[:],
                                            ALU.mult, ALU.mult)
                    dve.drain()
                    nc.vector.tensor_scalar(p[:, 0:n], p[:, 0:n], coef[:], None, ALU.mult).then_inc(p_ready, 1)
                    dve.wait_ge(pst_ready, 2 * b + br + 1)
                    nc.vector.tensor_copy(pT[:, 0:tiles].rearrange("p i h -> p (i h)"), X[0][:, 0:tiles * NH])
                    nc.vector.tensor_copy(pnT[:], X[0][0:DB, PG * NH:(PG + 1) * NH]).then_inc(pst_copied, 1)
                dve.wait_ge(o_done, 3 * b + 3)
                nc.vector.tensor_tensor(od[:], OB[0:NH, :].rearrange("h (g n) -> h g n", g=G4),
                                        hmask[:].rearrange("h (g o) -> h g o", o=1).to_broadcast([NH, G4, P]),
                                        ALU.mult).then_inc(ob_used, 1)
                dve.drain()
                nc.vector.tensor_reduce(o16[:], od[:].rearrange("h g n -> h n g"), axis=AX, op=ALU.add).then_inc(o16_ready, 1)
                dve.wait_ge(ot_ready, b + 1)
                og = m.ogT[:, :, bass.ds(SEQ + b, 1)].rearrange("p h b -> p (h b)")
                nc.vector.tensor_tensor(og, MI[:, 0:NH], og, ALU.mult).then_inc(ot_used, 1)


def sparse_attention(nc, m):
    a = Mem()
    with ExitStack() as outer:
        def alloc(ctx, name, shape):
            return ctx.enter_context(nc.sbuf_tensor("a_" + name, shape, F32))

        a.gain = alloc(outer, "gain", [P, 4])
        a.bg = alloc(outer, "bg", [P, TT, 3 * NH])
        a.w2 = alloc(outer, "w2", [P, 2, P])
        a.peT = alloc(outer, "peT", [P, 2 * CL])
        a.bias = alloc(outer, "bias", [P, 2])
        a.qs = alloc(outer, "qs", [P, NH, DB])
        a.ks = alloc(outer, "ks", [P, 2, KVH, DB])
        with ExitStack() as ctx:
            a.qT = alloc(ctx, "qT", [P, NH, TOK])
            a.skT = alloc(ctx, "skT", [P, KVH, TOK])
            a.wkT = alloc(ctx, "wkT", [P, KVH, TOK])
            a.sv = alloc(ctx, "sv", [P, TT, KVH * HD])
            a.wv = alloc(ctx, "wv", [P, TT, KVH * HD])
            a.XT = alloc(ctx, "XT", [P, 2 * KVH, SEQ])
            nsa_project(nc, m, a)
            a.ckT = alloc(ctx, "ckT", [P, KVH, NCP])
            a.cv = alloc(ctx, "cv", [P, KVH * HD])
            with ExitStack() as wctx:
                a.w1 = alloc(wctx, "w1", [P, 2 * CL, P])
                nsa_compress(nc, m, a)
            nsa_prompt(nc, m, a)
        a.w1 = outer.enter_context(nc.sbuf_tensor("a_w1_again", [P, 2 * CL, P], F32))
        nsa_samples(nc, m, a)


def sparse_inputs(m, x, give):
    cols = [[(512 * g, 512 * (g + 1))] for g in range(QP + KVP)]
    gate = DI + 3 * 2 * KVH * HD
    cols += [[(gate + 512 * g, gate + 512 * (g + 1))] for g in range(GP)]
    w = x["l1_w_in"]
    m.w_in[1] = give("l1_w_in", by_columns(w, cols))
    b = w[:, gate + DI:].reshape(KM, P, NH, 3).transpose(1, 0, 3, 2).reshape(P, KM, 3 * NH)
    m.w1_bgate = give("l1_w_bgate", b)
    m.c_gain = give("l1_qk_norm", x["l1_qk_norm"].T)
    m.c_peT = give("l1_cmp_pe", x["l1_cmp_pe"].transpose(2, 1, 0).reshape(HD, 2 * CL))
    m.cmp_w1, m.cmp_w2 = give("l1_cmp_w1", x["l1_cmp_w1"]), give("l1_cmp_w2", x["l1_cmp_w2"])
    m.state_l1_win = give("state_l1_win", x["state_l1_win"])
    m.cache_cmp = give("cache_l1_cmp", x["cache_l1_cmp"])
    m.cache_slc = give("cache_l1_slc", x["cache_l1_slc"])
    m.page_table = give("page_table", x["page_table"])
    head, block = np.arange(NH), np.arange(NSL)
    same = (head[:, None] // HPG == np.arange(KVH)[None, :]).astype(np.float32)
    m.c_gmask = give("c_gmask", np.broadcast_to(same.T, (P, KVH, NH)))
    m.c_hmask = give("c_hmask", same)
    m.c_group = give("c_group", same @ same.T)
    n, lo = np.arange(NCS)[:, None], block[None, :] * 64
    over = np.minimum(n * CS + CL, lo + 64) - np.maximum(n * CS, lo)
    m.c_smap = give("c_smap", (np.maximum(over, 0) / CS).astype(np.float32))
    m.c_blocks = give("c_blocks", np.broadcast_to(block.astype(np.float32), (NH, NSL)))
    m.c_e16 = give("c_e16", np.broadcast_to(np.eye(DB, dtype=np.float32), (NH, DB, DB)))
    i = np.arange(P)
    m.c_causal = give("c_causal", np.where(i[None, :] <= i[:, None], 0.0, NEG).astype(np.float32))
    pos, end = np.arange(SEQ).reshape(NT, P), np.arange(NCP) * CS + CL - 1
    m.c_cmask = give("c_cmask", np.where(end <= pos[..., None], 0.0, NEG).astype(np.float32).transpose(1, 0, 2))


LEVELS = 7
EG, ONE, BETA, BG, EKD, GCUM, LA, EGL = range(8)
NPAR = 8


def gdn_decays(nc, m, d):
    with Stage(nc) as ctx:
        sb = lambda n, s: ctx.enter_context(nc.sbuf_tensor(f"gd_{n}", s, F32))
        ps = lambda n, s: ctx.enter_context(nc.psum_tensor(f"gd_{n}", s, F32))
        sem = lambda n: ctx.sem(f"gd_{n}")
        wab = sb("wab", [P, KM, 2 * GH])
        alog, dtb, nea = sb("alog", [P, GH]), sb("dtb", [P, GH]), sb("nea", [P, GH])
        x, nx, ex, sp_ = (sb(n, [P, TT, GH]) for n in ("x", "nx", "ex", "sp"))
        gl, dif = sb("gl", [P, NT, GH]), sb("dif", [P, NT, GH])
        ones, e8h = sb("ones", [P, P]), sb("e8h", [DB, GH, DB])
        AB = ps("AB", [P, TT, 2 * GH])
        GC, GL, EB = ps("GC", [P, 512]), ps("GL", [P, 512]), ps("EB", [P, 512])
        c_in, ab_ready, cleared, x_ready, ex_ready, ln_ready = (
            sem(n) for n in ("c_in", "ab_ready", "cleared", "x_ready", "ex_ready", "ln_ready"))
        nea_ready, la_ready, g_ready, dif_ready, e_ready, eb_in, eb_ready, beta_ready, g_used = (
            sem(n) for n in ("nea_ready", "la_ready", "g_ready", "dif_ready", "e_ready", "eb_in", "eb_ready", "beta_ready",
                             "g_used"))
        block = ctx.enter_context(nc.Block())
        tab = d.tab

        @block.sync
        def _(sp):
            sp.dma_start(wab[:], m.w2_ab).then_inc(c_in, 16)
            sp.dma_start(alog[:], m.A_log.rearrange("(o h) -> o h", o=1).to_broadcast([P, GH])).then_inc(c_in, 16)
            sp.dma_start(dtb[:], m.dt_bias.rearrange("(o h) -> o h", o=1).to_broadcast([P, GH])).then_inc(c_in, 16)
            sp.dma_start(d.ut[:], m.c_ut).then_inc(c_in, 16)

        @block.tensor
        def _(pe):
            pe.wait_ge(c_in, 64)
            for t in range(TT):
                mt = P if t < NT else DB
                for k in range(KM):
                    last = nc.tensor.matmul(AB[0:mt, t], m.hT[:, k, t * P:t * P + mt], wab[:, k],
                                            start=(k == 0), stop=(k == KM - 1))
            last.then_inc(ab_ready, 1)
            pe.wait_ge(la_ready, 1)
            la = tab[:, LA, 0:NT].rearrange("p t h -> p (t h)")
            nc.tensor.matmul(GC[:, 0:NT * GH], d.ut[:], la, start=True, stop=True)
            nc.tensor.matmul(GL[:, 0:NT * GH], ones[:], la, start=True, stop=True).then_inc(g_ready, 1)
            pe.wait_ge(eb_in, 1)
            nc.tensor.matmul(EB[:, 0:GH * DB], ones[0:DB], e8h[:].rearrange("a h b -> a (h b)"), start=True,
                             stop=True).then_inc(eb_ready, 1)

        @block.scalar
        def _(act):
            act.wait_ge(c_in, 64)
            nc.scalar.activation(nea[:], alog[:], ACT.Exp).then_inc(nea_ready, 1)
            act.wait_ge(x_ready, 1)
            nc.scalar.activation(ex[:], nx[:], ACT.Exp)
            act.drain()
            nc.scalar.activation(ex[:], ex[:], ACT.Ln, bias=1.0).then_inc(ln_ready, 1)
            act.wait_ge(dif_ready, 1)
            nc.scalar.activation(tab[:, EKD, 0:NT], dif[:], ACT.Exp)
            nc.scalar.activation(tab[:, EGL, 0:NT], gl[:], ACT.Exp)
            nc.scalar.activation(tab[:, EG], tab[:, GCUM], ACT.Exp).then_inc(e_ready, 1)
            nc.scalar.activation(tab[:, BETA, 0:NT], AB[:, 0:NT, GH:2 * GH], ACT.Sigmoid)
            nc.scalar.activation(tab[0:DB, BETA, NT], AB[0:DB, NT, GH:2 * GH], ACT.Sigmoid).then_inc(beta_ready, 1)

        @block.vector
        def _(dve):
            nc.vector.memset(tab[:], 1.0)
            nc.vector.memset(x[:], 0.0)
            nc.vector.memset(ones[:], 1.0)
            dve.drain()
            dve.wait_ge(ab_ready, 1)
            b = dtb[:].rearrange("p (o h) -> p o h", o=1)
            nc.vector.tensor_tensor(x[:, 0:NT], AB[:, 0:NT, 0:GH], b.to_broadcast([P, NT, GH]), ALU.add)
            nc.vector.tensor_tensor(x[0:DB, NT], AB[0:DB, NT, 0:GH], dtb[0:DB], ALU.add)
            dve.drain()
            nc.vector.tensor_scalar(nx[:], x[:], -1.0, None, ALU.mult)
            dve.drain()
            nc.vector.tensor_tensor(nx[:], nx[:], x[:], ALU.min).then_inc(x_ready, 1)
            dve.wait_ge(ln_ready, 1)
            nc.vector.scalar_tensor_tensor(sp_[:], x[:], 0.0, ex[:], ALU.max, ALU.add)
            dve.wait_ge(nea_ready, 1)
            dve.drain()
            nc.vector.scalar_tensor_tensor(tab[:, LA], sp_[:], -1.0, nea[:].rearrange("p (o h) -> p o h", o=1)
                                           .to_broadcast([P, TT, GH]), ALU.mult, ALU.mult).then_inc(la_ready, 1)
            dve.drain()
            nc.vector.tensor_copy(tab[:, GCUM, NT], tab[:, LA, NT])
            dve.wait_ge(g_ready, 1)
            nc.vector.tensor_copy(tab[:, GCUM, 0:NT], GC[:, 0:NT * GH].rearrange("p (t h) -> p t h", t=NT))
            nc.vector.tensor_copy(gl[:], GL[:, 0:NT * GH].rearrange("p (t h) -> p t h", t=NT))
            dve.drain()
            nc.vector.tensor_tensor(dif[:], gl[:], tab[:, GCUM, 0:NT], ALU.subtract).then_inc(dif_ready, 1)
            dve.wait_ge(e_ready, 1)
            nc.vector.tensor_tensor(e8h[:], tab[0:DB, EG, NT].rearrange("a (h o) -> a h o", o=1).to_broadcast([DB, GH, DB]),
                                    m.ident[0:DB, 0:DB].rearrange("a (o b) -> a o b", o=1).to_broadcast([DB, GH, DB]),
                                    ALU.mult).then_inc(eb_in, 1)
            dve.wait_ge(beta_ready, 1)
            nc.vector.tensor_tensor(tab[:, BG], tab[:, BETA], tab[:, EG], ALU.mult)
            dve.wait_ge(eb_ready, 1)
            nc.vector.tensor_copy(d.egb[:].rearrange("p h b -> p (h b)"), EB[:, 0:GH * DB])


def gated_delta(nc, m):
    d = Mem()
    with ExitStack() as ctx:
        def alloc(name, shape):
            return ctx.enter_context(nc.sbuf_tensor("d_" + name, shape, F32))

        d.tab = alloc("tab", [P, NPAR, TT, GH])
        d.egb = alloc("egb", [P, GH, DB])
        d.ut = alloc("ut", [P, P])
        gdn_decays(nc, m, d)
        gdn_heads(nc, m, d)


def gdn_heads(nc, m, d):
    with Stage(nc) as ctx:
        sb = lambda n, s: ctx.enter_context(nc.sbuf_tensor(f"g_{n}", s, F32))
        pb = lambda n: ctx.enter_context(nc.psum_tensor(f"g_{n}", [P, 512], F32))
        sem = lambda n: ctx.sem(f"g_{n}")
        two = lambda n: [sem(f"{n}{e}") for e in range(2)]
        four = lambda ap: ap.rearrange("p (c n) -> p c n", c=NT)
        bc = lambda ap, n: ap.rearrange("p (c o) -> p c o", o=1).to_broadcast([ap.shape[0], ap.shape[1], n])
        PB = [pb("P0"), pb("P1")]
        X = [[pb(f"X{e}{i}") for i in range(3)] for e in range(2)]
        w = sb("w", [P, 4, KM, P])
        cw = sb("cw", [P, GH, 13])
        mneg = sb("mneg", [P, P])
        lvl = sb("lvl", [P, LEVELS, P])
        d8, ones = sb("d8", [P, DB, DB]), sb("ones", [P, P])
        km = sb("km", [DB, DB, P])
        zs = sb("zs", [P, P])
        cs = sb("cs", [3 * DB, 2, 3, P])
        state = sb("state", [P, 2, DB, P])
        zT = sb("zT", [P, 2, 3, 3 + TOK])
        cvo = sb("cvo", [3 + DB, 2, 3, P])
        EB = []
        for e in range(2):
            b = Mem()
            b.par, b.hw = sb(f"par{e}", [P, NPAR, TT]), sb(f"hw{e}", [P, 13])
            b.cT = sb(f"cT{e}", [P, 3, TOK])
            b.csx, b.cpr = sb(f"csx{e}", [P, 3, 4, DB]), sb(f"cpr{e}", [P, 3, 4, DB])
            b.ss, b.ms, b.sd, b.rs = (sb(f"{n}{e}", [P, 2, TT]) for n in ("ss", "ms", "sd", "rs"))
            b.oss, b.oms, b.osd, b.ors = (sb(f"{n}{e}", [P, TT]) for n in ("oss", "oms", "osd", "ors"))
            b.cf = sb(f"cf{e}", [P, 6, TT])
            b.tk = sb(f"tk{e}", [P, 6, NT, P])
            b.vb = sb(f"vb{e}", [P, NT, P])
            b.stok = sb(f"stok{e}", [DB, 3, P])
            b.sqs, b.qks, b.us = sb(f"sqs{e}", [DB, 2, P]), sb(f"qks{e}", [DB, 2, P]), sb(f"us{e}", [DB, P])
            b.qkT = sb(f"qkT{e}", [P, 4, NT, P])
            b.qkTs, b.qkm = sb(f"qkTs{e}", [P, 2, DB]), sb(f"qkm{e}", [P, 2, DB, DB])
            b.BT = sb(f"BT{e}", [P, 2, NT, P])
            b.S = sb(f"S{e}", [P, NT, P])
            b.sq = b.tk[:, 4:6]
            b.ltab, b.BT1 = b.BT[:, 0], b.BT[:, 1]
            b.T, b.U, b.P1 = (four(b.cT[:, i, 0:SEQ]) for i in range(3))
            b.LT, b.att, b.dt, b.nsk = (b.tk[:, i] for i in range(4))
            b.u, b.on, b.ons = b.qkT[:, 1], b.qkT[:, 2], b.us
            EB.append(b)
        w_in, zs_ready, zs_copied, zst_ready, zst_copied, z_ready, z_copied = (
            sem(n) for n in ("w_in", "zs_ready", "zs_copied", "zst_ready", "zst_copied", "z_ready", "z_copied"))
        c_in, shifted, cleared = sem("c_in"), sem("shifted"), sem("cleared")
        cs_in, st_in, st_out, S_out, cv_out = (two(n) for n in ("cs_in", "st_in", "st_out", "S_out", "cv_out"))
        cst_ready, cst_used, cvo_ready, cvo_copied, conv_ready, silu_ready = (
            two(n) for n in ("cst_ready", "cst_used", "cvo_ready", "cvo_copied", "conv_ready", "silu_ready"))
        tok_ready, stok_copied, v_ready, sq_ready, ms_ready, sd_ready, scaled, kt_ready, kt_copied = (
            two(n) for n in ("tok_ready", "stok_copied", "v_ready", "sq_ready", "ms_ready", "sd_ready", "scaled",
                             "kt_ready", "kt_copied"))
        par_ready, ltab_ready, dg_ready, qg_copied, qkm_ready, dgm_ready, dt_ready, kk_ready, lt_ready, b1_ready = (
            two(n) for n in ("par_ready", "ltab_ready", "dg_ready", "qg_copied", "qkm_ready", "dgm_ready", "dt_ready",
                             "kk_ready", "lt_ready", "b1_ready"))
        bt_ready, bts_ready, tu_ready, p1_ready, p1_copied, lv_ready, solk_ready, nsk_ready = (
            two(n) for n in ("bt_ready", "bts_ready", "tu_ready", "p1_ready", "p1_copied", "lv_ready", "solk_ready",
                             "nsk_ready"))
        u_ready, u_copied, sp_ready, S_ready, o_ready = (
            two(n) for n in ("u_ready", "u_copied", "sp_ready", "S_ready", "o_ready"))
        sgs_ready, ks_ready, us_ready, outer_ready, sn_ready, os_ready = (
            two(n) for n in ("sgs_ready", "ks_ready", "us_ready", "outer_ready", "sn_ready", "os_ready"))
        osq_ready, oms_ready, osd_ready, on_ready, ont_ready, og_ready = (
            two(n) for n in ("osq_ready", "oms_ready", "osd_ready", "on_ready", "ont_ready", "og_ready"))
        block = ctx.enter_context(nc.Block())
        NL = LEVELS - 1
        NPAIR = GH // 2
        FS = (3, 0, 1, 2)

        def slots(eng, slot):
            slot(None, 0)
            with eng.Fori(0, NPAIR - 1) as p:
                slot(p, p + 1)
            slot(NPAIR - 1, None)

        conv_in = m.state_l2_conv.rearrange("b j (c h n) -> j b c h n", c=3, h=GH)
        conv_s = m.conv_sample.rearrange("b j (c h n) -> b j c h n", c=3, h=GH)
        conv_p = m.conv_prompt[0].rearrange("j (c h n) -> j c h n", c=3, h=GH)

        @block.sync
        def _(sp):
            for dst, src in ((cw, m.c_conv), (mneg, m.c_mneg), (lvl, m.c_lvl), (d8, m.c_d8)):
                sp.dma_start(dst[:], src).then_inc(c_in, 16)
            sp.dma_start(w[:], m.w_in[2][0]).then_inc(w_in, 16)
            with sp.Fori(0, GH - 1) as h:
                sp.wait_ge(zs_ready, h + 1)
                sp.dma_start(w[:], m.w_in[2][bass.ds(h + 1, 1)].rearrange("a p f k n -> p (a f) k n")).then_inc(w_in, 16)

        @block.gpsimd
        def _(pool):
            nc.gpsimd.memset(ones[:], 1.0)
            nc.gpsimd.memset(zT[:], 0.0).then_inc(cleared, 1)
            pool.dma_start(m.conv_sample[:, 0:2], m.state_l2_conv[:, 1:3]).then_inc(shifted, 16)

            def load(e, one):
                for j in range(3):
                    pool.dma_start(cs[j * DB:(j + 1) * DB, e], conv_in[j, :, :, one].rearrange("b c a n -> b (c a) n")
                                   ).then_inc(cs_in[e], 16)
                pool.dma_start(state[:, e], m.state_l2_gdn[:, one].rearrange("b a k v -> k (b a) v")).then_inc(st_in[e], 16)

            def early(p, e):
                b = EB[e]
                pool.wait_ge(par_ready[e], p + 1)
                nc.gpsimd.tensor_tensor(b.ltab, d.ut[:].rearrange("p (o n) -> p o n", o=1).to_broadcast([P, NT, P]),
                                        bc(b.par[:, LA, 0:NT], P), ALU.mult).then_inc(ltab_ready[e], 1)

            def level(p, e, li):
                b = EB[e]
                if li == 0:
                    pool.wait_ge(lt_ready[e], p + 1)
                    pool.wait_ge(dg_ready[e], p + 1)
                elif li == 1:
                    pool.wait_ge(tu_ready[e], LEVELS * p + 1)
                else:
                    pool.wait_ge(p1_ready[e], NL * p + li - 1)
                nc.gpsimd.tensor_tensor(b.BT[:, li % 2], b.LT, lvl[:, li + 1:li + 2].to_broadcast([P, NT, P]),
                                        ALU.mult).then_inc(bts_ready[e], 1)

            def stores(p, e, one):
                pool.wait_ge(c_in, 64)
                pool.wait_ge(cvo_copied[e], p + 1)
                pool.dma_start(conv_p[:, :, one].rearrange("j c a n -> j (c a) n"), cvo[0:3, e]).then_inc(cv_out[e], 16)
                pool.dma_start(conv_s[:, 2, :, one].rearrange("b c a n -> b (c a) n"), cvo[3:3 + DB, e]
                               ).then_inc(cv_out[e], 16)

            def late_stores(p, e, one):
                pool.wait_ge(c_in, 64)
                pool.wait_ge(S_ready[e], NT * p + NT)
                pool.dma_start(row(m.gdn_prompt[0, one]), EB[e].S[:, NT - 1]).then_inc(S_out[e], 16)
                pool.wait_ge(c_in, 64)
                pool.wait_ge(sn_ready[e], p + 1)
                pool.dma_start(m.gdn_sample[:, one].rearrange("b a k v -> k (b a) v"), state[:, e]).then_inc(st_out[e], 16)

            def mix(p, last):
                one = [bass.ds(2 * p + e, 1) for e in range(2)]
                for e in range(2):
                    early(p, e)
                for e in range(2):
                    stores(p, e, one[e])
                for li in range(NL):
                    for e in range(2):
                        level(p, e, li)
                for e in range(2):
                    late_stores(p, e, one[e])
                if not last:
                    for e in range(2):
                        pool.wait_ge(c_in, 64)
                        pool.wait_ge(st_out[e], 16 * p + 16)
                        pool.wait_ge(os_ready[e], p + 1)
                        load(e, bass.ds(2 * p + 2 + e, 1))

            for e in range(2):
                load(e, bass.ds(e, 1))
            pool.wait_ge(c_in, 64)
            with pool.Fori(0, NPAIR - 1) as p:
                mix(p, False)
            mix(NPAIR - 1, True)
            for e in range(2):
                pool.wait_ge(st_out[e], 16 * NPAIR)
                pool.wait_ge(S_out[e], 16 * NPAIR)
                pool.wait_ge(cv_out[e], 32 * NPAIR)
            pool.wait_ge(shifted, 16)

        @block.tensor
        def _(pe):
            ID = m.ident

            def project(q, e, i):
                if q is None:
                    return
                h = 2 * q + e
                if i == 0:
                    pe.wait_ge(w_in, h * 16 + 16)
                    pe.wait_ge(zs_copied, h)
                elif i == 1:
                    pe.wait_ge(zst_copied, h)
                else:
                    pe.wait_ge(z_copied, 4 * h + i - 1)
                for k in range(KM):
                    last = nc.tensor.matmul(PB[i % 2][:], w[:, FS[i], k], m.hT[:, k, 0:SEQ], start=(k == 0),
                                            stop=(k == KM - 1))
                last.then_inc(z_ready, 1)

            def project_samples(q, e):
                if q is None:
                    return
                h = 2 * q + e
                pe.wait_ge(z_copied, 4 * h + 3)
                for k in range(KM):
                    for f in range(4):
                        last = nc.tensor.matmul(PB[0][32 * f:32 * f + DB, 0:P], m.hT[:, k, SEQ:TOK], w[:, f, k],
                                                start=(k == 0), stop=(k == KM - 1))
                last.then_inc(zs_ready, 1)

            def turn_samples(q, e):
                if q is None:
                    return
                h = 2 * q + e
                pe.wait_ge(zs_copied, h + 1)
                pe.wait_ge(z_copied, 4 * h + 4)
                nc.tensor.transpose(PB[1][:, 0:P], zs[:], ID[:]).then_inc(zst_ready, 1)

            def conv_rows(p, e):
                pe.wait_ge(cs_in[e], p * 48 + 48)
                pe.wait_ge(og_ready[e], p)
                for c in range(3):
                    last = nc.tensor.matmul(X[e][0][:, c * 3 * DB:(c + 1) * 3 * DB], cs[:, e, c], ID[0:3 * DB, 0:3 * DB],
                                            start=True, stop=True)
                last.then_inc(cst_ready[e], 1)
                pe.wait_ge(zst_copied, 2 * p + e + 1)
                for c in range(3):
                    last = nc.tensor.transpose(X[e][1][0:3 + DB, c * P:(c + 1) * P], zT[:, e, c, SEQ:SEQ + 3 + DB], ID[:])
                last.then_inc(cvo_ready[e], 1)

            def tokens(p, e):
                b = EB[e]
                pe.wait_ge(silu_ready[e], p + 1)
                pe.wait_ge(cst_used[e], p + 1)
                pe.wait_ge(cvo_copied[e], p + 1)
                for c in range(3):
                    nc.tensor.transpose(X[e][2][0:DB, c * P:(c + 1) * P], b.cT[:, c, SEQ:TOK], ID[:])
                for c in range(2):
                    for t in range(NT):
                        last = nc.tensor.transpose(X[e][c][:, t * P:(t + 1) * P], b.cT[:, c, t * P:(t + 1) * P], ID[:])
                last.then_inc(tok_ready[e], 1)

            def tokens_v(p, e):
                b = EB[e]
                pe.wait_ge(stok_copied[e], p + 1)
                for t in range(NT):
                    last = nc.tensor.transpose(X[e][2][:, t * P:(t + 1) * P], b.cT[:, 2, t * P:(t + 1) * P], ID[:])
                last.then_inc(v_ready[e], 1)

            def turned_back(p, e):
                b = EB[e]
                pe.wait_ge(scaled[e], p + 1)
                for bank, i in ((0, 2), (1, 3), (2, 1)):
                    for t in range(NT):
                        last = nc.tensor.transpose(X[e][bank][:, t * P:(t + 1) * P], b.tk[:, i, t], ID[:])
                last.then_inc(kt_ready[e], 1)

            def decays(p, e):
                b = EB[e]
                pe.wait_ge(kt_copied[e], p + 1)
                for t in range(NT):
                    nc.tensor.transpose(X[e][0][:, t * P:(t + 1) * P], b.tk[:, 0, t], ID[:])
                for i in range(2):
                    nc.tensor.matmul(X[e][2][:, i * DB:(i + 1) * DB], b.qks[:, i], ID[0:DB, 0:DB], start=True, stop=True)
                pe.wait_ge(ltab_ready[e], p + 1)
                nc.tensor.matmul(X[e][1][:], ones[:], b.ltab.rearrange("p c n -> p (c n)"), start=True, stop=True
                                 ).then_inc(dg_ready[e], 1)

            def scores(p, e):
                b = EB[e]
                pe.wait_ge(qg_copied[e], p + 1)
                pe.wait_ge(dgm_ready[e], p + 1)
                for t in range(NT):
                    nc.tensor.matmul(X[e][0][:, t * P:(t + 1) * P], b.qkT[:, 2, t], b.qkT[:, 3, t], start=True, stop=True)
                    last = nc.tensor.matmul(X[e][1][:, t * P:(t + 1) * P], b.qkT[:, 2, t], b.qkT[:, 1, t],
                                            start=True, stop=True)
                last.then_inc(kk_ready[e], 1)

            def first_blocks(p, e):
                b = EB[e]
                pe.wait_ge(b1_ready[e], p + 1)
                pe.wait_ge(qkm_ready[e], p + 1)
                for t in range(NT):
                    last = nc.tensor.transpose(X[e][2][:, t * P:(t + 1) * P], b.BT1[:, t], ID[:])
                last.then_inc(bt_ready[e], 1)

            def level_a(p, e, li):
                b = EB[e]
                pe.wait_ge(tu_ready[e], LEVELS * p + li + 1)
                pe.wait_ge(bts_ready[e], NL * p + li + 1)
                for t in range(NT):
                    last = nc.tensor.matmul(X[e][0][:, t * P:(t + 1) * P], b.BT[:, li % 2, t], b.T[:, t], start=True, stop=True)
                last.then_inc(p1_ready[e], 1)

            def level_b(p, e, li):
                b = EB[e]
                pe.wait_ge(p1_copied[e], NL * p + li + 1)
                for t in range(NT):
                    last = nc.tensor.matmul(X[e][1][:, t * P:(t + 1) * P], b.P1[:, t], b.U[:, t], start=True, stop=True)
                if li < NL - 1:
                    for t in range(NT):
                        last = nc.tensor.matmul(X[e][2][:, t * P:(t + 1) * P], b.U[:, t], b.P1[:, t], start=True, stop=True)
                last.then_inc(lv_ready[e], 1)

            def solve_keys(p, e):
                b = EB[e]
                pe.wait_ge(tu_ready[e], LEVELS * p + LEVELS)
                for t in range(NT):
                    last = nc.tensor.matmul(X[e][0][:, t * P:(t + 1) * P], b.tk[:, 4, t], b.U[:, t], start=True, stop=True)
                last.then_inc(solk_ready[e], 1)

            def chunk_a(p, e, c):
                b = EB[e]
                if c == 0:
                    pe.wait_ge(nsk_ready[e], p + 1)
                else:
                    pe.wait_ge(S_ready[e], NT * p + c)
                cc = slice(c * P, (c + 1) * P)
                last = nc.tensor.matmul(X[e][1][:, cc], b.U[:, c], b.vb[:, c], start=True, stop=(c == 0))
                if c > 0:
                    last = nc.tensor.matmul(X[e][1][:, cc], b.nsk[:, c], b.S[:, c - 1], start=False, stop=True)
                last.then_inc(u_ready[e], 1)

            def chunk_b(p, e, c):
                b = EB[e]
                cc = slice(c * P, (c + 1) * P)
                pe.wait_ge(u_copied[e], NT * p + c + 1)
                nc.tensor.matmul(X[e][1][:, cc], b.tk[:, 5, c], b.u[:, c], start=True, stop=True).then_inc(sp_ready[e], 1)
                last = nc.tensor.matmul(X[e][2][:, cc], b.att[:, c], b.u[:, c], start=True, stop=(c == 0))
                if c > 0:
                    last = nc.tensor.matmul(X[e][2][:, cc], b.qkT[:, 0, c], b.S[:, c - 1], start=False, stop=True)
                if c == NT - 1:
                    last.then_inc(o_ready[e], 1)

            def samples_a(p, e):
                b = EB[e]
                pe.wait_ge(sgs_ready[e], p + 1)
                for n in range(DB):
                    last = nc.tensor.matmul(X[e][0][0:DB, 0:P], b.qkm[:, 1, n], state[:, e, n], start=(n == 0),
                                            stop=(n == DB - 1))
                last.then_inc(ks_ready[e], 1)

            def samples_b(p, e):
                b = EB[e]
                pe.wait_ge(us_ready[e], p + 1)
                pe.wait_ge(S_ready[e], NT * p + NT)
                for n in range(DB):
                    last = nc.tensor.matmul(X[e][n // 4][:, (n % 4) * P:(n % 4 + 1) * P], km[:, n], b.us[:],
                                            start=True, stop=True)
                last.then_inc(outer_ready[e], 1)

            def samples_c(p, e):
                b = EB[e]
                pe.wait_ge(sn_ready[e], p + 1)
                for n in range(DB):
                    last = nc.tensor.matmul(X[e][0][0:DB, 0:P], b.qkm[:, 0, n], state[:, e, n], start=(n == 0),
                                            stop=(n == DB - 1))
                last.then_inc(os_ready[e], 1)

            def outputs(p, e):
                b = EB[e]
                pe.wait_ge(on_ready[e], p + 1)
                for t in range(NT):
                    nc.tensor.transpose(X[e][1][:, t * P:(t + 1) * P], b.on[:, t], ID[:])
                nc.tensor.matmul(X[e][0][:, 0:DB], b.ons[:], ID[0:DB, 0:DB], start=True, stop=True).then_inc(ont_ready[e], 1)

            def slot(p, q):
                def both(step, *a):
                    if p is not None:
                        step(p, 0, *a)
                        step(p, 1, *a)

                both(conv_rows)
                project(q, 0, 0)
                both(tokens)
                project(q, 0, 1)
                both(tokens_v)
                both(turned_back)
                project(q, 0, 2)
                both(decays)
                both(scores)
                project(q, 0, 3)
                both(first_blocks)
                project_samples(q, 0)
                for li in range(NL):
                    both(level_a, li)
                    if li == 0:
                        turn_samples(q, 0)
                    if li == 1:
                        project(q, 1, 0)
                    both(level_b, li)
                    if li == 3:
                        project(q, 1, 1)
                both(solve_keys)
                project(q, 1, 2)
                for c in range(NT):
                    both(chunk_a, c)
                    if c == 0:
                        both(samples_a)
                    both(chunk_b, c)
                    if c == 2:
                        project(q, 1, 3)
                both(samples_b)
                project_samples(q, 1)
                both(samples_c)
                turn_samples(q, 1)
                both(outputs)

            pe.wait_ge(cleared, 1)
            slots(pe, slot)

        @block.scalar
        def _(act):
            def projected(q, e, i):
                if q is None:
                    return
                h = 2 * q + e
                act.wait_ge(z_ready, 4 * h + i + 1)
                if FS[i] == 3:
                    nc.scalar.activation(m.ogT[:, bass.ds(h, 1), 0:SEQ].rearrange("p a n -> p (a n)"), PB[i % 2][:],
                                         ACT.Silu).then_inc(z_copied, 1)
                else:
                    if i == 1:
                        act.wait_ge(conv_ready[e], 4 * q)
                        act.wait_ge(cvo_ready[e], q)
                    nc.scalar.copy(zT[:, e, FS[i], 3:3 + SEQ], PB[i % 2][:]).then_inc(z_copied, 1)

            def projected_samples(q, e):
                if q is None:
                    return
                h = 2 * q + e
                act.wait_ge(zs_ready, h + 1)
                act.wait_ge(zst_ready, h)
                nc.scalar.copy(zs[:], PB[0][:, 0:P]).then_inc(zs_copied, 1)

            def turned_samples(q, e):
                if q is None:
                    return
                h = 2 * q + e
                act.wait_ge(zst_ready, h + 1)
                z = four(PB[1][:])[:, 0].rearrange("p (f n) -> p f n", f=4)
                nc.scalar.copy(zT[:, e, :, 3 + SEQ:3 + TOK], z[:, 0:3, 0:DB])
                nc.scalar.activation(m.ogT[:, bass.ds(h, 1), SEQ:TOK].rearrange("p a n -> p (a n)"), z[:, 3, 0:DB],
                                     ACT.Silu).then_inc(zst_copied, 1)

            def conv_out(p, e):
                act.wait_ge(cvo_ready[e], p + 1)
                act.wait_ge(cv_out[e], 32 * p)
                nc.scalar.copy(cvo[:, e].rearrange("r c n -> r (c n)"), X[e][1][0:3 + DB, 0:3 * P]).then_inc(cvo_copied[e], 1)

            def silu(p, e):
                b = EB[e]
                for c in range(3):
                    act.wait_ge(conv_ready[e], 4 * p + c + 1)
                    nc.scalar.activation(b.cT[:, c, 0:SEQ], b.cT[:, c, 0:SEQ], ACT.Silu)
                act.wait_ge(conv_ready[e], 4 * p + 4)
                nc.scalar.activation(b.cT[:, :, SEQ:TOK], b.cT[:, :, SEQ:TOK], ACT.Silu).then_inc(silu_ready[e], 1)

            def squares(p, e):
                b = EB[e]
                act.wait_ge(tok_ready[e], p + 1)
                nc.scalar.copy(b.stok[:], X[e][2][0:DB, 0:3 * P].rearrange("b (c n) -> b c n", c=3)
                               ).then_inc(stok_copied[e], 1)
                for c in range(2):
                    nc.scalar.activation(b.sq[:, c], four(X[e][c][:]), ACT.Square)
                act.drain()
                nc.scalar.activation(b.sqs[:], b.stok[:, 0:2], ACT.Square).then_inc(sq_ready[e], 1)

            def root(p, e):
                act.wait_ge(ms_ready[e], p + 1)
                nc.scalar.activation(EB[e].sd[:], EB[e].ms[:], ACT.Sqrt).then_inc(sd_ready[e], 1)

            def turned_back(p, e):
                act.wait_ge(kt_ready[e], p + 1)
                for bank, i in ((0, 2), (1, 3), (2, 1)):
                    last = nc.scalar.copy(EB[e].qkT[:, i], four(X[e][bank][:]))
                last.then_inc(kt_copied[e], 1)

            def decays(p, e):
                b = EB[e]
                act.wait_ge(dg_ready[e], p + 1)
                nc.scalar.copy(b.qkT[:, 0], four(X[e][0][:])).then_inc(qg_copied[e], 1)

            def exps(p, e):
                b = EB[e]
                act.wait_ge(dgm_ready[e], p + 1)
                nc.scalar.activation(b.dt, b.dt, ACT.Exp).then_inc(dt_ready[e], 1)

            def level(p, e, li):
                act.wait_ge(p1_ready[e], NL * p + li + 1)
                nc.scalar.copy(EB[e].P1, four(X[e][0][:])).then_inc(p1_copied[e], 1)

            def solve_keys(p, e):
                act.wait_ge(solk_ready[e], p + 1)
                nc.scalar.mul(EB[e].nsk, four(X[e][0][:]), -1.0).then_inc(nsk_ready[e], 1)

            def chunk(p, e, c):
                act.wait_ge(u_ready[e], NT * p + c + 1)
                nc.scalar.copy(EB[e].u[:, c], X[e][1][:, c * P:(c + 1) * P]).then_inc(u_copied[e], 1)

            def out_squares(p, e):
                b = EB[e]
                act.wait_ge(o_ready[e], p + 1)
                act.wait_ge(os_ready[e], p + 1)
                nc.scalar.activation(b.sq[:, 0], four(X[e][2][:]), ACT.Square)
                nc.scalar.activation(b.sqs[:, 0], X[e][0][0:DB, 0:P], ACT.Square).then_inc(osq_ready[e], 1)

            def out_root(p, e):
                act.wait_ge(oms_ready[e], p + 1)
                nc.scalar.activation(EB[e].osd[:], EB[e].oms[:], ACT.Sqrt).then_inc(osd_ready[e], 1)

            def slot(p, q):
                def both(step, *a):
                    if p is not None:
                        step(p, 0, *a)
                        step(p, 1, *a)

                both(conv_out)
                both(silu)
                projected(q, 0, 0)
                both(squares)
                projected(q, 0, 1)
                both(root)
                both(turned_back)
                projected(q, 0, 2)
                both(decays)
                both(exps)
                projected(q, 0, 3)
                for li in range(NL):
                    if li == 0:
                        projected_samples(q, 0)
                    both(level, li)
                    if li == 0:
                        turned_samples(q, 0)
                    if li == 1:
                        projected(q, 1, 0)
                    if li == 3:
                        projected(q, 1, 1)
                both(solve_keys)
                projected(q, 1, 2)
                for c in range(NT):
                    both(chunk, c)
                    if c == 2:
                        projected(q, 1, 3)
                projected_samples(q, 1)
                both(out_squares)
                turned_samples(q, 1)
                both(out_root)

            act.wait_ge(cleared, 1)
            slots(act, slot)

        @block.vector
        def _(dve):
            dve.wait_ge(c_in, 64)
            for b in EB:
                nc.vector.memset(b.ss[:], 1.0)
                nc.vector.memset(b.oss[:], 1.0)
            dve.drain()
            idb = m.ident[:].rearrange("p (o n) -> p o n", o=1).to_broadcast([P, NT, P])

            def parameters(p, e):
                b, one = EB[e], bass.ds(2 * p + e, 1)
                nc.vector.tensor_copy(b.par[:], d.tab[:, :, :, one].rearrange("p a t h -> p a (t h)")
                                      ).then_inc(par_ready[e], 1)
                nc.vector.tensor_copy(b.hw[:], cw[:, one].rearrange("p h n -> p (h n)"))

            def conv(p, e, c):
                b = EB[e]
                dve.wait_ge(zst_copied, 2 * p + e + 1)
                y = b.cT[:, c, 0:SEQ]
                last = nc.vector.tensor_scalar(y, zT[:, e, c, 0:SEQ], b.hw[:, 4 * c:4 * c + 1], None, ALU.mult)
                for j in range(1, 4):
                    dve.drain()
                    last = nc.vector.scalar_tensor_tensor(y, zT[:, e, c, j:j + SEQ], b.hw[:, 4 * c + j:4 * c + j + 1], y,
                                                          ALU.mult, ALU.add)
                last.then_inc(conv_ready[e], 1)

            def conv_samples(p, e):
                b = EB[e]
                dve.wait_ge(cst_ready[e], p + 1)
                nc.vector.tensor_copy(b.csx[:, :, 0:3], X[e][0][:, 0:9 * DB].rearrange("p (c j b) -> p c j b", c=3, j=3)
                                      ).then_inc(cst_used[e], 1)
                nc.vector.tensor_copy(b.csx[:, :, 3], zT[:, e, :, 3 + SEQ:3 + TOK])
                dve.drain()
                nc.vector.tensor_tensor(b.cpr[:].rearrange("p c j b -> p (c j) b"), b.csx[:].rearrange("p c j b -> p (c j) b"),
                                        bc(b.hw[:, 0:12], DB), ALU.mult)
                dve.drain()
                nc.vector.tensor_reduce(b.cT[:, :, SEQ:TOK], b.cpr[:].rearrange("p c j b -> p c b j"), axis=AX, op=ALU.add
                                        ).then_inc(conv_ready[e], 1)

            def sums(p, e):
                b = EB[e]
                dve.wait_ge(sq_ready[e], p + 1)
                nc.vector.tensor_reduce(b.ss[:, :, 0:NT], b.sq, axis=AX, op=ALU.add)
                nc.vector.tensor_reduce(b.ss[0:DB, :, NT], b.sqs[:], axis=AX, op=ALU.add)
                dve.drain()
                nc.vector.tensor_scalar(b.ms[:], b.ss[:], EPS, None, ALU.add).then_inc(ms_ready[e], 1)

            def scale(p, e):
                b = EB[e]
                dve.wait_ge(sd_ready[e], p + 1)
                nc.vector.reciprocal(b.rs[:], b.sd[:])
                dve.drain()
                nc.vector.tensor_scalar(b.rs[:, 0], b.rs[:, 0], P ** -0.5, None, ALU.mult)
                dve.drain()
                nc.vector.tensor_tensor(b.cf[:, 0:2], b.par[:, EG:ONE + 1], b.rs[:, 0:1].to_broadcast([P, 2, TT]), ALU.mult)
                nc.vector.tensor_tensor(b.cf[:, 2:6], b.par[:, ONE:EKD + 1], b.rs[:, 1:2].to_broadcast([P, 4, TT]), ALU.mult)
                dve.drain()
                for i in range(6):
                    nc.vector.tensor_tensor(b.tk[:, i], four(X[e][0 if i < 2 else 1][:]), bc(b.cf[:, i, 0:NT], P), ALU.mult)
                nc.vector.tensor_scalar(b.qks[:, 0], b.stok[:, 0], b.cf[0:DB, 1, NT:TT], None, ALU.mult)
                nc.vector.tensor_scalar(b.qks[:, 1], b.stok[:, 1], b.cf[0:DB, 2, NT:TT], None, ALU.mult)
                dve.wait_ge(v_ready[e], p + 1)
                nc.vector.tensor_tensor(b.vb[:], four(X[e][2][:]), bc(b.par[:, BETA, 0:NT], P), ALU.mult
                                        ).then_inc(scaled[e], 1)

            def decay_state(p, e):
                dve.wait_ge(st_in[e], p * 16 + 16)
                one = bass.ds(2 * p + e, 1)
                nc.vector.tensor_tensor(state[:, e], state[:, e], bc(d.egb[:, one].rearrange("p h b -> p (h b)"), P),
                                        ALU.mult).then_inc(sgs_ready[e], 1)

            def decays(p, e):
                b = EB[e]
                dve.wait_ge(dg_ready[e], p + 1)
                nc.vector.tensor_tensor(b.dt, four(X[e][1][:]), bc(b.par[:, GCUM, 0:NT], P), ALU.subtract)
                nc.vector.tensor_copy(b.qkTs[:].rearrange("p i b -> p (i b)"), X[e][2][:, 0:2 * DB])
                dve.drain()
                nc.vector.scalar_tensor_tensor(b.dt, b.dt, 0.0, mneg[:].rearrange("p (o n) -> p o n", o=1)
                                               .to_broadcast([P, NT, P]), ALU.min, ALU.add).then_inc(dgm_ready[e], 1)
                for i in range(2):
                    last = nc.vector.tensor_tensor(b.qkm[:, i], b.qkTs[:, i:i + 1].to_broadcast([P, DB, DB]), d8[:], ALU.mult)
                last.then_inc(qkm_ready[e], 1)

            def scores(p, e):
                b = EB[e]
                dve.wait_ge(dt_ready[e], p + 1)
                dve.wait_ge(kk_ready[e], p + 1)
                nc.vector.tensor_tensor(b.LT, four(X[e][0][:]), b.dt, ALU.mult).then_inc(lt_ready[e], 1)
                nc.vector.tensor_tensor(b.att, four(X[e][1][:]), b.dt, ALU.mult)
                dve.drain()
                nc.vector.tensor_tensor(b.BT1, b.LT, lvl[:, 0:1].to_broadcast([P, NT, P]), ALU.mult).then_inc(b1_ready[e], 1)
                dve.drain()
                nc.vector.tensor_tensor(b.U, idb, b.BT1, ALU.subtract)

            def first_blocks(p, e):
                b = EB[e]
                dve.wait_ge(bt_ready[e], p + 1)
                nc.vector.tensor_tensor(b.T, idb, four(X[e][2][:]), ALU.subtract).then_inc(tu_ready[e], 1)

            def level(p, e, li):
                b = EB[e]
                dve.wait_ge(lv_ready[e], NL * p + li + 1)
                last = nc.vector.tensor_tensor(b.U, b.U, four(X[e][1][:]), ALU.subtract)
                if li < NL - 1:
                    last = nc.vector.tensor_tensor(b.T, b.T, four(X[e][2][:]), ALU.subtract)
                last.then_inc(tu_ready[e], 1)

            def chunk(p, e, c):
                b = EB[e]
                dve.wait_ge(sp_ready[e], NT * p + c + 1)
                sp_c = X[e][1][:, c * P:(c + 1) * P]
                if c == 0:
                    dve.wait_ge(S_out[e], 16 * p)
                    nc.vector.tensor_copy(b.S[:, 0], sp_c).then_inc(S_ready[e], 1)
                else:
                    nc.vector.scalar_tensor_tensor(b.S[:, c], b.S[:, c - 1], b.par[:, EGL, c:c + 1], sp_c, ALU.mult,
                                                   ALU.add).then_inc(S_ready[e], 1)

            def samples_a(p, e):
                b = EB[e]
                dve.wait_ge(outer_ready[1 - e], p + e)
                nc.vector.tensor_tensor(km[:], b.qks[:, 1:2].to_broadcast([DB, DB, P]),
                                        m.ident[0:DB, 0:DB].rearrange("a (b o) -> a b o", o=1).to_broadcast([DB, DB, P]),
                                        ALU.mult)
                dve.wait_ge(ks_ready[e], p + 1)
                nc.vector.tensor_tensor(b.us[:], b.stok[:, 2], X[e][0][0:DB, 0:P], ALU.subtract)
                dve.drain()
                nc.vector.tensor_scalar(b.us[:], b.us[:], b.par[0:DB, BETA, NT:TT], None, ALU.mult).then_inc(us_ready[e], 1)

            def samples_b(p, e):
                dve.wait_ge(outer_ready[e], p + 1)
                for q in range(2):
                    st = state[:, e, 4 * q:4 * q + 4]
                    last = nc.vector.tensor_tensor(st, st, four(X[e][q][:]), ALU.add)
                last.then_inc(sn_ready[e], 1)

            def out_sums(p, e):
                b = EB[e]
                dve.wait_ge(osq_ready[e], p + 1)
                nc.vector.tensor_reduce(b.oss[:, 0:NT], b.sq[:, 0], axis=AX, op=ALU.add)
                nc.vector.tensor_reduce(b.oss[0:DB, NT:TT], b.sqs[:, 0], axis=AX, op=ALU.add)
                dve.drain()
                nc.vector.tensor_scalar(b.oms[:], b.oss[:], 1.0 / P, EPS, ALU.mult, ALU.add).then_inc(oms_ready[e], 1)

            def out_scale(p, e):
                b = EB[e]
                dve.wait_ge(osd_ready[e], p + 1)
                nc.vector.reciprocal(b.ors[:], b.osd[:])
                dve.drain()
                nc.vector.tensor_tensor(b.on, four(X[e][2][:]), bc(b.ors[:, 0:NT], P), ALU.mult)
                nc.vector.tensor_scalar(b.ons[:], X[e][0][0:DB, 0:P], b.ors[0:DB, NT:TT], None, ALU.mult
                                        ).then_inc(on_ready[e], 1)

            def outputs(p, e):
                b, one = EB[e], bass.ds(2 * p + e, 1)
                dve.wait_ge(ont_ready[e], p + 1)
                og = m.ogT[:, one, 0:SEQ].rearrange("p h n -> p (h n)")
                nc.vector.scalar_tensor_tensor(og, X[e][1][:], b.hw[:, 12:13], og, ALU.mult, ALU.mult)
                og = m.ogT[:, one, SEQ:TOK].rearrange("p h n -> p (h n)")
                nc.vector.scalar_tensor_tensor(og, X[e][0][:, 0:DB], b.hw[:, 12:13], og, ALU.mult, ALU.mult
                                               ).then_inc(og_ready[e], 1)

            def mix(p):
                def both(step, *a):
                    step(p, 0, *a)
                    step(p, 1, *a)

                dve.drain()
                both(parameters)
                dve.drain()
                for e in range(2):
                    for c in range(3):
                        conv(p, e, c)
                    conv_samples(p, e)
                both(decay_state)
                both(sums)
                both(scale)
                both(decays)
                both(scores)
                both(first_blocks)
                for li in range(NL):
                    both(level, li)
                for c in range(NT):
                    both(chunk, c)
                for e in range(2):
                    samples_a(p, e)
                both(samples_b)
                both(out_sums)
                both(out_scale)
                both(outputs)

            with dve.Fori(0, NPAIR - 1) as p:
                mix(p)
            mix(NPAIR - 1)


def delta_inputs(m, x, give):
    w = x["l2_w_in"]
    v = w[:, 0:4 * DI].reshape(KM, P, 4, GH, P)
    m.w_in[2] = give("l2_w_in", v.transpose(3, 1, 2, 0, 4))
    m.w2_ab = give("l2_w_ab", w[:, 4 * DI:].reshape(KM, P, 2 * GH).transpose(1, 0, 2))
    m.A_log, m.dt_bias = give("l2_A_log", x["l2_A_log"]), give("l2_dt_bias", x["l2_dt_bias"])
    m.state_l2_conv, m.state_l2_gdn = give("state_l2_conv", x["state_l2_conv"]), give("state_l2_gdn", x["state_l2_gdn"])
    taps = x["l2_conv_w"].reshape(4, 3, GH, P).transpose(3, 2, 1, 0).reshape(P, GH, 12)
    m.c_conv = give("l2_conv", np.concatenate([taps, np.broadcast_to(x["l2_onorm"][:, None, None], (P, GH, 1))], 2))
    i = np.arange(P)
    m.c_ut = give("c_ut", (i[:, None] <= i[None, :]).astype(np.float32))
    m.c_mneg = give("c_mneg", np.where(i[:, None] <= i[None, :], 0.0, NEG).astype(np.float32))
    lvl = [(i[None, :] // s % 2 == 1) & (i[:, None] // s == i[None, :] // s - 1) for s in (1 << n for n in range(LEVELS))]
    m.c_lvl = give("c_lvl", np.stack(lvl, 1).astype(np.float32))


def build(nc, m):
    with ExitStack() as ctx:
        sb = lambda n, s: ctx.enter_context(nc.sbuf_tensor(n, s, F32))
        m.xres = sb("xres", [P, TT, DM])
        m.hT = sb("hT", [P, KM, TOK])
        m.ogT = sb("ogT", [P, KI, TOK])
        m.ident = sb("ident", [P, P])
        load_tokens(nc, m)
        mixers = [
            lambda: retention(nc, m, 0, m.state_l0_ret, m.s0_prompt, m.s0_sample, m.w_in[0], m.c_ret[0]),
            lambda: sparse_attention(nc, m),
            lambda: gated_delta(nc, m),
            lambda: retention(nc, m, 3, m.state_l3_ret, m.s3_prompt, m.s3_sample, m.w_in[3], m.c_ret[3]),
        ]
        for layer in range(LAYERS):
            norm_and_transpose(nc, m, layer)
            mixers[layer]()
            output_projection(nc, m, layer)
        store_tokens(nc, m)


def retention_constants():
    out = np.zeros((RH, P, 2 * P + 3), np.float32)
    i = np.arange(P, dtype=np.float64)
    for h in range(RH):
        lg = np.log1p(-np.exp2(-5.0 - h))
        diff = i[None, :] - i[:, None]
        out[h, :, 0:P] = np.where(diff >= 0, np.exp(lg * np.maximum(diff, 0)), 0)
        out[h, :, P:2 * P] = np.exp(lg * (i + 1))[None, :]
        out[h, :, 2 * P] = np.exp(lg * (P - 1 - i))
        out[h, :, 2 * P + 1] = np.exp(lg * P)
        out[h, :, 2 * P + 2] = np.exp(lg)
    return out


def rope_constants(past):
    half = RK // 2
    inv = (np.float32(10000.0) ** (-np.arange(half, dtype=np.float32) / half)).astype(np.float32)
    pos = np.zeros((TT, P), np.float32)
    pos[:NT] = np.arange(SEQ).reshape(NT, P)
    pos[NT] = past
    ang = (pos[..., None] * inv).astype(np.float32).astype(np.float64)
    c, s = np.cos(ang), np.sin(ang)
    sc = RK ** -0.5
    cos = np.concatenate([c, c, c * sc, c * sc], -1)
    sin = np.concatenate([-s, s, -s * sc, s * sc], -1)
    return np.ascontiguousarray(np.stack([cos, sin], 2).transpose(1, 0, 2, 3), dtype=np.float32)


def by_columns(w, pieces):
    v = w.reshape(w.shape[0] // P, P, w.shape[1]).transpose(1, 0, 2)
    return np.stack([np.concatenate([v[:, :, a:b] for a, b in unit], 2) for unit in pieces])


def kernel(**inputs):
    import concourse.bacc as bacc
    from concourse.bass_utils import run_bass_kernel_spmd as run

    x = {k: np.asarray(v) for k, v in inputs.items()}
    nc = bacc.Bacc("TRN2", target_bir_lowering=False, num_devices=1)
    arrays = {}
    m = Mem()

    def give(name, a):
        a = np.ascontiguousarray(a)
        arrays["in_" + name] = a
        return nc.dram_tensor("in_" + name, a.shape, mybir.dt.from_np(a.dtype), kind="ExternalInput").ap()

    outs = []

    def take(*shape):
        name = f"out_{len(outs)}"
        outs.append(name)
        return nc.dram_tensor(name, shape, F32, kind="ExternalOutput").ap()

    m.x_prompt, m.x_sample = give("x_prompt", x["x_prompt"]), give("x_sample", x["x_sample"])
    m.state_l0_ret, m.state_l3_ret = give("state_l0_ret", x["state_l0_ret"]), give("state_l3_ret", x["state_l3_ret"])
    m.norm = [give(f"l{i}_norm", x[f"l{i}_norm"]) for i in range(4)]
    m.w_out = [give(f"l{i}_w_out", x[f"l{i}_w_out"]) for i in range(4)]
    m.w_in, m.c_ret = {}, {}
    heads = [[(RK * h, RK * (h + 1)), (DM + RK * h, DM + RK * (h + 1)), (2 * DM + RV * h, 2 * DM + RV * (h + 1)),
              (2 * DM + DI + RV * h, 2 * DM + DI + RV * (h + 1))] for h in range(RH)]
    for i in (0, 3):
        m.w_in[i] = give(f"l{i}_w_in", by_columns(x[f"l{i}_w_in"], heads))
        gn = x[f"l{i}_gn"].reshape(RH, 2, P).transpose(0, 2, 1)
        m.c_ret[i] = give(f"c_ret{i}", np.concatenate([retention_constants(), gn], 2))
    m.c_ident = give("c_ident", np.eye(P, dtype=np.float32))
    m.c_rope = give("c_rope", rope_constants(1024))
    e = np.eye(DB, dtype=np.float32)
    m.c_d8 = give("c_d8", np.broadcast_to(e, (P, DB, DB)))
    m.c_e8 = give("c_e8", np.broadcast_to(e[:, :, None], (DB, DB, P)))
    sparse_inputs(m, x, give)
    delta_inputs(m, x, give)
    m.y_prompt, m.y_sample = take(1, SEQ, DM), take(DB, 1, DM)
    m.s0_prompt, m.s0_sample = take(1, RH, RK, RV), take(DB, RH, RK, RV)
    m.cmp_prompt, m.cmp_sample = take(1, SEQ, 2, KVH, HD), take(DB, 1, 2, KVH, HD)
    m.slc_prompt, m.slc_sample = take(1, SEQ, 2, KVH, HD), take(DB, 1, 2, KVH, HD)
    m.win_prompt, m.win_sample = take(1, SEQ, 2, KVH, HD), take(DB, 512, 2, KVH, HD)
    m.conv_prompt, m.conv_sample = take(1, 3, 3 * DI), take(DB, 3, 3 * DI)
    m.gdn_prompt, m.gdn_sample = take(1, GH, 128, 128), take(DB, GH, 128, 128)
    m.s3_prompt, m.s3_sample = take(1, RH, RK, RV), take(DB, RH, RK, RV)
    build(nc, m)
    r = run(nc, [arrays], core_ids=[0])
    return tuple(r.results[0][n] for n in outs)
```

```python
from contextlib import ExitStack

import numpy as np
import concourse.bass as bass
from concourse import mybir

F32 = mybir.dt.float32
I32 = mybir.dt.int32
ALU = mybir.AluOpType
ACT = mybir.ActivationFunctionType
AX = mybir.AxisListType.X

P = 128
DM = 1024
KM = DM // P
DI = 2 * DM
KI = DI // P
SEQ = 512
NT = SEQ // P
DB = 8
TT = NT + 1
TOK = SEQ + DB
EPS = 1e-6
NEG = -1e30

RH, RK, RV = 8, 128, 256
NH, KVH, HD = 16, 4, 128
HPG = NH // KVH
CL, CS = 32, 16
GH = 16
LAYERS = 4


class Mem:
    pass


class Stage(ExitStack):

    def __init__(self, nc):
        super().__init__()
        self.nc, self.sems = nc, []
        self.callback(self.clear)

    def sem(self, name):
        self.sems.append(self.nc.alloc_semaphore(name))
        return self.sems[-1]

    def clear(self):
        self.nc.clear_and_free_semaphores(self.sems)
        self.nc.all_engine_barrier()


def row(ap):
    return ap.rearrange("a p n -> p (a n)")


def load_tokens(nc, m):
    with Stage(nc) as ctx:
        zeroed = ctx.sem("zeroed")
        loaded = ctx.sem("loaded")
        block = ctx.enter_context(nc.Block())

        @block.vector
        def _(dve):
            nc.vector.memset(m.xres[:, NT, :], 0.0).then_inc(zeroed, 1)

        @block.sync
        def _(sp):
            sp.dma_start(m.xres[:, 0:NT, :], m.x_prompt.rearrange("b (t p) d -> p (b t) d", p=P)).then_inc(loaded, 16)
            sp.dma_start(m.ident[:], m.c_ident).then_inc(loaded, 16)
            sp.wait_ge(zeroed, 1)
            sp.dma_start(m.xres[0:DB, NT, :], m.x_sample.rearrange("b s d -> (b s) d")).then_inc(loaded, 16)
            sp.wait_ge(loaded, 48)


def norm_and_transpose(nc, m, layer):
    with Stage(nc) as ctx:
        sb = lambda n, s: ctx.enter_context(nc.sbuf_tensor(f"n{layer}_{n}", s, F32))
        sem = lambda n: ctx.sem(f"n{layer}_{n}")
        gain = sb("gain", [P, DM])
        squares = sb("squares", [P, 2, DM])
        normed = sb("normed", [P, 2, DM])
        sumsq = sb("sumsq", [P, TT])
        ms = sb("ms", [P, TT])
        rms = sb("rms", [P, TT])
        rinv = sb("rinv", [P, TT])
        tp = ctx.enter_context(nc.psum_tensor(f"n{layer}_tp", [P, 2, KM, P], F32))
        gain_in, sums_ready, ms_ready, rms_ready = sem("gain_in"), sem("sums"), sem("ms"), sem("rms")
        normed_ready, tp_ready, tp_used = sem("normed"), sem("tp_ready"), sem("tp_used")
        block = ctx.enter_context(nc.Block())

        @block.sync
        def _(sp):
            g = m.norm[layer].rearrange("(o d) -> o d", o=1)
            sp.dma_start(gain[:], g.to_broadcast([P, DM])).then_inc(gain_in, 16)

        @block.scalar
        def _(act):
            for t in range(TT):
                if t >= 2:
                    act.wait_ge(sums_ready, t - 1)
                nc.scalar.activation(squares[:, t % 2], m.xres[:, t], ACT.Square,
                                     accum_out=sumsq[:, t:t + 1]).then_inc(sums_ready, 1)
            act.wait_ge(ms_ready, 1)
            nc.scalar.activation(rms[:], ms[:], ACT.Sqrt).then_inc(rms_ready, 1)
            for t in range(TT):
                act.wait_ge(tp_ready, t + 1)
                n = P if t < NT else DB
                nc.scalar.copy(m.hT[:, :, t * P:t * P + n], tp[:, t % 2, :, 0:n]).then_inc(tp_used, 1)

        @block.vector
        def _(dve):
            dve.wait_ge(sums_ready, TT)
            nc.vector.tensor_scalar(ms[:], sumsq[:], 1.0 / DM, EPS, ALU.mult, ALU.add).then_inc(ms_ready, 1)
            dve.wait_ge(rms_ready, 1)
            nc.vector.reciprocal(rinv[:], rms[:])
            dve.drain()
            dve.wait_ge(gain_in, 16)
            for t in range(TT):
                if t >= 2:
                    dve.wait_ge(tp_ready, t - 1)
                nc.vector.scalar_tensor_tensor(normed[:, t % 2], m.xres[:, t], rinv[:, t:t + 1], gain[:],
                                               ALU.mult, ALU.mult).then_inc(normed_ready, 1)

        @block.tensor
        def _(pe):
            for t in range(TT):
                pe.wait_ge(normed_ready, t + 1)
                if t >= 2:
                    pe.wait_ge(tp_used, t - 1)
                for k in range(KM):
                    last = nc.tensor.transpose(tp[:, t % 2, k], normed[:, t % 2, k * P:(k + 1) * P], m.ident[:])
                last.then_inc(tp_ready, 1)


def output_projection(nc, m, layer):
    HALF, QUARTER = DM // 2, DM // 4
    with Stage(nc) as ctx:
        sem = lambda n: ctx.sem(f"o{layer}_{n}")
        w = ctx.enter_context(nc.sbuf_tensor(f"o{layer}_w", [P, 2, KI, HALF], F32))
        acc = ctx.enter_context(nc.psum_tensor(f"o{layer}_acc", [P, 4, HALF], F32))
        accs = ctx.enter_context(nc.psum_tensor(f"o{layer}_accs", [P, QUARTER], F32))
        w_in = [sem(f"w_in{i}") for i in range(4)]
        y_ready, y_added = sem("y_ready"), sem("y_added")
        block = ctx.enter_context(nc.Block())
        wv = m.w_out[layer].rearrange("(k p) n -> p k n", p=P)

        @block.sync
        def _(sp):
            for i in range(4):
                half, kk = i // 2, (i % 2) * (KI // 2)
                sp.dma_start(w[:, half, kk:kk + KI // 2, :],
                             wv[:, kk:kk + KI // 2, half * HALF:(half + 1) * HALF]).then_inc(w_in[i], 16)

        @block.tensor
        def _(pe):
            for half in range(2):
                for t in range(NT):
                    n = half * NT + t
                    if n >= 4:
                        pe.wait_ge(y_added, n - 3)
                    for k in range(KI):
                        if t == 0 and k % (KI // 2) == 0:
                            pe.wait_ge(w_in[2 * half + k // (KI // 2)], 16)
                        last = nc.tensor.matmul(acc[:, n % 4, :], m.ogT[:, k, t * P:(t + 1) * P], w[:, half, k, :],
                                                start=(k == 0), stop=(k == KI - 1))
                    last.then_inc(y_ready, 1)
            for k in range(KI):
                for j in range(4):
                    last = nc.tensor.matmul(accs[32 * j:32 * j + DB], m.ogT[:, k, SEQ:TOK],
                                            w[:, j // 2, k, j % 2 * QUARTER:(j % 2 + 1) * QUARTER],
                                            start=(k == 0), stop=(k == KI - 1))
            last.then_inc(y_ready, 1)

        @block.vector
        def _(dve):
            for half in range(2):
                for t in range(NT):
                    n = half * NT + t
                    x = m.xres[:, t, half * HALF:(half + 1) * HALF]
                    dve.wait_ge(y_ready, n + 1)
                    nc.vector.tensor_tensor(x, x, acc[:, n % 4, :], ALU.add).then_inc(y_added, 1)
            dve.wait_ge(y_ready, 2 * NT + 1)
            for j in range(4):
                x = m.xres[0:DB, NT, j * QUARTER:(j + 1) * QUARTER]
                nc.vector.tensor_tensor(x, x, accs[32 * j:32 * j + DB], ALU.add)


def store_tokens(nc, m):
    with Stage(nc) as ctx:
        stored = ctx.sem("stored")
        block = ctx.enter_context(nc.Block())

        @block.sync
        def _(sp):
            sp.dma_start(m.y_prompt.rearrange("b (t p) d -> p (b t) d", p=P), m.xres[:, 0:NT, :]).then_inc(stored, 16)
            sp.dma_start(m.y_sample.rearrange("b s d -> (b s) d"), m.xres[0:DB, NT, :]).then_inc(stored, 16)
            sp.wait_ge(stored, 32)


RW = 2 * RK + 2 * RV
RC = 2 * P + 3 + 2


def retention(nc, m, layer, state_in, state_prompt, state_sample, w_heads, head_consts):
    with Stage(nc) as ctx:
        sb = lambda n, s: ctx.enter_context(nc.sbuf_tensor(f"r{layer}_{n}", s, F32))
        ps = lambda n: ctx.enter_context(nc.psum_tensor(f"r{layer}_{n}", [P, 512], F32))
        sem = lambda n: ctx.sem(f"r{layer}_{n}")
        w = sb("w", [P, 2, KM, RW])
        hc = sb("hc", [P, 2, RC])
        rope = sb("rope", [P, TT, 2, 2 * RK])
        d8 = sb("d8", [P, DB, DB])
        e8 = sb("e8", [DB, DB, P])
        state = sb("state", [P, 2, DB, RV])
        rot = sb("rot", [P, TT, 2 * RK])
        t1 = sb("t1", [P, 2, 2 * RK])
        t2 = sb("t2", [P, 2, 2 * RK])
        z = sb("z", [P, 2, TT, 512])
        gs = sb("gs", [DB, 2, RV])
        qT = sb("qT", [P, NT, P])
        kT = sb("kT", [P, NT, P])
        qgT = sb("qgT", [P, NT, P])
        kd = sb("kd", [P, NT, RK])
        km = sb("km", [DB, DB, RK])
        qm = sb("qm", [P, DB, DB])
        qs = sb("qs", [P, DB])
        att = sb("att", [P, NT, P])
        S = sb("S", [P, NT, RV])
        stats = sb("stats", [P, TT, 6])
        mv = sb("mv", [P, TT, 2])
        var = sb("var", [P, TT])
        sd = sb("sd", [P, TT])
        rs = sb("rs", [P, TT])
        y = sb("y", [P, TT, RV])
        PB = [ps("P0"), ps("P1")]
        X = [ps(f"X{i}") for i in range(6)]
        OUTER = X[1:5]
        o_banks = [X[5], X[0]]
        w_in, hc_in = [sem("w_in0"), sem("w_in1")], [sem("hc_in0"), sem("hc_in1")]
        st_in, st_out = [sem("st_in0"), sem("st_in1")], [sem("st_out0"), sem("st_out1")]
        c_in, z_ready, z_copied = sem("c_in"), sem("z_ready"), sem("z_copied")
        qk_ready, q_copied, k_copied = sem("qk_ready"), sem("q_copied"), sem("k_copied")
        rot_ready, kd_ready, qm_ready, qg_ready = sem("rot_ready"), sem("kd_ready"), sem("qm_ready"), sem("qg_ready")
        sup_ready, S_ready, att_ready, att_masked = sem("sup_ready"), sem("S_ready"), sem("att_ready"), sem("att_masked")
        outer_ready, state_new, o_ready, os_ready = sem("outer_ready"), sem("state_new"), sem("o_ready"), sem("os_ready")
        var_ready, sd_ready, y_ready, yT_ready, og_ready = (sem("var_ready"), sem("sd_ready"), sem("y_ready"),
                                                            sem("yT_ready"), sem("og_ready"))
        S_out = sem("S_out")
        block = ctx.enter_context(nc.Block())

        SAMPLES, GATE, UNITS = NT, NT + 1, NT + 3
        bank = lambda s, i: PB[(s + i) % 2]

        def slots(eng, slot):
            slot(None, None, 0, 0)
            with eng.Fori(0, RH // 2 - 1) as pair:
                slot(2 * pair, 0, 2 * pair + 1, 1)
                slot(2 * pair + 1, 1, 2 * pair + 2, 0)
            slot(RH - 2, 0, RH - 1, 1)
            slot(RH - 1, 1, None, None)

        def heads(eng, body):
            with eng.Fori(0, RH // 2) as pair:
                for s in range(2):
                    body(pair, s, 2 * pair + s)

        @block.sync
        def _(sp):
            sp.dma_start(rope[:], m.c_rope).then_inc(c_in, 16)
            sp.dma_start(d8[:], m.c_d8).then_inc(c_in, 16)
            sp.dma_start(e8[:], m.c_e8).then_inc(c_in, 16)

            for s in range(2):
                sp.dma_start(w[:, s], w_heads[s]).then_inc(w_in[s], 16)
                sp.dma_start(hc[:, s], head_consts[s]).then_inc(hc_in[s], 16)
                sp.dma_start(state[:, s], state_in[:, s].rearrange("b k v -> k b v")).then_inc(st_in[s], 16)
            with sp.Fori(0, RH // 2 - 1) as pair:
                for s in range(2):
                    h = 2 * pair + s
                    sp.wait_ge(z_ready, (h + 1) * UNITS)
                    sp.dma_start(w[:, s], row4(w_heads[bass.ds(h + 2, 1)])).then_inc(w_in[s], 16)
                    sp.wait_ge(state_new, h + 1)
                    sp.dma_start(state_sample[:, bass.ds(h, 1)].rearrange("b a k v -> k (b a) v"),
                                 state[:, s]).then_inc(st_out[s], 16)
                    sp.wait_ge(S_ready, h + 1)
                    sp.dma_start(row(state_prompt[0, bass.ds(h, 1)]), S[:, NT - 1]).then_inc(S_out, 16)
                    sp.wait_ge(st_out[s], pair * 16 + 16)
                    sp.wait_ge(os_ready, h + 1)
                    sp.dma_start(state[:, s], state_in[:, bass.ds(h + 2, 1)].rearrange("b a k v -> k (b a) v")
                                 ).then_inc(st_in[s], 16)
                    sp.wait_ge(og_ready, h + 1)
                    sp.dma_start(hc[:, s], row(head_consts[bass.ds(h + 2, 1)])).then_inc(hc_in[s], 16)
            for s in range(2):
                h = RH - 2 + s
                sp.wait_ge(state_new, h + 1)
                sp.dma_start(state_sample[:, h].rearrange("b k v -> k b v"), state[:, s]).then_inc(st_out[s], 16)
                sp.wait_ge(S_ready, h + 1)
                sp.dma_start(state_prompt[0, h], S[:, NT - 1]).then_inc(S_out, 16)
                sp.wait_ge(st_out[s], 16 * (RH // 2))
            sp.wait_ge(S_out, 16 * RH)

        @block.tensor
        def _(pe):
            def project(q, s, i):
                if q is None:
                    return
                if i == 0:
                    pe.wait_ge(w_in[s], (q + 2 - s) * 8)
                    pe.wait_ge(z_copied, q * UNITS)
                else:
                    pe.wait_ge(z_copied, q * UNITS + i - 1)
                z_bank = bank(s, i)
                if i < SAMPLES:
                    for k in range(KM):
                        last = nc.tensor.matmul(z_bank[:], m.hT[:, k, i * P:(i + 1) * P], w[:, s, k, 0:512],
                                                start=(k == 0), stop=(k == KM - 1))
                elif i == SAMPLES:
                    for first, groups in ((0, 4), (4, 2)):
                        for k in range(KM):
                            for j in range(groups):
                                last = nc.tensor.matmul(z_bank[32 * j:32 * j + DB, first * 32:first * 32 + P],
                                                        m.hT[:, k, SEQ:TOK],
                                                        w[:, s, k, (first + j) * P:(first + j + 1) * P],
                                                        start=(k == 0), stop=(k == KM - 1))
                else:
                    at = 512 + (i - GATE) * P
                    for k in range(KM):
                        last = nc.tensor.matmul(z_bank[:], w[:, s, k, at:at + P], m.hT[:, k, 0:SEQ],
                                                start=(k == 0), stop=(k == KM - 1))
                last.then_inc(z_ready, 1)

            def turn(h, s):
                pe.wait_ge(rot_ready, h + 1)
                pe.wait_ge(og_ready, h)
                for c in range(NT):
                    nc.tensor.transpose(X[0][:, c * P:(c + 1) * P], rot[:, c, 0:RK], m.ident[:])
                    nc.tensor.transpose(X[1][:, c * P:(c + 1) * P], rot[:, c, RK:2 * RK], m.ident[:])
                nc.tensor.transpose(X[2][:, 0:DB], rot[0:DB, NT, 0:RK], m.ident[0:DB, 0:DB]).then_inc(qk_ready, 1)

            def supplements(h, s):
                pe.wait_ge(kd_ready, h + 1)
                pe.wait_ge(k_copied, h + 1)
                pe.wait_ge(qg_ready, h + 1)
                for c in range(NT):
                    last = nc.tensor.matmul(X[1 + c // 2][:, (c % 2) * RV:(c % 2 + 1) * RV], kd[:, c],
                                            z[:, s, c, 2 * RK:512], start=True, stop=True)
                last.then_inc(sup_ready, 1)

            def scores(h, s):
                pe.wait_ge(q_copied, h + 1)
                for c in range(NT):
                    last = nc.tensor.matmul(X[0][:, c * P:(c + 1) * P], kT[:, c], qT[:, c], start=True, stop=True)
                last.then_inc(att_ready, 1)

            def outer(h, s):
                pe.wait_ge(S_ready, h + 1)
                for b in range(DB):
                    last = nc.tensor.matmul(OUTER[b // 2][:, (b % 2) * RV:(b % 2 + 1) * RV], km[:, b],
                                            z[0:DB, s, NT, 2 * RK:512], start=True, stop=True)
                last.then_inc(outer_ready, 1)

            def outputs(h, s):
                pe.wait_ge(att_masked, h + 1)
                for c in range(NT):
                    o = o_banks[c // 2][:, (c % 2) * RV:(c % 2 + 1) * RV]
                    last = nc.tensor.matmul(o, att[:, c], z[:, s, c, 2 * RK:512], start=True, stop=(c == 0))
                    if c > 0:
                        last = nc.tensor.matmul(o, qgT[:, c], S[:, c - 1], start=False, stop=True)
                last.then_inc(o_ready, 1)

            def sample_outputs(h, s):
                pe.wait_ge(state_new, h + 1)
                pe.wait_ge(qm_ready, h + 1)
                for b in range(DB):
                    last = nc.tensor.matmul(X[1][0:DB, 0:RV], qm[:, b], state[:, s, b], start=(b == 0), stop=(b == DB - 1))
                last.then_inc(os_ready, 1)

            def turn_outputs(h, s):
                pe.wait_ge(y_ready, h + 1)
                for f in range(2):
                    for c in range(NT):
                        nc.tensor.transpose(X[3 + f][:, c * P:(c + 1) * P], y[:, c, f * P:(f + 1) * P], m.ident[:])
                    last = nc.tensor.transpose(X[2][:, f * DB:(f + 1) * DB], y[0:DB, NT, f * P:(f + 1) * P],
                                               m.ident[0:DB, 0:DB])
                last.then_inc(yT_ready, 1)

            def slot(h, s, q, r):
                def mix(*steps):
                    if h is not None:
                        for step in steps:
                            step(h, s)

                mix(turn)
                project(q, r, 0)
                mix(supplements, scores)
                project(q, r, 1)
                mix(outer)
                project(q, r, 2)
                mix(outputs, sample_outputs)
                project(q, r, 3)
                project(q, r, SAMPLES)
                mix(turn_outputs)
                project(q, r, GATE)
                project(q, r, GATE + 1)

            slots(pe, slot)

        @block.scalar
        def _(act):
            def projected(q, s, i):
                if q is None:
                    return
                act.wait_ge(z_ready, q * UNITS + i + 1)
                z_bank = bank(s, i)
                if i < SAMPLES:
                    nc.scalar.copy(z[:, s, i], z_bank[:]).then_inc(z_copied, 1)
                elif i == SAMPLES:
                    for j in range(4):
                        nc.scalar.copy(z[0:DB, s, NT, j * P:(j + 1) * P], z_bank[32 * j:32 * j + DB, 0:P])
                    for f in range(2):
                        last = nc.scalar.activation(gs[:, s, f * P:(f + 1) * P], z_bank[32 * f:32 * f + DB, P:2 * P], ACT.Silu)
                    last.then_inc(z_copied, 1)
                else:
                    nc.scalar.activation(m.ogT[:, bass.ds(2 * q + i - GATE, 1), 0:SEQ].rearrange("p a n -> p (a n)"),
                                         z_bank[:], ACT.Silu).then_inc(z_copied, 1)

            def turned(h, s):
                act.wait_ge(qk_ready, h + 1)
                nc.scalar.copy(kT[:].rearrange("p c n -> p (c n)"), X[1][:]).then_inc(k_copied, 1)
                nc.scalar.copy(qT[:].rearrange("p c n -> p (c n)"), X[0][:]).then_inc(q_copied, 1)

            def root(h, s):
                act.wait_ge(var_ready, h + 1)
                nc.scalar.activation(sd[:], var[:], ACT.Sqrt).then_inc(sd_ready, 1)

            def slot(h, s, q, r):
                if h is not None:
                    turned(h, s)
                for i in range(3):
                    projected(q, r, i)
                if h is not None:
                    root(h, s)
                for i in range(3, UNITS):
                    projected(q, r, i)

            slots(act, slot)

        @block.vector
        def _(dve):
            dve.wait_ge(c_in, 48)
            nc.vector.memset(mv[:], 0.0)
            nc.vector.memset(rot[:], 0.0)
            dve.drain()

            def head(pair, s, h):
                for t in range(TT):
                    n = P if t < NT else DB
                    dve.wait_ge(z_copied, h * UNITS + t + 1)
                    zh = z[0:n, s, t, 0:2 * RK].rearrange("p (a b n) -> p a b n", a=2, b=2)
                    u = t2[0:n, t % 2].rearrange("p (a b n) -> p a b n", a=2, b=2)
                    sn = rope[0:n, t, 1].rearrange("p (a b n) -> p a b n", a=2, b=2)
                    nc.vector.tensor_tensor(t1[0:n, t % 2], z[0:n, s, t, 0:2 * RK], rope[0:n, t, 0], ALU.mult)
                    nc.vector.tensor_tensor(u[:, :, 0], zh[:, :, 1], sn[:, :, 0], ALU.mult)
                    nc.vector.tensor_tensor(u[:, :, 1], zh[:, :, 0], sn[:, :, 1], ALU.mult)
                    dve.drain()
                    last = nc.vector.tensor_tensor(rot[0:n, t], t1[0:n, t % 2], t2[0:n, t % 2], ALU.add)
                last.then_inc(rot_ready, 1)
                dve.drain()
                dve.wait_ge(hc_in[s], pair * 16 + 16)
                last = nc.vector.tensor_scalar(kd[:], rot[:, 0:NT, RK:2 * RK], hc[:, s, 2 * P:2 * P + 1], None, ALU.mult)
                nc.vector.tensor_tensor(km[:], rot[0:DB, NT:TT, RK:2 * RK].to_broadcast([DB, DB, RK]), e8[:],
                                        ALU.mult).then_inc(kd_ready, 1)
                dve.wait_ge(q_copied, h + 1)
                nc.vector.tensor_tensor(qgT[:], qT[:],
                                        hc[:, s:s + 1, P:2 * P].to_broadcast([P, NT, P]), ALU.mult)
                nc.vector.tensor_copy(qs[:], X[2][:, 0:DB]).then_inc(qg_ready, 1)
                dve.drain()
                nc.vector.tensor_tensor(qm[:], qs[:].rearrange("p (a b) -> p a b", a=1).to_broadcast([P, DB, DB]), d8[:],
                                        ALU.mult).then_inc(qm_ready, 1)
                dve.wait_ge(sup_ready, h + 1)
                dve.wait_ge(S_out, h * 16)
                nc.vector.tensor_copy(S[:, 0], X[1][:, 0:RV])
                for c in range(1, NT):
                    dve.drain()
                    last = nc.vector.scalar_tensor_tensor(S[:, c], S[:, c - 1], hc[:, s, 2 * P + 1:2 * P + 2],
                                                          X[1 + c // 2][:, (c % 2) * RV:(c % 2 + 1) * RV],
                                                          ALU.mult, ALU.add)
                last.then_inc(S_ready, 1)
                dve.wait_ge(att_ready, h + 1)
                nc.vector.tensor_tensor(att[:], X[0][:].rearrange("p (c n) -> p c n", c=NT),
                                        hc[:, s:s + 1, 0:P].to_broadcast([P, NT, P]), ALU.mult).then_inc(att_masked, 1)
                dve.wait_ge(outer_ready, h + 1)
                dve.wait_ge(st_in[s], pair * 16 + 16)
                for q in range(4):
                    st = state[:, s, 2 * q:2 * q + 2].rearrange("p b v -> p (b v)")
                    last = nc.vector.scalar_tensor_tensor(st, st, hc[:, s, 2 * P + 2:2 * P + 3], OUTER[q][:],
                                                          ALU.mult, ALU.add)
                last.then_inc(state_new, 1)
                o = [o_banks[c // 2][:, (c % 2) * RV:(c % 2 + 1) * RV] for c in range(NT)] + [X[1][0:DB, 0:RV]]
                dve.wait_ge(o_ready, h + 1)
                dve.wait_ge(os_ready, h + 1)
                for t in range(TT):
                    n = P if t < NT else DB
                    nc.vector.bn_stats(stats[0:n, t], o[t])
                dve.drain()
                for t in range(TT):
                    n = P if t < NT else DB
                    nc.vector.bn_aggr(mv[0:n, t], stats[0:n, t])
                dve.drain()
                nc.vector.tensor_scalar(var[:], mv[:, :, 1], EPS, None, ALU.add).then_inc(var_ready, 1)
                dve.wait_ge(sd_ready, h + 1)
                nc.vector.reciprocal(rs[:], sd[:])
                dve.drain()
                for t in range(TT):
                    n = P if t < NT else DB
                    nc.vector.tensor_scalar(y[0:n, t], o[t], mv[0:n, t, 0:1], rs[0:n, t:t + 1],
                                            ALU.subtract, ALU.mult)
                dve.drain()
                nc.vector.tensor_tensor(y[0:DB, NT], y[0:DB, NT], gs[:, s], ALU.mult).then_inc(y_ready, 1)
                dve.wait_ge(yT_ready, h + 1)
                dve.wait_ge(z_copied, (h + 1) * UNITS)
                for f in range(2):
                    g = hc[:, s, 2 * P + 3 + f:2 * P + 4 + f]
                    og = m.ogT[:, bass.ds(2 * h + f, 1), 0:SEQ].rearrange("p a n -> p (a n)")
                    nc.vector.scalar_tensor_tensor(og, X[3 + f][:], g, og, ALU.mult, ALU.mult)
                    last = nc.vector.tensor_scalar(m.ogT[:, bass.ds(2 * h + f, 1), SEQ:TOK].rearrange("p a n -> p (a n)"),
                                                   X[2][:, f * DB:(f + 1) * DB], g, None, ALU.mult)
                last.then_inc(og_ready, 1)

            heads(dve, head)


def row4(ap):
    return ap.rearrange("a p k n -> p (a k) n")


QP = NH // HPG
KVP = 6
GP = DI // 512
NP = QP + KVP + GP
NCP = (SEQ - CL) // CS + 1
PAST = 1024
NCS = (PAST + 1 - CL) // CS + 1
LOW = 1e25


def nsa_project(nc, m, a):
    with Stage(nc) as ctx:
        sb = lambda n, s: ctx.enter_context(nc.sbuf_tensor(f"np_{n}", s, F32))
        ps = lambda n, s: ctx.enter_context(nc.psum_tensor(f"np_{n}", s, F32))
        sem = lambda n: ctx.sem(f"np_{n}")
        w = sb("w", [P, 2, KM, 512])
        wb = sb("wb", [P, KM, 3 * NH])
        stage = sb("stage", [P, TT, 512])
        nrm = sb("nrm", [P, 2, 512])
        gs = sb("gs", [DB, 4, P])
        ss, ms, sd, rs = sb("ss", [P, 4]), sb("ms", [P, 4]), sb("sd", [P, 4]), sb("rs", [P, 4])
        Z = ps("Z", [P, 2, 512])
        TP = ps("TP", [P, 2, 512])
        B = ps("B", [P, 512])
        sq = ps("sq", [P, 512])
        G = ps("G", [P, 2, 512])
        w_in = [sem("w_in0"), sem("w_in1")]
        c_in, z_ready, z_copied, nrm_ready = sem("c_in"), sem("z_ready"), sem("z_copied"), sem("nrm_ready")
        tp_ready, tp_copied, sq_ready, ms_ready, sd_ready = (sem("tp_ready"), sem("tp_copied"), sem("sq_ready"),
                                                             sem("ms_ready"), sem("sd_ready"))
        gate_ready, gate_used, b_ready, b_used = (sem("gate_ready"), sem("gate_used"),
                                                              sem("b_ready"), sem("b_used"))
        sq_used = sem("sq_used")
        gs_ready, gs_copied, gst_ready, gs_used = sem("gs_ready"), sem("gs_copied"), sem("gst_ready"), sem("gs_used")
        stored, shifted = sem("stored"), sem("shifted")
        block = ctx.enter_context(nc.Block())

        ROWS = [(m.cmp_prompt, m.cmp_sample), (m.slc_prompt, m.slc_sample), (m.win_prompt, None)]
        KINDS = ["raw", "raw", "key", "value", "key", "value"]
        KT = [a.XT[:, 0:KVH], a.XT[:, KVH:2 * KVH], a.skT[:], None, a.wkT[:], None]
        GAIN = [None, None, 2, None, 3, None]
        TILE = [stage, stage, stage, a.sv, stage, a.wv]
        NB = [QP * TT + n for n in (0, 0, 0, TT, TT, 2 * TT)]
        UB = [QP * TT + n for n in (0, NT, 2 * NT, 2 * NT + TT, 2 * NT + TT, 2 * NT + 2 * TT)]

        @block.sync
        def _(sp):
            sp.dma_start(a.gain[:], m.c_gain).then_inc(c_in, 16)
            sp.dma_start(wb[:], m.w1_bgate).then_inc(c_in, 16)
            for s in range(2):
                sp.dma_start(w[:, s], m.w_in[1][s]).then_inc(w_in[s], 16)
            sp.dma_start(m.win_sample[:, 0:511], m.state_l1_win[:, 1:512]).then_inc(shifted, 16)
            with sp.Fori(1, (NP - 2) // 2) as pair:
                for s in range(2):
                    sp.wait_ge(z_ready, (2 * pair + s - 1) * TT)
                    sp.dma_start(w[:, s], row4(m.w_in[1][bass.ds(2 * pair + s, 1)])).then_inc(w_in[s], 16)
            for s in range(2):
                sp.wait_ge(gate_ready, 4 * (s + 1))
                sp.dma_start(w[:, s], m.w_in[1][NP - 2 + s]).then_inc(w_in[s], 16)
            sp.wait_ge(shifted, 16)

        @block.gpsimd
        def _(pool):
            for j in range(KVP):
                pool.wait_ge(z_copied, (QP + j + 1) * TT)
                prompt, sample = ROWS[j // 2]
                pool.dma_start(prompt[0, :, j % 2].rearrange("(t p) g d -> p t (g d)", p=P), TILE[j][:, 0:NT]
                               ).then_inc(stored, 16)
                dst = sample[:, 0, j % 2] if sample is not None else m.win_sample[:, 511, j % 2]
                pool.dma_start(dst.rearrange("b g d -> b (g d)"), TILE[j][0:DB, NT]).then_inc(stored, 16)
            pool.wait_ge(stored, 32 * KVP)

        @block.tensor
        def _(pe):
            def project_samples(out, s, k):
                for j in range(4):
                    last = nc.tensor.matmul(out[32 * j:32 * j + DB], m.hT[:, k, SEQ:TOK],
                                            w[:, s, k, j * P:(j + 1) * P], start=(k == 0), stop=(k == KM - 1))
                return last

            def project(n, s, t):
                if t > 0:
                    pe.wait_ge(z_copied, n - 1)
                else:
                    pe.wait_ge(z_copied, n)
                for k in range(KM):
                    if t < NT:
                        last = nc.tensor.matmul(Z[:, t % 2], m.hT[:, k, t * P:(t + 1) * P], w[:, s, k],
                                                start=(k == 0), stop=(k == KM - 1))
                    else:
                        last = project_samples(Z[:, t % 2, 0:P], s, k)
                last.then_inc(z_ready, 1)

            def turn(src, t, u):
                pe.wait_ge(tp_copied, u - 1 if t > 0 else u)
                for r in range(4):
                    last = nc.tensor.transpose(TP[:, t % 2, r * P:(r + 1) * P], src[:, r * P:(r + 1) * P], m.ident[:])
                last.then_inc(tp_ready, 1)

            with pe.Fori(0, QP // 2) as pair:
                for s in range(2):
                    piece = 2 * pair + s
                    pe.wait_ge(w_in[s], pair * 16 + 16)
                    for t in range(TT + 1):
                        if t < TT:
                            project(piece * TT + t, s, t)
                        if t > 0:
                            pe.wait_ge(nrm_ready, piece * TT + t)
                            turn(nrm[:, (t - 1) % 2], t - 1, piece * TT + t - 1)
            for j in range(KVP):
                piece, s = QP + j, (QP + j) % 2
                pe.wait_ge(w_in[s], 16 * (piece // 2 + 1))
                for t in range(TT + 1):
                    if t < TT:
                        project(piece * TT + t, s, t)
                    if t > 0 and KINDS[j] == "key":
                        pe.wait_ge(nrm_ready, NB[j] + t)
                        turn(nrm[:, (t - 1) % 2], t - 1, UB[j] + t - 1)
                    if 0 < t <= NT and KINDS[j] == "raw":
                        pe.wait_ge(z_copied, piece * TT + t)
                        turn(stage[:, t - 1], t - 1, UB[j] + t - 1)
            with pe.Fori(0, GP // 2) as pair:
                for s in range(2):
                    piece = QP + KVP + 2 * pair + s
                    pe.wait_ge(w_in[s], ((QP + KVP) // 2 + pair) * 16 + 16)
                    pe.wait_ge(gs_used, 2 * pair + s)
                    for k in range(KM):
                        last = project_samples(B[:, 0:P], s, k)
                    last.then_inc(gs_ready, 1)
                    for f in range(4):
                        n = (2 * pair + s) * 4 + f
                        pe.wait_ge(gate_used, n - 1 if s + f > 0 else n)
                        if f == 2:
                            pe.wait_ge(gs_copied, 2 * pair + s + 1)
                        for k in range(KM):
                            last = nc.tensor.matmul(G[:, f % 2], w[:, s, k, f * P:(f + 1) * P], m.hT[:, k, 0:SEQ],
                                                    start=(k == 0), stop=(k == KM - 1))
                        last.then_inc(gate_ready, 1)
                        if f == 2:
                            for j in range(4):
                                last = nc.tensor.transpose(B[:, P + j * DB:P + (j + 1) * DB], gs[:, j], m.ident[0:DB, 0:DB])
                            last.then_inc(gst_ready, 1)
            pe.wait_ge(c_in, 32)
            pe.wait_ge(gs_used, GP)
            for t in range(TT):
                mt = P if t < NT else DB
                pe.wait_ge(b_used, t)
                for k in range(KM):
                    last = nc.tensor.matmul(B[0:mt, 0:3 * NH], m.hT[:, k, t * P:t * P + mt], wb[:, k],
                                            start=(k == 0), stop=(k == KM - 1))
                last.then_inc(b_ready, 1)

        @block.scalar
        def _(act):
            def leave(dst, t):
                if t < NT:
                    return nc.scalar.copy(dst[:, t], Z[:, t % 2])
                for j in range(4):
                    last = nc.scalar.copy(dst[0:DB, t, j * P:(j + 1) * P], Z[32 * j:32 * j + DB, t % 2, 0:P])
                return last

            def norm(n, t):
                mt = P if t < NT else DB
                act.drain()
                act.wait_ge(sq_used, n)
                nc.scalar.activation(sq[0:mt], stage[0:mt, t], ACT.Square).then_inc(sq_ready, 1)
                act.wait_ge(ms_ready, n + 1)
                nc.scalar.activation(sd[0:mt], ms[0:mt], ACT.Sqrt).then_inc(sd_ready, 1)

            def out(u, t, dst, gain):
                mt = P if t < NT else DB
                act.wait_ge(tp_ready, u + 1)
                src = TP[:, t % 2].rearrange("p (r n) -> p r n", r=4)[:, :, 0:mt]
                at = dst[:, :, t * P:t * P + mt]
                if gain is None:
                    nc.scalar.copy(at, src).then_inc(tp_copied, 1)
                else:
                    nc.scalar.activation(at, src, ACT.Copy, scale=a.gain[:, gain:gain + 1]).then_inc(tp_copied, 1)

            act.wait_ge(c_in, 32)
            with act.Fori(0, QP) as piece:
                for t in range(TT):
                    act.wait_ge(z_ready, piece * TT + t + 1)
                    act.wait_ge(nrm_ready, piece * TT)
                    leave(stage, t).then_inc(z_copied, 1)
                    norm(piece * TT + t, t)
                    if t > 0:
                        out(piece * TT + t - 1, t - 1, a.qT[:, bass.ds(piece * HPG, HPG)], 0)
                out(piece * TT + TT - 1, TT - 1, a.qT[:, bass.ds(piece * HPG, HPG)], 0)
            for j in range(KVP):
                kind = KINDS[j]
                tiles = NT if kind == "raw" else TT
                act.wait_ge(nrm_ready, NB[j])
                act.wait_ge(stored, 32 * j)
                for t in range(TT + 1):
                    if t < TT:
                        act.wait_ge(z_ready, (QP + j) * TT + t + 1)
                        leave(TILE[j], t).then_inc(z_copied, 1)
                        if kind == "key":
                            norm(NB[j] + t, t)
                    if kind != "value" and 0 < t <= tiles:
                        out(UB[j] + t - 1, t - 1, KT[j], GAIN[j])
            with act.Fori(0, GP) as piece:
                act.wait_ge(gs_ready, piece + 1)
                for j in range(4):
                    last = nc.scalar.copy(gs[:, j], B[32 * j:32 * j + DB, 0:P])
                last.then_inc(gs_copied, 1)
                for f in range(4):
                    act.wait_ge(gate_ready, 4 * piece + f + 1)
                    nc.scalar.activation(m.ogT[:, bass.ds(4 * piece + f, 1), 0:SEQ].rearrange("p a n -> p (a n)"),
                                         G[:, f % 2], ACT.Silu).then_inc(gate_used, 1)
                act.wait_ge(gst_ready, piece + 1)
                nc.scalar.activation(m.ogT[:, bass.ds(4 * piece, 4), SEQ:TOK],
                                     B[:, P:P + 4 * DB].rearrange("p (j b) -> p j b", j=4), ACT.Silu).then_inc(gs_used, 1)
            for t in range(TT):
                mt = P if t < NT else DB
                act.wait_ge(b_ready, t + 1)
                nc.scalar.activation(a.bg[0:mt, t], B[0:mt, 0:3 * NH], ACT.Sigmoid).then_inc(b_used, 1)

        @block.vector
        def _(dve):
            def norm(u, t, scale):
                mt = P if t < NT else DB
                dve.wait_ge(sq_ready, u + 1)
                nc.vector.tensor_reduce(ss[0:mt], sq[0:mt].rearrange("p (r n) -> p r n", r=4), axis=AX,
                                        op=ALU.add).then_inc(sq_used, 1)
                dve.drain()
                nc.vector.tensor_scalar(ms[0:mt], ss[0:mt], 1.0 / HD, EPS, ALU.mult, ALU.add).then_inc(ms_ready, 1)
                dve.wait_ge(sd_ready, u + 1)
                nc.vector.reciprocal(rs[0:mt], sd[0:mt])
                dve.drain()
                if scale is not None:
                    nc.vector.tensor_scalar(rs[0:mt], rs[0:mt], scale, None, ALU.mult)
                    dve.drain()
                nc.vector.tensor_tensor(nrm[0:mt, t % 2].rearrange("p (r n) -> p r n", r=4),
                                        stage[0:mt, t].rearrange("p (r n) -> p r n", r=4),
                                        rs[0:mt].rearrange("p (r o) -> p r o", o=1).to_broadcast([mt, 4, P]),
                                        ALU.mult).then_inc(nrm_ready, 1)

            with dve.Fori(0, QP) as piece:
                for t in range(TT):
                    u = piece * TT + t
                    dve.wait_ge(tp_ready, u - 1 if t > 0 else u)
                    norm(u, t, HD ** -0.5)
            for j in range(KVP):
                if KINDS[j] == "key":
                    for t in range(TT):
                        dve.wait_ge(tp_ready, UB[j] + (t - 1 if t > 0 else 0))
                        norm(NB[j] + t, t, None)


def nsa_compress(nc, m, a):
    G4, N = KVH, NCP
    with Stage(nc) as ctx:
        sb = lambda n, s: ctx.enter_context(nc.sbuf_tensor(f"nc_{n}", s, F32))
        ps = lambda n, s: ctx.enter_context(nc.psum_tensor(f"nc_{n}", s, F32))
        sem = lambda n: ctx.sem(f"nc_{n}")
        pcs = sb("pcs", [P, 2, G4, N])
        ck = sb("ck", [N, G4, P])
        sq = sb("sq", [N, G4, P])
        ckn = sb("ckn", [N, G4, P])
        ss, ms, sd, rs = sb("ss", [N, 4]), sb("ms", [N, 4]), sb("sd", [N, 4]), sb("rs", [N, 4])
        BI = ps("BI", [P, 512])
        PRE = ps("PRE", [P, 512])
        CK = ps("CK", [P, 512])
        CV = ps("CV", [P, 512])
        TC = ps("TC", [P, 512])
        w_in, bias_ready, bias_copied, pre_ready, pcs_ready = (sem("w_in"), sem("bias_ready"), sem("bias_copied"),
                                                               sem("pre_ready"), sem("pcs_ready"))
        ck_ready, ck_copied, sq_ready, ms_ready, sd_ready = (sem("ck_ready"), sem("ck_copied"), sem("sq_ready"),
                                                             sem("ms_ready"), sem("sd_ready"))
        ckn_ready, tc_ready, done, cv_cleared = sem("ckn_ready"), sem("tc_ready"), sem("done"), sem("cv_cleared")
        block = ctx.enter_context(nc.Block())

        @block.sync
        def _(sp):
            sp.dma_start(a.w1[:], m.cmp_w1.rearrange("c l d h -> d (c l) h")).then_inc(w_in, 16)
            sp.dma_start(a.w2[:], m.cmp_w2.rearrange("c h d -> h c d")).then_inc(w_in, 16)
            sp.dma_start(a.peT[:], m.c_peT).then_inc(w_in, 16)

        @block.tensor
        def _(pe):
            pe.wait_ge(w_in, 48)
            for c in range(2):
                for l in range(CL):
                    last = nc.tensor.matmul(BI[:, c:c + 1], a.w1[:, c * CL + l], a.peT[:, c * CL + l:c * CL + l + 1],
                                            start=(l == 0), stop=(l == CL - 1))
            last.then_inc(bias_ready, 1)
            for c in range(2):
                for l in range(CL):
                    last = nc.tensor.matmul(PRE[:, c * G4 * N:(c + 1) * G4 * N], a.w1[:, c * CL + l],
                                            a.XT[:, c * G4:(c + 1) * G4, l:l + CS * (N - 1) + 1:CS],
                                            start=(l == 0), stop=(l == CL - 1))
            last.then_inc(pre_ready, 1)
            pe.wait_ge(pcs_ready, 1)
            for c, bank in ((0, CK), (1, CV)):
                for g in range(G4):
                    last = nc.tensor.matmul(bank[0:N, g * P:(g + 1) * P], pcs[:, c, g], a.w2[:, c], start=True, stop=True)
            last.then_inc(ck_ready, 1)
            pe.wait_ge(ckn_ready, 1)
            for g in range(G4):
                last = nc.tensor.transpose(TC[:, g * N:(g + 1) * N], ckn[:, g], m.ident[0:N, 0:N])
            last.then_inc(tc_ready, 1)

        @block.scalar
        def _(act):
            act.wait_ge(bias_ready, 1)
            nc.scalar.copy(a.bias[:], BI[:, 0:2])
            act.wait_ge(pre_ready, 1)
            act.drain()
            for c in range(2):
                last = nc.scalar.activation(pcs[:, c].rearrange("p g n -> p (g n)"), PRE[:, c * G4 * N:(c + 1) * G4 * N],
                                            ACT.Silu, bias=a.bias[:, c:c + 1])
            last.then_inc(pcs_ready, 1)
            act.wait_ge(ck_ready, 1)
            nc.scalar.copy(ck[:].rearrange("n g d -> n (g d)"), CK[0:N, :])
            act.wait_ge(cv_cleared, 1)
            nc.scalar.copy(a.cv[0:N], CV[0:N, :])
            act.drain()
            nc.scalar.activation(sq[:], ck[:], ACT.Square).then_inc(sq_ready, 1)
            act.wait_ge(ms_ready, 1)
            nc.scalar.activation(sd[:], ms[:], ACT.Sqrt).then_inc(sd_ready, 1)
            act.wait_ge(tc_ready, 1)
            nc.scalar.activation(a.ckT[:].rearrange("p g n -> p (g n)"), TC[:, 0:G4 * N], ACT.Copy,
                                 scale=a.gain[:, 1:2]).then_inc(done, 1)

        @block.vector
        def _(dve):
            nc.vector.memset(a.cv[:], 0.0).then_inc(cv_cleared, 1)
            dve.wait_ge(sq_ready, 1)
            nc.vector.tensor_reduce(ss[:], sq[:], axis=AX, op=ALU.add)
            dve.drain()
            nc.vector.tensor_scalar(ms[:], ss[:], 1.0 / HD, EPS, ALU.mult, ALU.add).then_inc(ms_ready, 1)
            dve.wait_ge(sd_ready, 1)
            nc.vector.reciprocal(rs[:], sd[:])
            dve.drain()
            nc.vector.tensor_tensor(ckn[:], ck[:], rs[:].rearrange("n (g o) -> n g o", o=1).to_broadcast([N, G4, P]),
                                    ALU.mult).then_inc(ckn_ready, 1)


def nsa_prompt(nc, m, a):
    R = HPG
    H2 = 2
    BR = 3
    with Stage(nc) as ctx:
        sb = lambda n, s: ctx.enter_context(nc.sbuf_tensor(f"na_{n}", s, F32))
        ps = lambda n, s: ctx.enter_context(nc.psum_tensor(f"na_{n}", s, F32))
        sem = lambda n: ctx.sem(f"na_{n}")
        causal = sb("causal", [P, P])
        cmask = sb("cmask", [P, NT, NCP])
        qg = sb("qg", [P, R, SEQ])
        prob = sb("prob", [P, 2, H2, SEQ])
        pT = a.XT[:, 0:2 * H2].rearrange("p (s r) n -> p s r n", s=2)
        mx, nmx, den, rden, coef = (sb(n, [P, H2]) for n in ("mx", "nmx", "den", "rden", "coef"))
        o_sb = sb("o_sb", [P, R, P])
        S = ps("S", [P, 2, H2, 512])
        PT = ps("PT", [P, H2, 512])
        O = ps("O", [P, R, P])
        OT = ps("OT", [P, R, P])
        c_in, qg_ready, s_ready, max_ready, exp_ready, p_ready = (sem("c_in"), sem("qg_ready"), sem("s_ready"),
                                                                  sem("max_ready"), sem("exp_ready"), sem("p_ready"))
        pt_ready, pt_copied, pv_done, o_copied, ot_ready, ot_used = (
            sem("pt_ready"), sem("pt_copied"), sem("pv_done"), sem("o_copied"), sem("ot_ready"), sem("ot_used"))
        block = ctx.enter_context(nc.Block())

        STEPS = [(it, br, pr) for it in range(NT) for br in range(BR) for pr in range(R // H2)]
        NS, UNIT = len(STEPS), BR * R // H2
        width = lambda it, br: (it + 1) * P if br < 2 else NCP
        ends = lambda k: k >= 0 and (k + 1) % UNIT == 0

        @block.gpsimd
        def _(pool):
            nc.gpsimd.tensor_copy(a.qs[:], a.qT[:, :, SEQ:TOK])
            nc.gpsimd.tensor_copy(a.ks[:, 0], a.skT[:, :, SEQ:TOK])
            nc.gpsimd.tensor_copy(a.ks[:, 1], a.wkT[:, :, SEQ:TOK])

        @block.sync
        def _(sp):
            sp.dma_start(causal[:], m.c_causal).then_inc(c_in, 16)
            sp.dma_start(cmask[:], m.c_cmask).then_inc(c_in, 16)

        @block.tensor
        def _(pe):
            def scores(g, k):
                it, br, pr = STEPS[k]
                n, keys = width(it, br), [a.skT, a.wkT, a.ckT][br]
                pe.wait_ge(exp_ready, g * NS + (k - 1 if k > 0 else 0))
                for r in range(H2):
                    last = nc.tensor.matmul(S[:, k % 2, r, 0:n], qg[:, pr * H2 + r, it * P:(it + 1) * P],
                                            keys[:, bass.ds(g, 1), 0:n].rearrange("p a n -> p (a n)"),
                                            start=True, stop=True)
                last.then_inc(s_ready, 1)

            def turn(g, k):
                it, br, pr = STEPS[k]
                pe.wait_ge(p_ready, g * NS + k + 1)
                for r in range(H2):
                    pe.wait_ge(pt_copied, (g * NS + k) * H2 + (r - 1 if k > 0 else 0))
                    if br < 2:
                        for j in range(it + 1):
                            last = nc.tensor.transpose(PT[:, r, j * P:(j + 1) * P],
                                                       prob[:, k % 2, r, j * P:(j + 1) * P], m.ident[:])
                    else:
                        last = nc.tensor.transpose(PT[0:NCP, r, 0:P], prob[:, k % 2, r, 0:NCP], m.ident[:])
                    last.then_inc(pt_ready, 1)

            def values(g, k):
                it, br, pr = STEPS[k]
                cols = bass.ds(g * HD, HD)
                if ends(k - 1) or k == 0:
                    pe.wait_ge(o_copied, g * NT + it)
                for r in range(H2):
                    pe.wait_ge(pt_copied, (g * NS + k) * H2 + r + 1)
                    o = O[:, pr * H2 + r]
                    if br < 2:
                        v = [a.sv, a.wv][br]
                        for j in range(it + 1):
                            last = nc.tensor.matmul(o, pT[:, k % 2, r, j * P:(j + 1) * P], v[:, j, cols],
                                                    start=(br == 0 and pr == 0 and r == 0 and j == 0), stop=False,
                                                    skip_group_check=True)
                    else:
                        last = nc.tensor.matmul(o, pT[:, k % 2, r, 0:P], a.cv[:, cols], start=False,
                                                stop=(ends(k) and r == H2 - 1), skip_group_check=True)
                    last.then_inc(pv_done, 1)

            def outputs(g, it):
                pe.wait_ge(o_copied, g * NT + it + 1)
                pe.wait_ge(ot_used, g * NT + it)
                for r in range(R):
                    last = nc.tensor.transpose(OT[:, r], o_sb[:, r], m.ident[:])
                last.then_inc(ot_ready, 1)

            with pe.Fori(0, KVH) as g:
                pe.wait_ge(qg_ready, g + 1)
                scores(g, 0)
                for k in range(NS):
                    if k + 1 < NS:
                        scores(g, k + 1)
                    if ends(k - 2):
                        outputs(g, STEPS[k - 2][0])
                    if k > 0:
                        values(g, k - 1)
                    turn(g, k)
                values(g, NS - 1)
                outputs(g, NT - 1)

        @block.scalar
        def _(act):
            def exponentials(g, k):
                it, br, pr = STEPS[k]
                n = width(it, br)
                act.wait_ge(max_ready, g * NS + k + 1)
                act.wait_ge(pt_ready, (g * NS + (k - 1 if k > 0 else 0)) * H2)
                for r in range(H2):
                    last = nc.scalar.activation(prob[:, k % 2, r, 0:n], S[:, k % 2, r, 0:n], ACT.Exp,
                                                bias=nmx[:, r:r + 1], accum_out=den[:, r:r + 1])
                last.then_inc(exp_ready, 1)

            def turned(g, k):
                it, br, pr = STEPS[k]
                for r in range(H2):
                    act.wait_ge(pt_ready, (g * NS + k) * H2 + r + 1)
                    act.wait_ge(pv_done, (g * NS + k - 2) * H2 + r + 1 if k > 1 else g * NS * H2)
                    if br < 2:
                        n = width(it, br)
                        nc.scalar.copy(pT[:, k % 2, r, 0:n], PT[:, r, 0:n]).then_inc(pt_copied, 1)
                    else:
                        nc.scalar.copy(pT[0:NCP, k % 2, r, 0:P], PT[0:NCP, r, 0:P]).then_inc(pt_copied, 1)

            def outputs(g, it):
                act.wait_ge(pv_done, (g * NS + (it + 1) * UNIT) * H2)
                act.wait_ge(ot_ready, g * NT + it)
                nc.scalar.copy(o_sb[:], O[:]).then_inc(o_copied, 1)

            with act.Fori(0, KVH) as g:
                act.wait_ge(s_ready, g * NS)
                nc.scalar.copy(qg[:], a.qT[:, bass.ds(g * R, R), 0:SEQ]).then_inc(qg_ready, 1)
                exponentials(g, 0)
                for k in range(NS):
                    if k + 1 < NS:
                        exponentials(g, k + 1)
                    if ends(k - 1):
                        outputs(g, STEPS[k - 1][0])
                    turned(g, k)
                outputs(g, NT - 1)

        @block.vector
        def _(dve):
            def maximum(g, k):
                it, br, pr = STEPS[k]
                n = width(it, br)
                lo = n - P if br < 2 else 0
                mask = causal[:] if br < 2 else cmask[:, it]
                s = S[:, k % 2]
                dve.wait_ge(s_ready, g * NS + k + 1)
                nc.vector.tensor_tensor(s[:, :, lo:n], s[:, :, lo:n], mask.rearrange("p (o n) -> p o n", o=1)
                                        .to_broadcast([P, H2, n - lo]), ALU.add)
                dve.drain()
                nc.vector.tensor_reduce(mx[:], s[:, :, 0:n], axis=AX, op=ALU.max)
                dve.drain()
                nc.vector.tensor_scalar(nmx[:], mx[:], -1.0, LOW, ALU.mult, ALU.min).then_inc(max_ready, 1)

            def probabilities(g, k):
                it, br, pr = STEPS[k]
                n, gate = width(it, br), (1, 2, 0)[br]
                dve.wait_ge(exp_ready, g * NS + k + 1)
                nc.vector.tensor_scalar(rden[:], den[:], 1e-30, None, ALU.max)
                dve.drain()
                nc.vector.reciprocal(rden[:], rden[:])
                dve.drain()
                nc.vector.tensor_tensor(coef[:], rden[:], a.bg[:, it, bass.ds(g * R + gate * NH + pr * H2, H2)], ALU.mult)
                dve.drain()
                p = prob[:, k % 2, :, 0:n]
                nc.vector.tensor_tensor(p, p, coef[:].rearrange("p (r o) -> p r o", o=1).to_broadcast([P, H2, n]),
                                        ALU.mult).then_inc(p_ready, 1)

            def outputs(g, it):
                dve.wait_ge(ot_ready, g * NT + it + 1)
                og = m.ogT[:, bass.ds(g * R, R), it * P:(it + 1) * P]
                nc.vector.tensor_tensor(og, OT[:], og, ALU.mult).then_inc(ot_used, 1)

            dve.wait_ge(c_in, 32)
            with dve.Fori(0, KVH) as g:
                maximum(g, 0)
                probabilities(g, 0)
                for k in range(NS):
                    if k + 1 < NS:
                        maximum(g, k + 1)
                    if ends(k - 2):
                        outputs(g, STEPS[k - 2][0])
                    if k + 1 < NS:
                        probabilities(g, k + 1)
                outputs(g, NT - 1)


NSL = (PAST + 1 + 63) // 64
PG = 8
WP = 4
KTP = PG + WP


def nsa_samples(nc, m, a):
    N, G4, Q = NCS, KVH, P // KVH
    NEWEST = PAST
    with Stage(nc) as ctx:
        sb = lambda n, s: ctx.enter_context(nc.sbuf_tensor(f"s_{n}", s, F32))
        ps = lambda n, s: ctx.enter_context(nc.psum_tensor(f"s_{n}", s, F32))
        sem = lambda n: ctx.sem(f"s_{n}")
        groups = lambda ap: ap.rearrange("p (g n) -> p g n", g=G4)
        pt = ctx.enter_context(nc.sbuf_tensor("s_pt", [1, DB * PG], I32))
        A, B, C = (sb(n, [P, 4, 2 * G4 * HD]) for n in "ABC")
        W = m.hT[:].rearrange("p k n -> p (k n)")[:, 0:4 * 2 * G4 * HD].rearrange("p (t n) -> p t n", t=4)
        XT = sb("XT", [P, 2 * G4, PAST])
        flat = XT[:].rearrange("p c n -> p (c n)")
        at = G4 * PAST
        KT = XT[:, 0:G4]
        WT = flat[:, at:at + G4 * WP * P].rearrange("p (g n) -> p g n", g=G4)
        at += G4 * WP * P
        p_s, p_w = flat[:, at:at + PAST + 1], flat[:, at + PAST + 1:at + PAST + WP * P + 2]
        wide = flat[:, at:at + KTP * P].rearrange("p (t g q) -> p (t g) q", g=G4, q=Q)
        at += PAST + WP * P + 2
        pcs = flat[:, at:at + 2 * G4 * N].rearrange("p (c g n) -> p c g n", c=2, g=G4)
        psT, pwT = (flat[:, i * P:(i + n) * P].rearrange("p (t n) -> p t n", n=P) for i, n in ((0, PG), (PG, WP)))
        vs = sb("vs", [DB, 2, G4 * HD])
        group, d8, one_col = sb("group", [P, P]), sb("d8", [P, DB, DB]), sb("one_col", [P, 1])
        smap, blocks = sb("smap", [N, NSL]), sb("blocks", [P, NSL])
        bgT, gb = sb("bgT", [P, 3, DB]), sb("gb", [P, 3])
        sn = sb("sn", [P, 2, DB])
        products = XT[:, 0:2].rearrange("p c (b g q) -> p (c b) g q", g=G4, q=Q)
        bgp = XT[0:DB, 2, 0:3 * P].rearrange("b (r g q) -> b r g q", r=3, g=G4)
        qp = sb("qp", [P, 3, G4, Q])
        ck, cv, ckn = sb("ck", [N, G4, P]), sb("cv", [N, G4 * HD]), sb("ckn", [N, G4, P])
        ckT = sb("ckT", [P, G4, N])
        css, cms, csd, crs = (sb(n, [N, 4]) for n in ("css", "cms", "csd", "crs"))
        ksq = sb("ksq", [P, 2, G4 * HD])
        kss, kms, ksd, krs = (sb(n, [P, KTP, G4]) for n in ("kss", "kms", "ksd", "krs"))
        mx, nmx, den, rden, coef = (sb(n, [P, 3]) for n in ("mx", "nmx", "den", "rden", "coef"))
        pc, pcg, pcT = sb("pc", [P, N]), sb("pcg", [P, N]), sb("pcT", [N, 2, P])
        pn, pnT = sb("pn", [P, 2, DB]), sb("pnT", [DB, 2, P])
        imp, least, at_least = sb("imp", [P, NSL]), sb("least", [P, 1]), sb("at_least", [P, NSL])
        drop, dmask = sb("drop", [P, 1]), sb("dmask", [P, NSL])
        o_sb = sb("o_sb", [P, P])
        X = [ps(f"X{i}", [P, 512]) for i in range(4)]
        SA, SB, MI, OB = (ps(n, [P, 512]) for n in ("SA", "SB", "MI", "OB"))
        SC = MI[:, 2 * P:2 * P + N]
        c_in, a_in, b_in, s0_in, s1_in, w_in = (sem(n) for n in ("c_in", "a_in", "b_in", "s0_in", "s1_in", "w_in"))
        bgp_ready, products_ready, first_ready, first_copied = (
            sem(n) for n in ("bgp_ready", "products_ready", "first_ready", "first_copied"))
        turned, xk_copied, xv_copied, pre_ready, pcs_ready = (
            sem(n) for n in ("turned", "xk_copied", "xv_copied", "pre_ready", "pcs_ready"))
        ck_ready, ck_sq, ck_ms, ck_sd, ckn_ready, tc_ready, ckT_ready, qp_ready = (
            sem(n) for n in ("ck_ready", "ck_sq", "ck_ms", "ck_sd", "ckn_ready", "tc_ready", "ckT_ready", "qp_ready"))
        sc_ready, max_ready, exp_ready, pc_ready, pct_ready, pct_copied, imp_ready, dmask_ready = (
            sem(n) for n in ("sc_ready", "max_ready", "exp_ready", "pc_ready", "pct_ready", "pct_copied", "imp_ready",
                             "dmask_ready"))
        sq_ready, sq_used, kms_ready, ksd_ready, krs_ready, kt_ready, ke_copied, ko_copied = (
            sem(n) for n in ("sq_ready", "sq_used", "kms_ready", "ksd_ready", "krs_ready", "kt_ready", "ke_copied",
                             "ko_copied"))
        s_ready, pw_ready, ps_ready, pwt_ready, pwt_copied, pst_ready, pst_copied = (
            sem(n) for n in ("s_ready", "pw_ready", "ps_ready", "pwt_ready", "pwt_copied", "pst_ready", "pst_copied"))
        wide_ready, norms_ready, norms_copied = sem("wide_ready"), sem("norms_ready"), sem("norms_copied")
        w_used, a_used, o_ready, o_copied, ot_ready = (
            sem(n) for n in ("w_used", "a_used", "o_ready", "o_copied", "ot_ready"))
        block = ctx.enter_context(nc.Block())
        ID = m.ident
        TURN = (4, 5, 6, 7, 0, 1, 2, 3)
        SQUARED = (0, 1, 2, 3, 8, 9, 10, 11, 4, 5, 6, 7)
        tile = lambda i: (C, A, W)[i // 4][:, i % 4]

        @block.sync
        def _(sp):
            def pages(cache, slot, b, first, sem_in):
                for i in range(4):
                    page = sp.value_load(pt[0:1, bass.ds(b * PG + first + i, 1)], min_val=0, max_val=cache.shape[0] - 1)
                    sp.dma_start(slot[:, i], cache[bass.ds(page, 1)].rearrange("a r c g d -> r (a c g d)")
                                 ).then_inc(sem_in, 16)

            def window(b):
                sp.dma_start(W, m.state_l1_win[bass.ds(b, 1)].rearrange("a (t r) c g d -> r (a t) (c g d)", r=P)
                             ).then_inc(w_in, 16)

            sp.dma_start(pt[:], m.page_table.rearrange("(o b) n -> o (b n)", o=1)).then_inc(c_in, 16)
            sp.wait_ge(c_in, 16)
            pages(m.cache_cmp, B, 0, 4, b_in)
            pages(m.cache_cmp, A, 0, 0, a_in)
            for dst, src in ((group, m.c_group), (d8, m.c_d8), (smap, m.c_smap), (blocks, m.c_blocks)):
                sp.dma_start(dst[:], src).then_inc(c_in, 16)
            sp.dma_start(a.w1[:], m.cmp_w1.rearrange("c l d h -> d (c l) h")).then_inc(c_in, 16)
            sp.dma_start(vs[:, 0], m.slc_sample[:, 0, 1].rearrange("b g d -> b (g d)")).then_inc(c_in, 16)
            sp.dma_start(vs[:, 1], m.win_sample[:, 511, 1].rearrange("b g d -> b (g d)")).then_inc(c_in, 16)
            pages(m.cache_slc, C, 0, 0, s0_in)
            window(0)
            with sp.Fori(0, DB - 1) as b:
                sp.wait_ge(c_in, 128)
                sp.wait_ge(turned, b * PG + PG)
                pages(m.cache_slc, A, b, 4, s1_in)
                pages(m.cache_cmp, B, b + 1, 4, b_in)
                sp.wait_ge(w_used, b + 1)
                window(b + 1)
                sp.wait_ge(c_in, 128)
                sp.wait_ge(a_used, b + 1)
                pages(m.cache_cmp, A, b + 1, 0, a_in)
                sp.wait_ge(c_in, 128)
                sp.wait_ge(o_ready, b + 1)
                pages(m.cache_slc, C, b + 1, 0, s0_in)
            sp.wait_ge(turned, DB * PG)
            pages(m.cache_slc, A, DB - 1, 4, s1_in)

        @block.gpsimd
        def _(pool):
            nc.gpsimd.memset(one_col[:], 1.0)
            nc.gpsimd.memset(bgp, 0.0)
            nc.gpsimd.memset(products, 0.0)
            pool.drain()
            nc.gpsimd.tensor_copy(bgp[:, :, :, 0:HPG], a.bg[0:DB, NT].rearrange("b (r g q) -> b r g q", r=3, g=G4)
                                  ).then_inc(bgp_ready, 1)
            for br in range(2):
                for b in range(DB):
                    last = nc.gpsimd.tensor_tensor(products[:, br * DB + b, :, 0:HPG],
                                                   a.qs[:, :, b].rearrange("p (g q) -> p g q", g=G4),
                                                   a.ks[:, br, :, b].rearrange("p (g o) -> p g o", o=1)
                                                   .to_broadcast([P, G4, HPG]), ALU.mult)
            last.then_inc(products_ready, 1)
            with pool.Fori(0, DB) as b:
                for n, i in enumerate(SQUARED):
                    if n == 0:
                        pool.wait_ge(s0_in, b * 64 + 64)
                    if n == 4:
                        pool.wait_ge(w_in, b * 16 + 16)
                    if n == 8:
                        pool.wait_ge(s1_in, b * 64 + 64)
                    pool.wait_ge(sq_used, b * KTP + (n - 1 if n > 0 else 0))
                    k = tile(i)[:, 0:G4 * HD]
                    nc.gpsimd.tensor_tensor(ksq[:, n % 2], k, k, ALU.mult).then_inc(sq_ready, 1)
                pool.wait_ge(krs_ready, b + 1)
                nc.gpsimd.tensor_tensor(wide, krs[:].rearrange("p t (g o) -> p (t g) o", o=1)
                                        .to_broadcast([P, KTP * G4, Q]), one_col[:].rearrange("p (a b) -> p a b", a=1)
                                        .to_broadcast([P, KTP * G4, Q]), ALU.mult).then_inc(wide_ready, 1)

        @block.tensor
        def _(pe):
            pe.wait_ge(bgp_ready, 1)
            pe.wait_ge(products_ready, 1)
            for br in range(3):
                nc.tensor.transpose(MI[:, br * DB:(br + 1) * DB], bgp[:, br].rearrange("b g q -> b (g q)"), ID[0:DB, 0:DB])
            for i in range(2 * DB):
                last = nc.tensor.matmul(MI[:, 3 * DB + i:3 * DB + i + 1], products[:, i].rearrange("p g q -> p (g q)"),
                                        one_col[:], start=True, stop=True)
            last.then_inc(first_ready, 1)
            pe.wait_ge(first_copied, 1)

            def by_group(bank, q, keys):
                for g in range(G4):
                    last = nc.tensor.matmul(bank[g * Q:(g + 1) * Q, :], q[:, g], keys[:, g], start=True, stop=True)
                return last

            def add_values(pT, v, start=False, stop=False):
                for g in range(G4):
                    last = nc.tensor.matmul(OB[g * Q:(g + 1) * Q, 0:HD], pT[:, g * Q:(g + 1) * Q],
                                            v[:, g * HD:(g + 1) * HD], start=start, stop=stop)
                return last

            with pe.Fori(0, DB) as b:
                for n, i in enumerate(TURN):
                    if n == 0:
                        pe.wait_ge(b_in, b * 64 + 64)
                    if n == 4:
                        pe.wait_ge(a_in, b * 64 + 64)
                    if n >= 2:
                        pe.wait_ge(xk_copied, b * PG + n - 1)
                        pe.wait_ge(xv_copied, b * PG + n - 1)
                    src = (A, B)[i // 4][:, i % 4]
                    for cg in range(2 * G4):
                        last = nc.tensor.transpose(X[2 * (n % 2) + cg // G4][:, (cg % G4) * P:(cg % G4 + 1) * P],
                                                   src[:, cg * P:(cg + 1) * P], ID[:])
                    last.then_inc(turned, 1)
                pe.wait_ge(xk_copied, b * PG + PG)
                pe.wait_ge(xv_copied, b * PG + PG)
                pe.wait_ge(c_in, 128)
                for c in range(2):
                    for l in range(CL):
                        last = nc.tensor.matmul(SA[:, c * G4 * N:(c + 1) * G4 * N], a.w1[:, c * CL + l],
                                                XT[:, c * G4:(c + 1) * G4, l:l + CS * (N - 1) + 1:CS],
                                                start=(l == 0), stop=(l == CL - 1))
                last.then_inc(pre_ready, 1)
                for i in range(KTP):
                    if i == 0:
                        pe.wait_ge(s0_in, b * 64 + 64)
                    if i == 4:
                        pe.wait_ge(pcs_ready, b + 1)
                        for c, bank in ((0, SA), (1, SB)):
                            for g in range(G4):
                                last = nc.tensor.matmul(bank[0:N, g * P:(g + 1) * P], pcs[:, c, g], a.w2[:, c],
                                                        start=True, stop=True)
                        last.then_inc(ck_ready, 1)
                        pe.wait_ge(s1_in, b * 64 + 64)
                    if i == 8:
                        pe.wait_ge(w_in, b * 16 + 16)
                    if i >= 4:
                        pe.wait_ge(ko_copied if i % 2 else ke_copied, b * (KTP // 2) + (i - 4) // 2 + 1)
                    for g in range(G4):
                        last = nc.tensor.transpose(X[i % 4][:, g * P:(g + 1) * P], tile(i)[:, g * P:(g + 1) * P], ID[:])
                    last.then_inc(kt_ready, 1)
                pe.wait_ge(c_in, 128)
                pe.wait_ge(ckn_ready, b + 1)
                for g in range(G4):
                    last = nc.tensor.transpose(MI[:, g * N:(g + 1) * N], ckn[:, g], ID[0:N, 0:N])
                last.then_inc(tc_ready, 1)
                pe.wait_ge(c_in, 128)
                pe.wait_ge(ckT_ready, b + 1)
                pe.wait_ge(qp_ready, b + 1)
                by_group(SC, qp[:, 0], ckT[:]).then_inc(sc_ready, 1)
                pe.wait_ge(ke_copied, b * (KTP // 2) + KTP // 2)
                pe.wait_ge(ko_copied, b * (KTP // 2) + KTP // 2)
                pe.wait_ge(wide_ready, b + 1)
                by_group(X[2], qp[:, 2], WT)
                for i in range(KTP):
                    last = nc.tensor.transpose(X[(0, 1, 3)[i // 4]][:, (i % 4) * P:(i % 4 + 1) * P],
                                        wide[:, i * G4:(i + 1) * G4].rearrange("p g q -> p (g q)"), ID[:])
                last.then_inc(norms_ready, 1)
                for h in range(2):
                    last = by_group((SA, SB)[h], qp[:, 1], KT[:, :, h * 512:(h + 1) * 512])
                last.then_inc(s_ready, 1)
                pe.wait_ge(pc_ready, b + 1)
                nc.tensor.matmul(MI[0:N, 0:P], pc[:], group[:], start=True, stop=True)
                nc.tensor.transpose(MI[0:N, P:2 * P], pcg[:], ID[:]).then_inc(pct_ready, 1)
                pe.wait_ge(c_in, 128)
                pe.wait_ge(pct_copied, b + 1)
                nc.tensor.matmul(MI[:, 0:NSL], pcT[:, 0], smap[:], start=True, stop=True).then_inc(imp_ready, 1)
                add_values(pcT[:, 1], cv[:], start=True)
                pe.wait_ge(pw_ready, b + 1)
                for i in range(WP):
                    nc.tensor.transpose(X[2][:, i * P:(i + 1) * P], p_w[:, i * P:(i + 1) * P], ID[:])
                nc.tensor.transpose(X[3][0:DB, 0:P], pn[:, 1], ID[:]).then_inc(pwt_ready, 1)
                pe.wait_ge(pwt_copied, b + 1)
                for i in range(WP):
                    add_values(pwT[:, i], tile(PG + i)[:, G4 * HD:])
                add_values(pnT[:, 1], vs[:, 1]).then_inc(w_used, 1)
                pe.wait_ge(ps_ready, b + 1)
                for i in range(PG):
                    nc.tensor.transpose(X[i // 4][:, (i % 4) * P:(i % 4 + 1) * P], p_s[:, i * P:(i + 1) * P], ID[:])
                nc.tensor.transpose(X[3][0:DB, 0:P], pn[:, 0], ID[:]).then_inc(pst_ready, 1)
                pe.wait_ge(pst_copied, b + 1)
                for i in TURN:
                    last = add_values(psT[:, i], tile(i)[:, G4 * HD:])
                    if i == 7:
                        last.then_inc(a_used, 1)
                add_values(pnT[:, 0], vs[:, 0], stop=True).then_inc(o_ready, 1)
                pe.wait_ge(o_copied, b + 1)
                nc.tensor.transpose(MI[:, 0:P], o_sb[:], ID[:]).then_inc(ot_ready, 1)

        @block.scalar
        def _(act):
            act.wait_ge(c_in, 128)
            with act.Fori(0, DB) as b:
                def keys(i):
                    act.wait_ge(kt_ready, b * KTP + i + 1)
                    at = (KT if i < PG else WT)[:, :, (i % PG) * P:(i % PG + 1) * P]
                    nc.scalar.copy(at, groups(X[i % 4][:])).then_inc(ke_copied, 1)

                def exponentials(k, p, s):
                    act.wait_ge(max_ready, 3 * b + k + 1)
                    nc.scalar.activation(p, s, ACT.Exp, bias=nmx[:, k:k + 1], accum_out=den[:, k:k + 1]
                                         ).then_inc(exp_ready, 1)

                for n, i in enumerate(TURN):
                    act.wait_ge(turned, b * PG + n + 1)
                    if n == 0:
                        act.wait_ge(s_ready, b)
                    nc.scalar.copy(XT[:, 0:G4, i * P:(i + 1) * P], groups(X[2 * (n % 2)][:])).then_inc(xk_copied, 1)
                act.wait_ge(pre_ready, b + 1)
                for c in range(2):
                    last = nc.scalar.activation(pcs[:, c].rearrange("p g n -> p (g n)"),
                                                SA[:, c * G4 * N:(c + 1) * G4 * N], ACT.Silu, bias=a.bias[:, c:c + 1])
                last.then_inc(pcs_ready, 1)
                keys(0)
                keys(2)
                act.wait_ge(ck_ready, b + 1)
                nc.scalar.copy(ck[:].rearrange("n g d -> n (g d)"), SA[0:N, :])
                nc.scalar.copy(cv[:], SB[0:N, :])
                act.drain()
                nc.scalar.activation(ckn[:], ck[:], ACT.Square).then_inc(ck_sq, 1)
                keys(4)
                act.wait_ge(ck_ms, b + 1)
                nc.scalar.activation(csd[:], cms[:], ACT.Sqrt).then_inc(ck_sd, 1)
                act.wait_ge(kms_ready, b + 1)
                nc.scalar.activation(ksd[:], kms[:], ACT.Sqrt).then_inc(ksd_ready, 1)
                for i in (6, 8, 10):
                    keys(i)
                act.wait_ge(tc_ready, b + 1)
                nc.scalar.activation(ckT[:].rearrange("p g n -> p (g n)"), MI[:, 0:G4 * N], ACT.Copy,
                                     scale=a.gain[:, 1:2]).then_inc(ckT_ready, 1)
                exponentials(0, pc[:], SC)
                act.wait_ge(norms_ready, b + 1)
                nc.scalar.copy(p_w[:, 0:WP * P], X[3][:])
                for h in range(2):
                    last = nc.scalar.copy(p_s[:, h * 512:(h + 1) * 512], X[h][:])
                last.then_inc(norms_copied, 1)
                exponentials(1, p_w, p_w)
                act.wait_ge(pwt_ready, b + 1)
                nc.scalar.copy(pwT.rearrange("p t n -> p (t n)"), X[2][:])
                nc.scalar.copy(pnT[:, 1], X[3][0:DB, 0:P]).then_inc(pwt_copied, 1)
                exponentials(2, p_s, p_s)
                act.wait_ge(pst_ready, b + 1)
                for h in range(2):
                    nc.scalar.copy(psT[:, 4 * h:4 * h + 4].rearrange("p t n -> p (t n)"), X[h][:])
                nc.scalar.copy(pnT[:, 0], X[3][0:DB, 0:P]).then_inc(pst_copied, 1)
                act.wait_ge(o_ready, b + 1)
                nc.scalar.copy(o_sb[:], OB[:, 0:HD]).then_inc(o_copied, 1)

        @block.vector
        def _(dve):
            nc.vector.memset(qp[:], 0.0)
            dve.wait_ge(c_in, 128)
            dve.wait_ge(first_ready, 1)
            nc.vector.tensor_copy(bgT[:].rearrange("h r b -> h (r b)"), MI[:, 0:3 * DB])
            nc.vector.tensor_copy(sn[:].rearrange("h r b -> h (r b)"), MI[:, 3 * DB:5 * DB]).then_inc(first_copied, 1)
            dve.drain()
            with dve.Fori(0, DB) as b:
                one = bass.ds(b, 1)

                def keys(i):
                    dve.wait_ge(kt_ready, b * KTP + i + 1)
                    at = (KT if i < PG else WT)[:, :, (i % PG) * P:(i % PG + 1) * P]
                    nc.vector.tensor_copy(at, groups(X[i % 4][:])).then_inc(ko_copied, 1)

                def maximum(k, s):
                    nc.vector.tensor_reduce(mx[:, k:k + 1], s, axis=AX, op=ALU.max)
                    dve.drain()
                    nc.vector.tensor_scalar(nmx[:, k:k + 1], mx[:, k:k + 1], -1.0, LOW, ALU.mult, ALU.min
                                            ).then_inc(max_ready, 1)

                def shares(k, gate):
                    dve.wait_ge(exp_ready, 3 * b + k + 1)
                    nc.vector.reciprocal(rden[:, k:k + 1], den[:, k:k + 1])
                    dve.drain()
                    nc.vector.tensor_tensor(coef[:, k:k + 1], rden[:, k:k + 1], gb[:, gate:gate + 1], ALU.mult)
                    dve.drain()

                def probabilities(k, gate, br, p, n, done):
                    shares(k, gate)
                    nc.vector.tensor_scalar(pn[:, br], d8[:, one].rearrange("p a b -> p (a b)"), p[:, n:n + 1],
                                            coef[:, k:k + 1], ALU.mult, ALU.mult)
                    nc.vector.tensor_scalar(p[:, 0:n], p[:, 0:n], coef[:, k:k + 1], None, ALU.mult).then_inc(done, 1)

                q = a.qs[:, :, one].rearrange("p (g r) b -> p g (r b)", g=G4)
                nc.vector.tensor_copy(qp[:, 0, :, 0:HPG], q)
                nc.vector.tensor_scalar(qp[:, 1, :, 0:HPG], q, a.gain[:, 2:3], None, ALU.mult)
                nc.vector.tensor_scalar(qp[:, 2, :, 0:HPG], q, a.gain[:, 3:4], None, ALU.mult).then_inc(qp_ready, 1)
                nc.vector.tensor_copy(gb[:], bgT[:, :, one].rearrange("h r b -> h (r b)"))
                for n, i in enumerate(TURN):
                    dve.wait_ge(turned, b * PG + n + 1)
                    nc.vector.tensor_copy(XT[:, G4:2 * G4, i * P:(i + 1) * P], groups(X[2 * (n % 2) + 1][:])
                                          ).then_inc(xv_copied, 1)
                for n, i in enumerate(SQUARED):
                    dve.wait_ge(sq_ready, b * KTP + n + 1)
                    nc.vector.tensor_reduce(kss[:, i], groups(ksq[:, n % 2]), axis=AX, op=ALU.add).then_inc(sq_used, 1)
                dve.drain()
                nc.vector.tensor_scalar(kms[:], kss[:], 1.0 / HD, EPS, ALU.mult, ALU.add).then_inc(kms_ready, 1)
                dve.wait_ge(pre_ready, b + 1)
                keys(1)
                keys(3)
                dve.wait_ge(ck_sq, b + 1)
                nc.vector.tensor_reduce(css[:], ckn[:], axis=AX, op=ALU.add)
                dve.drain()
                nc.vector.tensor_scalar(cms[:], css[:], 1.0 / HD, EPS, ALU.mult, ALU.add).then_inc(ck_ms, 1)
                keys(5)
                dve.wait_ge(ck_sd, b + 1)
                nc.vector.reciprocal(crs[:], csd[:])
                dve.drain()
                nc.vector.tensor_tensor(ckn[:], ck[:], crs[:].rearrange("n (g o) -> n g o", o=1)
                                        .to_broadcast([N, G4, P]), ALU.mult).then_inc(ckn_ready, 1)
                dve.wait_ge(ksd_ready, b + 1)
                nc.vector.reciprocal(krs[:], ksd[:]).then_inc(krs_ready, 1)
                for i in (7, 9, 11):
                    keys(i)
                dve.wait_ge(sc_ready, b + 1)
                maximum(0, SC)
                shares(0, 0)
                nc.vector.tensor_scalar(pcg[:], pc[:], coef[:, 0:1], None, ALU.mult)
                dve.drain()
                nc.vector.tensor_scalar(pc[:], pc[:], rden[:, 0:1], None, ALU.mult).then_inc(pc_ready, 1)
                n = WP * P
                dve.wait_ge(s_ready, b + 1)
                nc.vector.tensor_copy(p_w[:, n:n + 1], sn[:, 1, one])
                dve.wait_ge(norms_copied, b + 1)
                nc.vector.tensor_tensor(p_w[:, 0:n], X[2][:], p_w[:, 0:n], ALU.mult)
                dve.wait_ge(pct_ready, b + 1)
                nc.vector.tensor_copy(pcT[:].rearrange("n r h -> n (r h)"), MI[0:N, 0:2 * P]).then_inc(pct_copied, 1)
                dve.drain()
                maximum(1, p_w)
                for h in range(2):
                    nc.vector.tensor_tensor(p_s[:, h * 512:(h + 1) * 512], (SA, SB)[h][:],
                                            p_s[:, h * 512:(h + 1) * 512], ALU.mult)
                probabilities(1, 2, 1, p_w, n, pw_ready)
                dve.wait_ge(imp_ready, b + 1)
                nc.vector.tensor_copy(imp[:], MI[:, 0:NSL])
                dve.drain()
                nc.vector.tensor_reduce(least[:], imp[:, 1:NSL - 2], axis=AX, op=ALU.min)
                dve.drain()
                nc.vector.scalar_tensor_tensor(at_least[:, 1:NSL - 2], imp[:, 1:NSL - 2], least[:], blocks[:, 1:NSL - 2],
                                               ALU.is_le, ALU.mult)
                dve.drain()
                nc.vector.tensor_reduce(drop[:], at_least[:, 1:NSL - 2], axis=AX, op=ALU.max)
                dve.drain()
                nc.vector.tensor_scalar(dmask[:], blocks[:], drop[:], NEG, ALU.is_equal, ALU.mult)
                dve.drain()
                by_block = p_s[:, 0:PAST].rearrange("p (j n) -> p j n", n=64)
                nc.vector.tensor_tensor(by_block, by_block, dmask[:, 0:NSL - 1].rearrange("p (j o) -> p j o", o=1)
                                        .to_broadcast([P, NSL - 1, 64]), ALU.add)
                nc.vector.tensor_copy(p_s[:, NEWEST:NEWEST + 1], sn[:, 0, one])
                dve.drain()
                maximum(2, p_s)
                probabilities(2, 1, 0, p_s, PAST, ps_ready)
                dve.wait_ge(ot_ready, b + 1)
                og = m.ogT[:, :, bass.ds(SEQ + b, 1)].rearrange("p (g r) b -> p g (r b)", g=G4)
                nc.vector.tensor_tensor(og, MI[:, 0:P].rearrange("p (g q) -> p g q", q=Q)[:, :, 0:HPG], og, ALU.mult)


def sparse_attention(nc, m):
    a = Mem()
    with ExitStack() as outer:
        def alloc(ctx, name, shape):
            return ctx.enter_context(nc.sbuf_tensor("a_" + name, shape, F32))

        a.gain = alloc(outer, "gain", [P, 4])
        a.bg = alloc(outer, "bg", [P, TT, 3 * NH])
        a.w2 = alloc(outer, "w2", [P, 2, P])
        a.peT = alloc(outer, "peT", [P, 2 * CL])
        a.bias = alloc(outer, "bias", [P, 2])
        a.qs = alloc(outer, "qs", [P, NH, DB])
        a.ks = alloc(outer, "ks", [P, 2, KVH, DB])
        with ExitStack() as ctx:
            a.qT = alloc(ctx, "qT", [P, NH, TOK])
            a.skT = alloc(ctx, "skT", [P, KVH, TOK])
            a.wkT = alloc(ctx, "wkT", [P, KVH, TOK])
            a.sv = alloc(ctx, "sv", [P, TT, KVH * HD])
            a.wv = alloc(ctx, "wv", [P, TT, KVH * HD])
            a.XT = alloc(ctx, "XT", [P, 2 * KVH, SEQ])
            nsa_project(nc, m, a)
            a.ckT = alloc(ctx, "ckT", [P, KVH, NCP])
            a.cv = alloc(ctx, "cv", [P, KVH * HD])
            with ExitStack() as wctx:
                a.w1 = alloc(wctx, "w1", [P, 2 * CL, P])
                nsa_compress(nc, m, a)
            nsa_prompt(nc, m, a)
        a.w1 = outer.enter_context(nc.sbuf_tensor("a_w1_again", [P, 2 * CL, P], F32))
        nsa_samples(nc, m, a)


def sparse_inputs(m, x, give):
    cols = [[(512 * g, 512 * (g + 1))] for g in range(QP + KVP)]
    gate = DI + 3 * 2 * KVH * HD
    cols += [[(gate + 512 * g, gate + 512 * (g + 1))] for g in range(GP)]
    w = x["l1_w_in"]
    m.w_in[1] = give("l1_w_in", by_columns(w, cols))
    b = w[:, gate + DI:].reshape(KM, P, NH, 3).transpose(1, 0, 3, 2).reshape(P, KM, 3 * NH)
    m.w1_bgate = give("l1_w_bgate", b)
    m.c_gain = give("l1_qk_norm", x["l1_qk_norm"].T)
    m.c_peT = give("l1_cmp_pe", x["l1_cmp_pe"].transpose(2, 1, 0).reshape(HD, 2 * CL))
    m.cmp_w1, m.cmp_w2 = give("l1_cmp_w1", x["l1_cmp_w1"]), give("l1_cmp_w2", x["l1_cmp_w2"])
    m.state_l1_win = give("state_l1_win", x["state_l1_win"])
    m.cache_cmp = give("cache_l1_cmp", x["cache_l1_cmp"])
    m.cache_slc = give("cache_l1_slc", x["cache_l1_slc"])
    m.page_table = give("page_table", x["page_table"])
    line, block = np.arange(P), np.arange(NSL)
    Q = P // KVH
    same = (line[:, None] // Q == line[None, :] // Q) & (line[:, None] % Q < HPG)
    m.c_group = give("c_group", same.astype(np.float32))
    n, lo = np.arange(NCS)[:, None], block[None, :] * 64
    over = np.minimum(n * CS + CL, lo + 64) - np.maximum(n * CS, lo)
    m.c_smap = give("c_smap", (np.maximum(over, 0) / CS).astype(np.float32))
    m.c_blocks = give("c_blocks", np.broadcast_to(block.astype(np.float32), (P, NSL)))
    i = np.arange(P)
    m.c_causal = give("c_causal", np.where(i[None, :] <= i[:, None], 0.0, NEG).astype(np.float32))
    pos, end = np.arange(SEQ).reshape(NT, P), np.arange(NCP) * CS + CL - 1
    m.c_cmask = give("c_cmask", np.where(end <= pos[..., None], 0.0, NEG).astype(np.float32).transpose(1, 0, 2))


LEVELS = 7
EG, ONE, BETA, BG, EKD, GCUM, LA, EGL = range(8)
NPAR = 8


def gdn_decays(nc, m, d):
    with Stage(nc) as ctx:
        sb = lambda n, s: ctx.enter_context(nc.sbuf_tensor(f"gd_{n}", s, F32))
        ps = lambda n, s: ctx.enter_context(nc.psum_tensor(f"gd_{n}", s, F32))
        sem = lambda n: ctx.sem(f"gd_{n}")
        wab = sb("wab", [P, KM, 2 * GH])
        alog, dtb, nea = sb("alog", [P, GH]), sb("dtb", [P, GH]), sb("nea", [P, GH])
        x, nx, ex, sp_ = (sb(n, [P, TT, GH]) for n in ("x", "nx", "ex", "sp"))
        gl, dif = sb("gl", [P, NT, GH]), sb("dif", [P, NT, GH])
        ones, e8h = sb("ones", [P, P]), sb("e8h", [DB, GH, DB])
        AB = ps("AB", [P, TT, 2 * GH])
        GC, GL, EB = ps("GC", [P, 512]), ps("GL", [P, 512]), ps("EB", [P, 512])
        c_in, ab_ready, cleared, x_ready, ex_ready, ln_ready = (
            sem(n) for n in ("c_in", "ab_ready", "cleared", "x_ready", "ex_ready", "ln_ready"))
        nea_ready, la_ready, g_ready, dif_ready, e_ready, eb_in, eb_ready, beta_ready, g_used = (
            sem(n) for n in ("nea_ready", "la_ready", "g_ready", "dif_ready", "e_ready", "eb_in", "eb_ready", "beta_ready",
                             "g_used"))
        block = ctx.enter_context(nc.Block())
        tab = d.tab

        @block.sync
        def _(sp):
            sp.dma_start(wab[:], m.w2_ab).then_inc(c_in, 16)
            sp.dma_start(alog[:], m.A_log.rearrange("(o h) -> o h", o=1).to_broadcast([P, GH])).then_inc(c_in, 16)
            sp.dma_start(dtb[:], m.dt_bias.rearrange("(o h) -> o h", o=1).to_broadcast([P, GH])).then_inc(c_in, 16)
            sp.dma_start(d.ut[:], m.c_ut).then_inc(c_in, 16)

        @block.tensor
        def _(pe):
            pe.wait_ge(c_in, 64)
            for t in range(TT):
                mt = P if t < NT else DB
                for k in range(KM):
                    last = nc.tensor.matmul(AB[0:mt, t], m.hT[:, k, t * P:t * P + mt], wab[:, k],
                                            start=(k == 0), stop=(k == KM - 1))
            last.then_inc(ab_ready, 1)
            pe.wait_ge(la_ready, 1)
            la = tab[:, LA, 0:NT].rearrange("p t h -> p (t h)")
            nc.tensor.matmul(GC[:, 0:NT * GH], d.ut[:], la, start=True, stop=True)
            nc.tensor.matmul(GL[:, 0:NT * GH], ones[:], la, start=True, stop=True).then_inc(g_ready, 1)
            pe.wait_ge(eb_in, 1)
            nc.tensor.matmul(EB[:, 0:GH * DB], ones[0:DB], e8h[:].rearrange("a h b -> a (h b)"), start=True,
                             stop=True).then_inc(eb_ready, 1)

        @block.scalar
        def _(act):
            act.wait_ge(c_in, 64)
            nc.scalar.activation(nea[:], alog[:], ACT.Exp).then_inc(nea_ready, 1)
            act.wait_ge(x_ready, 1)
            nc.scalar.activation(ex[:], nx[:], ACT.Exp)
            act.drain()
            nc.scalar.activation(ex[:], ex[:], ACT.Ln, bias=1.0).then_inc(ln_ready, 1)
            act.wait_ge(dif_ready, 1)
            nc.scalar.activation(tab[:, EKD, 0:NT], dif[:], ACT.Exp)
            nc.scalar.activation(tab[:, EGL, 0:NT], gl[:], ACT.Exp)
            nc.scalar.activation(tab[:, EG], tab[:, GCUM], ACT.Exp).then_inc(e_ready, 1)
            nc.scalar.activation(tab[:, BETA, 0:NT], AB[:, 0:NT, GH:2 * GH], ACT.Sigmoid)
            nc.scalar.activation(tab[0:DB, BETA, NT], AB[0:DB, NT, GH:2 * GH], ACT.Sigmoid).then_inc(beta_ready, 1)

        @block.vector
        def _(dve):
            nc.vector.memset(tab[:], 1.0)
            nc.vector.memset(x[:], 0.0)
            nc.vector.memset(ones[:], 1.0)
            dve.drain()
            dve.wait_ge(ab_ready, 1)
            b = dtb[:].rearrange("p (o h) -> p o h", o=1)
            nc.vector.tensor_tensor(x[:, 0:NT], AB[:, 0:NT, 0:GH], b.to_broadcast([P, NT, GH]), ALU.add)
            nc.vector.tensor_tensor(x[0:DB, NT], AB[0:DB, NT, 0:GH], dtb[0:DB], ALU.add)
            dve.drain()
            nc.vector.tensor_scalar(nx[:], x[:], -1.0, None, ALU.mult)
            dve.drain()
            nc.vector.tensor_tensor(nx[:], nx[:], x[:], ALU.min).then_inc(x_ready, 1)
            dve.wait_ge(ln_ready, 1)
            nc.vector.scalar_tensor_tensor(sp_[:], x[:], 0.0, ex[:], ALU.max, ALU.add)
            dve.wait_ge(nea_ready, 1)
            dve.drain()
            nc.vector.scalar_tensor_tensor(tab[:, LA], sp_[:], -1.0, nea[:].rearrange("p (o h) -> p o h", o=1)
                                           .to_broadcast([P, TT, GH]), ALU.mult, ALU.mult).then_inc(la_ready, 1)
            dve.drain()
            nc.vector.tensor_copy(tab[:, GCUM, NT], tab[:, LA, NT])
            dve.wait_ge(g_ready, 1)
            nc.vector.tensor_copy(tab[:, GCUM, 0:NT], GC[:, 0:NT * GH].rearrange("p (t h) -> p t h", t=NT))
            nc.vector.tensor_copy(gl[:], GL[:, 0:NT * GH].rearrange("p (t h) -> p t h", t=NT))
            dve.drain()
            nc.vector.tensor_tensor(dif[:], gl[:], tab[:, GCUM, 0:NT], ALU.subtract).then_inc(dif_ready, 1)
            dve.wait_ge(e_ready, 1)
            nc.vector.tensor_tensor(e8h[:], tab[0:DB, EG, NT].rearrange("a (h o) -> a h o", o=1).to_broadcast([DB, GH, DB]),
                                    m.ident[0:DB, 0:DB].rearrange("a (o b) -> a o b", o=1).to_broadcast([DB, GH, DB]),
                                    ALU.mult).then_inc(eb_in, 1)
            dve.wait_ge(beta_ready, 1)
            nc.vector.tensor_tensor(tab[:, BG], tab[:, BETA], tab[:, EG], ALU.mult)
            dve.wait_ge(eb_ready, 1)
            nc.vector.tensor_copy(d.egb[:].rearrange("p h b -> p (h b)"), EB[:, 0:GH * DB])


def gated_delta(nc, m):
    d = Mem()
    with ExitStack() as ctx:
        def alloc(name, shape):
            return ctx.enter_context(nc.sbuf_tensor("d_" + name, shape, F32))

        d.tab = alloc("tab", [P, NPAR, TT, GH])
        d.egb = alloc("egb", [P, GH, DB])
        d.ut = alloc("ut", [P, P])
        gdn_decays(nc, m, d)
        gdn_heads(nc, m, d)


def gdn_heads(nc, m, d):
    with Stage(nc) as ctx:
        sb = lambda n, s: ctx.enter_context(nc.sbuf_tensor(f"g_{n}", s, F32))
        pb = lambda n: ctx.enter_context(nc.psum_tensor(f"g_{n}", [P, 512], F32))
        sem = lambda n: ctx.sem(f"g_{n}")
        two = lambda n: [sem(f"{n}{e}") for e in range(2)]
        four = lambda ap: ap.rearrange("p (c n) -> p c n", c=NT)
        bc = lambda ap, n: ap.rearrange("p (c o) -> p c o", o=1).to_broadcast([ap.shape[0], ap.shape[1], n])
        PB = [pb("P0"), pb("P1")]
        X = [[pb(f"X{e}{i}") for i in range(3)] for e in range(2)]
        w = sb("w", [P, 4, KM, P])
        cw = sb("cw", [P, GH, 13])
        mneg = sb("mneg", [P, P])
        lvl = sb("lvl", [P, LEVELS, P])
        d8, ones = sb("d8", [P, DB, DB]), sb("ones", [P, P])
        km = sb("km", [DB, DB, P])
        zs = sb("zs", [P, P])
        cs = sb("cs", [3 * DB, 2, 3, P])
        state = sb("state", [P, 2, DB, P])
        zT = sb("zT", [P, 2, 3, 3 + TOK])
        cvo = sb("cvo", [3 + DB, 2, 3, P])
        EB = []
        for e in range(2):
            b = Mem()
            b.par, b.hw = sb(f"par{e}", [P, NPAR, TT]), sb(f"hw{e}", [P, 13])
            b.cT = sb(f"cT{e}", [P, 3, TOK])
            b.csx, b.cpr = sb(f"csx{e}", [P, 3, 4, DB]), sb(f"cpr{e}", [P, 3, 4, DB])
            b.ss, b.ms, b.sd, b.rs = (sb(f"{n}{e}", [P, 2, TT]) for n in ("ss", "ms", "sd", "rs"))
            b.oss, b.oms, b.osd, b.ors = (sb(f"{n}{e}", [P, TT]) for n in ("oss", "oms", "osd", "ors"))
            b.cf = sb(f"cf{e}", [P, 6, TT])
            b.tk = sb(f"tk{e}", [P, 6, NT, P])
            b.vb = sb(f"vb{e}", [P, NT, P])
            b.stok = sb(f"stok{e}", [DB, 3, P])
            b.sqs, b.qks, b.us = sb(f"sqs{e}", [DB, 2, P]), sb(f"qks{e}", [DB, 2, P]), sb(f"us{e}", [DB, P])
            b.qkT = sb(f"qkT{e}", [P, 4, NT, P])
            b.qkTs, b.qkm = sb(f"qkTs{e}", [P, 2, DB]), sb(f"qkm{e}", [P, 2, DB, DB])
            b.BT = sb(f"BT{e}", [P, 2, NT, P])
            b.S = sb(f"S{e}", [P, NT, P])
            b.sq = b.tk[:, 4:6]
            b.ltab, b.BT1 = b.BT[:, 0], b.BT[:, 1]
            b.T, b.U, b.P1 = (four(b.cT[:, i, 0:SEQ]) for i in range(3))
            b.LT, b.att, b.dt, b.nsk = (b.tk[:, i] for i in range(4))
            b.u, b.on, b.ons = b.qkT[:, 1], b.qkT[:, 2], b.us
            EB.append(b)
        w_in, zs_ready, zs_copied, zst_ready, zst_copied, z_ready, z_copied = (
            sem(n) for n in ("w_in", "zs_ready", "zs_copied", "zst_ready", "zst_copied", "z_ready", "z_copied"))
        c_in, shifted, cleared = sem("c_in"), sem("shifted"), sem("cleared")
        cs_in, st_in, st_out, S_out, cv_out = (two(n) for n in ("cs_in", "st_in", "st_out", "S_out", "cv_out"))
        cst_ready, cst_used, cvo_ready, cvo_copied, conv_ready, silu_ready = (
            two(n) for n in ("cst_ready", "cst_used", "cvo_ready", "cvo_copied", "conv_ready", "silu_ready"))
        tok_ready, stok_copied, v_ready, sq_ready, ms_ready, sd_ready, scaled, kt_ready, kt_copied = (
            two(n) for n in ("tok_ready", "stok_copied", "v_ready", "sq_ready", "ms_ready", "sd_ready", "scaled",
                             "kt_ready", "kt_copied"))
        par_ready, ltab_ready, dg_ready, qg_copied, qkm_ready, dgm_ready, dt_ready, kk_ready, lt_ready, b1_ready = (
            two(n) for n in ("par_ready", "ltab_ready", "dg_ready", "qg_copied", "qkm_ready", "dgm_ready", "dt_ready",
                             "kk_ready", "lt_ready", "b1_ready"))
        bt_ready, bts_ready, tu_ready, p1_ready, p1_copied, lv_ready, solk_ready, nsk_ready = (
            two(n) for n in ("bt_ready", "bts_ready", "tu_ready", "p1_ready", "p1_copied", "lv_ready", "solk_ready",
                             "nsk_ready"))
        u_ready, u_copied, sp_ready, S_ready, o_ready = (
            two(n) for n in ("u_ready", "u_copied", "sp_ready", "S_ready", "o_ready"))
        sgs_ready, ks_ready, us_ready, outer_ready, sn_ready, os_ready = (
            two(n) for n in ("sgs_ready", "ks_ready", "us_ready", "outer_ready", "sn_ready", "os_ready"))
        osq_ready, oms_ready, osd_ready, on_ready, ont_ready, og_ready = (
            two(n) for n in ("osq_ready", "oms_ready", "osd_ready", "on_ready", "ont_ready", "og_ready"))
        block = ctx.enter_context(nc.Block())
        NL = LEVELS - 1
        NPAIR = GH // 2
        FS = (3, 0, 1, 2)

        def slots(eng, slot):
            slot(None, 0)
            with eng.Fori(0, NPAIR - 1) as p:
                slot(p, p + 1)
            slot(NPAIR - 1, None)

        conv_in = m.state_l2_conv.rearrange("b j (c h n) -> j b c h n", c=3, h=GH)
        conv_s = m.conv_sample.rearrange("b j (c h n) -> b j c h n", c=3, h=GH)
        conv_p = m.conv_prompt[0].rearrange("j (c h n) -> j c h n", c=3, h=GH)

        @block.sync
        def _(sp):
            for dst, src in ((cw, m.c_conv), (mneg, m.c_mneg), (lvl, m.c_lvl), (d8, m.c_d8)):
                sp.dma_start(dst[:], src).then_inc(c_in, 16)
            sp.dma_start(w[:], m.w_in[2][0]).then_inc(w_in, 16)
            with sp.Fori(0, GH - 1) as h:
                sp.wait_ge(zs_ready, h + 1)
                sp.dma_start(w[:], m.w_in[2][bass.ds(h + 1, 1)].rearrange("a p f k n -> p (a f) k n")).then_inc(w_in, 16)

        @block.gpsimd
        def _(pool):
            nc.gpsimd.memset(ones[:], 1.0)
            nc.gpsimd.memset(zT[:], 0.0).then_inc(cleared, 1)
            pool.dma_start(m.conv_sample[:, 0:2], m.state_l2_conv[:, 1:3]).then_inc(shifted, 16)

            def load(e, one):
                for j in range(3):
                    pool.dma_start(cs[j * DB:(j + 1) * DB, e], conv_in[j, :, :, one].rearrange("b c a n -> b (c a) n")
                                   ).then_inc(cs_in[e], 16)
                pool.dma_start(state[:, e], m.state_l2_gdn[:, one].rearrange("b a k v -> k (b a) v")).then_inc(st_in[e], 16)

            def early(p, e):
                b = EB[e]
                pool.wait_ge(par_ready[e], p + 1)
                nc.gpsimd.tensor_tensor(b.ltab, d.ut[:].rearrange("p (o n) -> p o n", o=1).to_broadcast([P, NT, P]),
                                        bc(b.par[:, LA, 0:NT], P), ALU.mult).then_inc(ltab_ready[e], 1)

            def level(p, e, li):
                b = EB[e]
                if li == 0:
                    pool.wait_ge(lt_ready[e], p + 1)
                    pool.wait_ge(dg_ready[e], p + 1)
                elif li == 1:
                    pool.wait_ge(tu_ready[e], LEVELS * p + 1)
                else:
                    pool.wait_ge(p1_ready[e], NL * p + li - 1)
                nc.gpsimd.tensor_tensor(b.BT[:, li % 2], b.LT, lvl[:, li + 1:li + 2].to_broadcast([P, NT, P]),
                                        ALU.mult).then_inc(bts_ready[e], 1)

            def stores(p, e, one):
                pool.wait_ge(c_in, 64)
                pool.wait_ge(cvo_copied[e], p + 1)
                pool.dma_start(conv_p[:, :, one].rearrange("j c a n -> j (c a) n"), cvo[0:3, e]).then_inc(cv_out[e], 16)
                pool.dma_start(conv_s[:, 2, :, one].rearrange("b c a n -> b (c a) n"), cvo[3:3 + DB, e]
                               ).then_inc(cv_out[e], 16)

            def late_stores(p, e, one):
                pool.wait_ge(c_in, 64)
                pool.wait_ge(S_ready[e], NT * p + NT)
                pool.dma_start(row(m.gdn_prompt[0, one]), EB[e].S[:, NT - 1]).then_inc(S_out[e], 16)
                pool.wait_ge(c_in, 64)
                pool.wait_ge(sn_ready[e], p + 1)
                pool.dma_start(m.gdn_sample[:, one].rearrange("b a k v -> k (b a) v"), state[:, e]).then_inc(st_out[e], 16)

            def mix(p, last):
                one = [bass.ds(2 * p + e, 1) for e in range(2)]
                for e in range(2):
                    early(p, e)
                for e in range(2):
                    stores(p, e, one[e])
                for li in range(NL):
                    for e in range(2):
                        level(p, e, li)
                for e in range(2):
                    late_stores(p, e, one[e])
                if not last:
                    for e in range(2):
                        pool.wait_ge(c_in, 64)
                        pool.wait_ge(st_out[e], 16 * p + 16)
                        pool.wait_ge(os_ready[e], p + 1)
                        load(e, bass.ds(2 * p + 2 + e, 1))

            for e in range(2):
                load(e, bass.ds(e, 1))
            pool.wait_ge(c_in, 64)
            with pool.Fori(0, NPAIR - 1) as p:
                mix(p, False)
            mix(NPAIR - 1, True)
            for e in range(2):
                pool.wait_ge(st_out[e], 16 * NPAIR)
                pool.wait_ge(S_out[e], 16 * NPAIR)
                pool.wait_ge(cv_out[e], 32 * NPAIR)
            pool.wait_ge(shifted, 16)

        @block.tensor
        def _(pe):
            ID = m.ident

            def project(q, e, i):
                if q is None:
                    return
                h = 2 * q + e
                if i == 0:
                    pe.wait_ge(w_in, h * 16 + 16)
                    pe.wait_ge(zs_copied, h)
                elif i == 1:
                    pe.wait_ge(zst_copied, h)
                else:
                    pe.wait_ge(z_copied, 4 * h + i - 1)
                for k in range(KM):
                    last = nc.tensor.matmul(PB[i % 2][:], w[:, FS[i], k], m.hT[:, k, 0:SEQ], start=(k == 0),
                                            stop=(k == KM - 1))
                last.then_inc(z_ready, 1)

            def project_samples(q, e):
                if q is None:
                    return
                h = 2 * q + e
                pe.wait_ge(z_copied, 4 * h + 3)
                for k in range(KM):
                    for f in range(4):
                        last = nc.tensor.matmul(PB[0][32 * f:32 * f + DB, 0:P], m.hT[:, k, SEQ:TOK], w[:, f, k],
                                                start=(k == 0), stop=(k == KM - 1))
                last.then_inc(zs_ready, 1)

            def turn_samples(q, e):
                if q is None:
                    return
                h = 2 * q + e
                pe.wait_ge(zs_copied, h + 1)
                pe.wait_ge(z_copied, 4 * h + 4)
                nc.tensor.transpose(PB[1][:, 0:P], zs[:], ID[:]).then_inc(zst_ready, 1)

            def conv_rows(p, e):
                pe.wait_ge(cs_in[e], p * 48 + 48)
                pe.wait_ge(og_ready[e], p)
                pe.wait_ge(zst_copied, 2 * p + e + 1)
                for c in range(3):
                    last = nc.tensor.transpose(X[e][1][0:3 + DB, c * P:(c + 1) * P], zT[:, e, c, SEQ:SEQ + 3 + DB], ID[:])
                last.then_inc(cvo_ready[e], 1)
                for c in range(3):
                    last = nc.tensor.transpose(X[e][0][:, c * 3 * DB:(c + 1) * 3 * DB], cs[:, e, c], ID[0:3 * DB, 0:3 * DB])
                last.then_inc(cst_ready[e], 1)

            def tokens(p, e):
                b = EB[e]
                pe.wait_ge(silu_ready[e], p + 1)
                pe.wait_ge(cst_used[e], p + 1)
                pe.wait_ge(cvo_copied[e], p + 1)
                for c in range(3):
                    nc.tensor.transpose(X[e][2][0:DB, c * P:(c + 1) * P], b.cT[:, c, SEQ:TOK], ID[:])
                for c in range(2):
                    for t in range(NT):
                        last = nc.tensor.transpose(X[e][c][:, t * P:(t + 1) * P], b.cT[:, c, t * P:(t + 1) * P], ID[:])
                last.then_inc(tok_ready[e], 1)

            def tokens_v(p, e):
                b = EB[e]
                pe.wait_ge(stok_copied[e], p + 1)
                for t in range(NT):
                    last = nc.tensor.transpose(X[e][2][:, t * P:(t + 1) * P], b.cT[:, 2, t * P:(t + 1) * P], ID[:])
                last.then_inc(v_ready[e], 1)

            def turned_back(p, e):
                b = EB[e]
                pe.wait_ge(scaled[e], p + 1)
                for bank, i in ((0, 2), (1, 3), (2, 1)):
                    for t in range(NT):
                        last = nc.tensor.transpose(X[e][bank][:, t * P:(t + 1) * P], b.tk[:, i, t], ID[:])
                last.then_inc(kt_ready[e], 1)

            def decays(p, e):
                b = EB[e]
                pe.wait_ge(kt_copied[e], p + 1)
                for t in range(NT):
                    nc.tensor.transpose(X[e][0][:, t * P:(t + 1) * P], b.tk[:, 0, t], ID[:])
                for i in range(2):
                    nc.tensor.transpose(X[e][2][:, i * DB:(i + 1) * DB], b.qks[:, i], ID[0:DB, 0:DB])
                pe.wait_ge(ltab_ready[e], p + 1)
                nc.tensor.matmul(X[e][1][:], ones[:], b.ltab.rearrange("p c n -> p (c n)"), start=True, stop=True
                                 ).then_inc(dg_ready[e], 1)

            def scores(p, e):
                b = EB[e]
                pe.wait_ge(qg_copied[e], p + 1)
                pe.wait_ge(dgm_ready[e], p + 1)
                for t in range(NT):
                    nc.tensor.matmul(X[e][0][:, t * P:(t + 1) * P], b.qkT[:, 2, t], b.qkT[:, 3, t], start=True, stop=True)
                    last = nc.tensor.matmul(X[e][1][:, t * P:(t + 1) * P], b.qkT[:, 2, t], b.qkT[:, 1, t],
                                            start=True, stop=True)
                last.then_inc(kk_ready[e], 1)

            def first_blocks(p, e):
                b = EB[e]
                pe.wait_ge(b1_ready[e], p + 1)
                pe.wait_ge(qkm_ready[e], p + 1)
                for t in range(NT):
                    last = nc.tensor.transpose(X[e][2][:, t * P:(t + 1) * P], b.BT1[:, t], ID[:])
                last.then_inc(bt_ready[e], 1)

            def level_a(p, e, li):
                b = EB[e]
                pe.wait_ge(tu_ready[e], LEVELS * p + li + 1)
                pe.wait_ge(bts_ready[e], NL * p + li + 1)
                for t in range(NT):
                    last = nc.tensor.matmul(X[e][0][:, t * P:(t + 1) * P], b.BT[:, li % 2, t], b.T[:, t], start=True, stop=True)
                last.then_inc(p1_ready[e], 1)

            def level_b(p, e, li):
                b = EB[e]
                pe.wait_ge(p1_copied[e], NL * p + li + 1)
                for t in range(NT):
                    last = nc.tensor.matmul(X[e][1][:, t * P:(t + 1) * P], b.P1[:, t], b.U[:, t], start=True, stop=True)
                if li < NL - 1:
                    for t in range(NT):
                        last = nc.tensor.matmul(X[e][2][:, t * P:(t + 1) * P], b.U[:, t], b.P1[:, t], start=True, stop=True)
                last.then_inc(lv_ready[e], 1)

            def solve_keys(p, e):
                b = EB[e]
                pe.wait_ge(tu_ready[e], LEVELS * p + LEVELS)
                for t in range(NT):
                    last = nc.tensor.matmul(X[e][0][:, t * P:(t + 1) * P], b.tk[:, 4, t], b.U[:, t], start=True, stop=True)
                last.then_inc(solk_ready[e], 1)

            def chunk_a(p, e, c):
                b = EB[e]
                if c == 0:
                    pe.wait_ge(nsk_ready[e], p + 1)
                else:
                    pe.wait_ge(S_ready[e], NT * p + c)
                cc = slice(c * P, (c + 1) * P)
                last = nc.tensor.matmul(X[e][1][:, cc], b.U[:, c], b.vb[:, c], start=True, stop=(c == 0))
                if c > 0:
                    last = nc.tensor.matmul(X[e][1][:, cc], b.nsk[:, c], b.S[:, c - 1], start=False, stop=True)
                last.then_inc(u_ready[e], 1)

            def chunk_b(p, e, c):
                b = EB[e]
                cc = slice(c * P, (c + 1) * P)
                pe.wait_ge(u_copied[e], NT * p + c + 1)
                nc.tensor.matmul(X[e][1][:, cc], b.tk[:, 5, c], b.u[:, c], start=True, stop=True).then_inc(sp_ready[e], 1)
                last = nc.tensor.matmul(X[e][2][:, cc], b.att[:, c], b.u[:, c], start=True, stop=(c == 0))
                if c > 0:
                    last = nc.tensor.matmul(X[e][2][:, cc], b.qkT[:, 0, c], b.S[:, c - 1], start=False, stop=True)
                if c == NT - 1:
                    last.then_inc(o_ready[e], 1)

            def samples_a(p, e):
                b = EB[e]
                pe.wait_ge(sgs_ready[e], p + 1)
                for n in range(DB):
                    last = nc.tensor.matmul(X[e][0][0:DB, 0:P], b.qkm[:, 1, n], state[:, e, n], start=(n == 0),
                                            stop=(n == DB - 1))
                last.then_inc(ks_ready[e], 1)

            def samples_b(p, e):
                b = EB[e]
                pe.wait_ge(us_ready[e], p + 1)
                pe.wait_ge(S_ready[e], NT * p + NT)
                for n in range(DB):
                    last = nc.tensor.matmul(X[e][n // 4][:, (n % 4) * P:(n % 4 + 1) * P], km[:, n], b.us[:],
                                            start=True, stop=True)
                last.then_inc(outer_ready[e], 1)

            def samples_c(p, e):
                b = EB[e]
                pe.wait_ge(sn_ready[e], p + 1)
                for n in range(DB):
                    last = nc.tensor.matmul(X[e][0][0:DB, 0:P], b.qkm[:, 0, n], state[:, e, n], start=(n == 0),
                                            stop=(n == DB - 1))
                last.then_inc(os_ready[e], 1)

            def outputs(p, e):
                b = EB[e]
                pe.wait_ge(on_ready[e], p + 1)
                for t in range(NT):
                    nc.tensor.transpose(X[e][1][:, t * P:(t + 1) * P], b.on[:, t], ID[:])
                nc.tensor.transpose(X[e][0][:, 0:DB], b.ons[:], ID[0:DB, 0:DB]).then_inc(ont_ready[e], 1)

            def slot(p, q):
                def mix(step, e, *a):
                    if p is not None:
                        step(p, e, *a)

                def both(step, *a):
                    mix(step, 0, *a)
                    mix(step, 1, *a)

                both(conv_rows)
                project(q, 0, 0)
                mix(tokens, 0)
                project(q, 0, 1)
                mix(tokens, 1)
                both(tokens_v)
                project(q, 0, 2)
                mix(turned_back, 0)
                project(q, 0, 3)
                mix(turned_back, 1)
                both(decays)
                project_samples(q, 0)
                both(scores)
                both(first_blocks)
                for li in range(NL):
                    both(level_a, li)
                    if li == 0:
                        turn_samples(q, 0)
                    if li == 1:
                        project(q, 1, 0)
                    both(level_b, li)
                    if li == 3:
                        project(q, 1, 1)
                both(solve_keys)
                project(q, 1, 2)
                for c in range(NT):
                    both(chunk_a, c)
                    if c == 0:
                        both(samples_a)
                    both(chunk_b, c)
                both(samples_b)
                project(q, 1, 3)
                both(samples_c)
                project_samples(q, 1)
                turn_samples(q, 1)
                both(outputs)

            pe.wait_ge(cleared, 1)
            slots(pe, slot)

        @block.scalar
        def _(act):
            def projected(q, e, i):
                if q is None:
                    return
                h = 2 * q + e
                act.wait_ge(z_ready, 4 * h + i + 1)
                if FS[i] == 3:
                    nc.scalar.activation(m.ogT[:, bass.ds(h, 1), 0:SEQ].rearrange("p a n -> p (a n)"), PB[i % 2][:],
                                         ACT.Silu).then_inc(z_copied, 1)
                else:
                    if i == 1:
                        act.wait_ge(conv_ready[e], 4 * q)
                        act.wait_ge(cvo_ready[e], q)
                    nc.scalar.copy(zT[:, e, FS[i], 3:3 + SEQ], PB[i % 2][:]).then_inc(z_copied, 1)

            def projected_samples(q, e):
                if q is None:
                    return
                h = 2 * q + e
                act.wait_ge(zs_ready, h + 1)
                act.wait_ge(zst_ready, h)
                nc.scalar.copy(zs[:], PB[0][:, 0:P]).then_inc(zs_copied, 1)

            def turned_samples(q, e):
                if q is None:
                    return
                h = 2 * q + e
                act.wait_ge(zst_ready, h + 1)
                z = four(PB[1][:])[:, 0].rearrange("p (f n) -> p f n", f=4)
                nc.scalar.copy(zT[:, e, :, 3 + SEQ:3 + TOK], z[:, 0:3, 0:DB])
                nc.scalar.activation(m.ogT[:, bass.ds(h, 1), SEQ:TOK].rearrange("p a n -> p (a n)"), z[:, 3, 0:DB],
                                     ACT.Silu).then_inc(zst_copied, 1)

            def conv_out(p, e):
                act.wait_ge(cvo_ready[e], p + 1)
                act.wait_ge(cv_out[e], 32 * p)
                nc.scalar.copy(cvo[:, e].rearrange("r c n -> r (c n)"), X[e][1][0:3 + DB, 0:3 * P]).then_inc(cvo_copied[e], 1)

            def silu(p, e):
                b = EB[e]
                for c in range(3):
                    act.wait_ge(conv_ready[e], 4 * p + c + 1)
                    nc.scalar.activation(b.cT[:, c, 0:SEQ], b.cT[:, c, 0:SEQ], ACT.Silu)
                act.wait_ge(conv_ready[e], 4 * p + 4)
                nc.scalar.activation(b.cT[:, :, SEQ:TOK], b.cT[:, :, SEQ:TOK], ACT.Silu).then_inc(silu_ready[e], 1)

            def squares(p, e):
                b = EB[e]
                act.wait_ge(tok_ready[e], p + 1)
                nc.scalar.copy(b.stok[:], X[e][2][0:DB, 0:3 * P].rearrange("b (c n) -> b c n", c=3)
                               ).then_inc(stok_copied[e], 1)
                for c in range(2):
                    nc.scalar.activation(b.sq[:, c], four(X[e][c][:]), ACT.Square)
                act.drain()
                nc.scalar.activation(b.sqs[:], b.stok[:, 0:2], ACT.Square).then_inc(sq_ready[e], 1)

            def root(p, e):
                act.wait_ge(ms_ready[e], p + 1)
                nc.scalar.activation(EB[e].sd[:], EB[e].ms[:], ACT.Sqrt).then_inc(sd_ready[e], 1)

            def turned_back(p, e):
                act.wait_ge(kt_ready[e], p + 1)
                for bank, i in ((0, 2), (1, 3), (2, 1)):
                    last = nc.scalar.copy(EB[e].qkT[:, i], four(X[e][bank][:]))
                last.then_inc(kt_copied[e], 1)

            def decays(p, e):
                b = EB[e]
                act.wait_ge(dg_ready[e], p + 1)
                nc.scalar.copy(b.qkT[:, 0], four(X[e][0][:])).then_inc(qg_copied[e], 1)

            def exps(p, e):
                b = EB[e]
                act.wait_ge(dgm_ready[e], p + 1)
                nc.scalar.activation(b.dt, b.dt, ACT.Exp).then_inc(dt_ready[e], 1)

            def level(p, e, li):
                act.wait_ge(p1_ready[e], NL * p + li + 1)
                nc.scalar.copy(EB[e].P1, four(X[e][0][:])).then_inc(p1_copied[e], 1)

            def solve_keys(p, e):
                act.wait_ge(solk_ready[e], p + 1)
                nc.scalar.mul(EB[e].nsk, four(X[e][0][:]), -1.0).then_inc(nsk_ready[e], 1)

            def chunk(p, e, c):
                act.wait_ge(u_ready[e], NT * p + c + 1)
                nc.scalar.copy(EB[e].u[:, c], X[e][1][:, c * P:(c + 1) * P]).then_inc(u_copied[e], 1)

            def out_squares(p, e):
                b = EB[e]
                act.wait_ge(o_ready[e], p + 1)
                act.wait_ge(os_ready[e], p + 1)
                nc.scalar.activation(b.sq[:, 0], four(X[e][2][:]), ACT.Square)
                nc.scalar.activation(b.sqs[:, 0], X[e][0][0:DB, 0:P], ACT.Square).then_inc(osq_ready[e], 1)

            def out_root(p, e):
                act.wait_ge(oms_ready[e], p + 1)
                nc.scalar.activation(EB[e].osd[:], EB[e].oms[:], ACT.Sqrt).then_inc(osd_ready[e], 1)

            def slot(p, q):
                def mix(step, e, *a):
                    if p is not None:
                        step(p, e, *a)

                def both(step, *a):
                    mix(step, 0, *a)
                    mix(step, 1, *a)

                both(conv_out)
                mix(silu, 0)
                projected(q, 0, 0)
                mix(silu, 1)
                projected(q, 0, 1)
                both(squares)
                both(root)
                projected(q, 0, 2)
                mix(turned_back, 0)
                projected(q, 0, 3)
                mix(turned_back, 1)
                both(decays)
                projected_samples(q, 0)
                both(exps)
                for li in range(NL):
                    both(level, li)
                    if li == 0:
                        turned_samples(q, 0)
                    if li == 1:
                        projected(q, 1, 0)
                    if li == 3:
                        projected(q, 1, 1)
                both(solve_keys)
                projected(q, 1, 2)
                for c in range(NT):
                    both(chunk, c)
                projected(q, 1, 3)
                both(out_squares)
                both(out_root)
                projected_samples(q, 1)
                turned_samples(q, 1)

            act.wait_ge(cleared, 1)
            slots(act, slot)

        @block.vector
        def _(dve):
            dve.wait_ge(c_in, 64)
            for b in EB:
                nc.vector.memset(b.ss[:], 1.0)
                nc.vector.memset(b.oss[:], 1.0)
            dve.drain()
            idb = m.ident[:].rearrange("p (o n) -> p o n", o=1).to_broadcast([P, NT, P])

            def parameters(p, e):
                b, one = EB[e], bass.ds(2 * p + e, 1)
                nc.vector.tensor_copy(b.par[:], d.tab[:, :, :, one].rearrange("p a t h -> p a (t h)")
                                      ).then_inc(par_ready[e], 1)
                nc.vector.tensor_copy(b.hw[:], cw[:, one].rearrange("p h n -> p (h n)"))

            def conv(p, e, c):
                b = EB[e]
                dve.wait_ge(zst_copied, 2 * p + e + 1)
                y = b.cT[:, c, 0:SEQ]
                last = nc.vector.tensor_scalar(y, zT[:, e, c, 0:SEQ], b.hw[:, 4 * c:4 * c + 1], None, ALU.mult)
                for j in range(1, 4):
                    dve.drain()
                    last = nc.vector.scalar_tensor_tensor(y, zT[:, e, c, j:j + SEQ], b.hw[:, 4 * c + j:4 * c + j + 1], y,
                                                          ALU.mult, ALU.add)
                last.then_inc(conv_ready[e], 1)

            def conv_samples(p, e):
                b = EB[e]
                dve.wait_ge(cst_ready[e], p + 1)
                nc.vector.tensor_copy(b.csx[:, :, 0:3], X[e][0][:, 0:9 * DB].rearrange("p (c j b) -> p c j b", c=3, j=3)
                                      ).then_inc(cst_used[e], 1)
                nc.vector.tensor_copy(b.csx[:, :, 3], zT[:, e, :, 3 + SEQ:3 + TOK])
                dve.drain()
                nc.vector.tensor_tensor(b.cpr[:].rearrange("p c j b -> p (c j) b"), b.csx[:].rearrange("p c j b -> p (c j) b"),
                                        bc(b.hw[:, 0:12], DB), ALU.mult)
                dve.drain()
                nc.vector.tensor_reduce(b.cT[:, :, SEQ:TOK], b.cpr[:].rearrange("p c j b -> p c b j"), axis=AX, op=ALU.add
                                        ).then_inc(conv_ready[e], 1)

            def sums(p, e):
                b = EB[e]
                dve.wait_ge(sq_ready[e], p + 1)
                nc.vector.tensor_reduce(b.ss[:, :, 0:NT], b.sq, axis=AX, op=ALU.add)
                nc.vector.tensor_reduce(b.ss[0:DB, :, NT], b.sqs[:], axis=AX, op=ALU.add)
                dve.drain()
                nc.vector.tensor_scalar(b.ms[:], b.ss[:], EPS, None, ALU.add).then_inc(ms_ready[e], 1)

            def scale(p, e):
                b = EB[e]
                dve.wait_ge(sd_ready[e], p + 1)
                nc.vector.reciprocal(b.rs[:], b.sd[:])
                dve.drain()
                nc.vector.tensor_scalar(b.rs[:, 0], b.rs[:, 0], P ** -0.5, None, ALU.mult)
                dve.drain()
                nc.vector.tensor_tensor(b.cf[:, 0:2], b.par[:, EG:ONE + 1], b.rs[:, 0:1].to_broadcast([P, 2, TT]), ALU.mult)
                nc.vector.tensor_tensor(b.cf[:, 2:6], b.par[:, ONE:EKD + 1], b.rs[:, 1:2].to_broadcast([P, 4, TT]), ALU.mult)
                dve.drain()
                for i in range(6):
                    nc.vector.tensor_tensor(b.tk[:, i], four(X[e][0 if i < 2 else 1][:]), bc(b.cf[:, i, 0:NT], P), ALU.mult)
                nc.vector.tensor_scalar(b.qks[:, 0], b.stok[:, 0], b.cf[0:DB, 1, NT:TT], None, ALU.mult)
                nc.vector.tensor_scalar(b.qks[:, 1], b.stok[:, 1], b.cf[0:DB, 2, NT:TT], None, ALU.mult)
                dve.wait_ge(v_ready[e], p + 1)
                nc.vector.tensor_tensor(b.vb[:], four(X[e][2][:]), bc(b.par[:, BETA, 0:NT], P), ALU.mult
                                        ).then_inc(scaled[e], 1)

            def decay_state(p, e):
                dve.wait_ge(st_in[e], p * 16 + 16)
                one = bass.ds(2 * p + e, 1)
                nc.vector.tensor_tensor(state[:, e], state[:, e], bc(d.egb[:, one].rearrange("p h b -> p (h b)"), P),
                                        ALU.mult).then_inc(sgs_ready[e], 1)

            def decays(p, e):
                b = EB[e]
                dve.wait_ge(dg_ready[e], p + 1)
                nc.vector.tensor_tensor(b.dt, four(X[e][1][:]), bc(b.par[:, GCUM, 0:NT], P), ALU.subtract)
                nc.vector.tensor_copy(b.qkTs[:].rearrange("p i b -> p (i b)"), X[e][2][:, 0:2 * DB])
                dve.drain()
                nc.vector.scalar_tensor_tensor(b.dt, b.dt, 0.0, mneg[:].rearrange("p (o n) -> p o n", o=1)
                                               .to_broadcast([P, NT, P]), ALU.min, ALU.add).then_inc(dgm_ready[e], 1)
                for i in range(2):
                    last = nc.vector.tensor_tensor(b.qkm[:, i], b.qkTs[:, i:i + 1].to_broadcast([P, DB, DB]), d8[:], ALU.mult)
                last.then_inc(qkm_ready[e], 1)

            def scores(p, e):
                b = EB[e]
                dve.wait_ge(dt_ready[e], p + 1)
                dve.wait_ge(kk_ready[e], p + 1)
                nc.vector.tensor_tensor(b.LT, four(X[e][0][:]), b.dt, ALU.mult).then_inc(lt_ready[e], 1)
                nc.vector.tensor_tensor(b.att, four(X[e][1][:]), b.dt, ALU.mult)
                dve.drain()
                nc.vector.tensor_tensor(b.BT1, b.LT, lvl[:, 0:1].to_broadcast([P, NT, P]), ALU.mult).then_inc(b1_ready[e], 1)
                dve.drain()
                nc.vector.tensor_tensor(b.U, idb, b.BT1, ALU.subtract)

            def first_blocks(p, e):
                b = EB[e]
                dve.wait_ge(bt_ready[e], p + 1)
                nc.vector.tensor_tensor(b.T, idb, four(X[e][2][:]), ALU.subtract).then_inc(tu_ready[e], 1)

            def level(p, e, li):
                b = EB[e]
                dve.wait_ge(lv_ready[e], NL * p + li + 1)
                last = nc.vector.tensor_tensor(b.U, b.U, four(X[e][1][:]), ALU.subtract)
                if li < NL - 1:
                    last = nc.vector.tensor_tensor(b.T, b.T, four(X[e][2][:]), ALU.subtract)
                last.then_inc(tu_ready[e], 1)

            def chunk(p, e, c):
                b = EB[e]
                dve.wait_ge(sp_ready[e], NT * p + c + 1)
                sp_c = X[e][1][:, c * P:(c + 1) * P]
                if c == 0:
                    dve.wait_ge(S_out[e], 16 * p)
                    nc.vector.tensor_copy(b.S[:, 0], sp_c).then_inc(S_ready[e], 1)
                else:
                    nc.vector.scalar_tensor_tensor(b.S[:, c], b.S[:, c - 1], b.par[:, EGL, c:c + 1], sp_c, ALU.mult,
                                                   ALU.add).then_inc(S_ready[e], 1)

            def samples_a(p, e):
                b = EB[e]
                dve.wait_ge(outer_ready[1 - e], p + e)
                nc.vector.tensor_tensor(km[:], b.qks[:, 1:2].to_broadcast([DB, DB, P]),
                                        m.ident[0:DB, 0:DB].rearrange("a (b o) -> a b o", o=1).to_broadcast([DB, DB, P]),
                                        ALU.mult)
                dve.wait_ge(ks_ready[e], p + 1)
                nc.vector.tensor_tensor(b.us[:], b.stok[:, 2], X[e][0][0:DB, 0:P], ALU.subtract)
                dve.drain()
                nc.vector.tensor_scalar(b.us[:], b.us[:], b.par[0:DB, BETA, NT:TT], None, ALU.mult).then_inc(us_ready[e], 1)

            def samples_b(p, e):
                dve.wait_ge(outer_ready[e], p + 1)
                for q in range(2):
                    st = state[:, e, 4 * q:4 * q + 4]
                    last = nc.vector.tensor_tensor(st, st, four(X[e][q][:]), ALU.add)
                last.then_inc(sn_ready[e], 1)

            def out_sums(p, e):
                b = EB[e]
                dve.wait_ge(osq_ready[e], p + 1)
                nc.vector.tensor_reduce(b.oss[:, 0:NT], b.sq[:, 0], axis=AX, op=ALU.add)
                nc.vector.tensor_reduce(b.oss[0:DB, NT:TT], b.sqs[:, 0], axis=AX, op=ALU.add)
                dve.drain()
                nc.vector.tensor_scalar(b.oms[:], b.oss[:], 1.0 / P, EPS, ALU.mult, ALU.add).then_inc(oms_ready[e], 1)

            def out_scale(p, e):
                b = EB[e]
                dve.wait_ge(osd_ready[e], p + 1)
                nc.vector.reciprocal(b.ors[:], b.osd[:])
                dve.drain()
                nc.vector.tensor_tensor(b.on, four(X[e][2][:]), bc(b.ors[:, 0:NT], P), ALU.mult)
                nc.vector.tensor_scalar(b.ons[:], X[e][0][0:DB, 0:P], b.ors[0:DB, NT:TT], None, ALU.mult
                                        ).then_inc(on_ready[e], 1)

            def outputs(p, e):
                b, one = EB[e], bass.ds(2 * p + e, 1)
                dve.wait_ge(ont_ready[e], p + 1)
                og = m.ogT[:, one, 0:SEQ].rearrange("p h n -> p (h n)")
                nc.vector.scalar_tensor_tensor(og, X[e][1][:], b.hw[:, 12:13], og, ALU.mult, ALU.mult)
                og = m.ogT[:, one, SEQ:TOK].rearrange("p h n -> p (h n)")
                nc.vector.scalar_tensor_tensor(og, X[e][0][:, 0:DB], b.hw[:, 12:13], og, ALU.mult, ALU.mult
                                               ).then_inc(og_ready[e], 1)

            def mix(p):
                def both(step, *a):
                    step(p, 0, *a)
                    step(p, 1, *a)

                dve.drain()
                both(parameters)
                dve.drain()
                for e in range(2):
                    for c in range(3):
                        conv(p, e, c)
                    conv_samples(p, e)
                both(decay_state)
                both(sums)
                both(scale)
                both(decays)
                both(scores)
                both(first_blocks)
                for li in range(NL):
                    both(level, li)
                for c in range(NT):
                    both(chunk, c)
                for e in range(2):
                    samples_a(p, e)
                both(samples_b)
                both(out_sums)
                both(out_scale)
                both(outputs)

            with dve.Fori(0, NPAIR - 1) as p:
                mix(p)
            mix(NPAIR - 1)


def delta_inputs(m, x, give):
    w = x["l2_w_in"]
    v = w[:, 0:4 * DI].reshape(KM, P, 4, GH, P)
    m.w_in[2] = give("l2_w_in", v.transpose(3, 1, 2, 0, 4))
    m.w2_ab = give("l2_w_ab", w[:, 4 * DI:].reshape(KM, P, 2 * GH).transpose(1, 0, 2))
    m.A_log, m.dt_bias = give("l2_A_log", x["l2_A_log"]), give("l2_dt_bias", x["l2_dt_bias"])
    m.state_l2_conv, m.state_l2_gdn = give("state_l2_conv", x["state_l2_conv"]), give("state_l2_gdn", x["state_l2_gdn"])
    taps = x["l2_conv_w"].reshape(4, 3, GH, P).transpose(3, 2, 1, 0).reshape(P, GH, 12)
    m.c_conv = give("l2_conv", np.concatenate([taps, np.broadcast_to(x["l2_onorm"][:, None, None], (P, GH, 1))], 2))
    i = np.arange(P)
    m.c_ut = give("c_ut", (i[:, None] <= i[None, :]).astype(np.float32))
    m.c_mneg = give("c_mneg", np.where(i[:, None] <= i[None, :], 0.0, NEG).astype(np.float32))
    lvl = [(i[None, :] // s % 2 == 1) & (i[:, None] // s == i[None, :] // s - 1) for s in (1 << n for n in range(LEVELS))]
    m.c_lvl = give("c_lvl", np.stack(lvl, 1).astype(np.float32))


def build(nc, m):
    with ExitStack() as ctx:
        sb = lambda n, s: ctx.enter_context(nc.sbuf_tensor(n, s, F32))
        m.xres = sb("xres", [P, TT, DM])
        m.hT = sb("hT", [P, KM, TOK])
        m.ogT = sb("ogT", [P, KI, TOK])
        m.ident = sb("ident", [P, P])
        load_tokens(nc, m)
        mixers = [
            lambda: retention(nc, m, 0, m.state_l0_ret, m.s0_prompt, m.s0_sample, m.w_in[0], m.c_ret[0]),
            lambda: sparse_attention(nc, m),
            lambda: gated_delta(nc, m),
            lambda: retention(nc, m, 3, m.state_l3_ret, m.s3_prompt, m.s3_sample, m.w_in[3], m.c_ret[3]),
        ]
        for layer in range(LAYERS):
            norm_and_transpose(nc, m, layer)
            mixers[layer]()
            output_projection(nc, m, layer)
        store_tokens(nc, m)


def retention_constants():
    out = np.zeros((RH, P, 2 * P + 3), np.float32)
    i = np.arange(P, dtype=np.float64)
    for h in range(RH):
        lg = np.log1p(-np.exp2(-5.0 - h))
        diff = i[None, :] - i[:, None]
        out[h, :, 0:P] = np.where(diff >= 0, np.exp(lg * np.maximum(diff, 0)), 0)
        out[h, :, P:2 * P] = np.exp(lg * (i + 1))[None, :]
        out[h, :, 2 * P] = np.exp(lg * (P - 1 - i))
        out[h, :, 2 * P + 1] = np.exp(lg * P)
        out[h, :, 2 * P + 2] = np.exp(lg)
    return out


def rope_constants(past):
    half = RK // 2
    inv = (np.float32(10000.0) ** (-np.arange(half, dtype=np.float32) / half)).astype(np.float32)
    pos = np.zeros((TT, P), np.float32)
    pos[:NT] = np.arange(SEQ).reshape(NT, P)
    pos[NT] = past
    ang = (pos[..., None] * inv).astype(np.float32).astype(np.float64)
    c, s = np.cos(ang), np.sin(ang)
    sc = RK ** -0.5
    cos = np.concatenate([c, c, c * sc, c * sc], -1)
    sin = np.concatenate([-s, s, -s * sc, s * sc], -1)
    return np.ascontiguousarray(np.stack([cos, sin], 2).transpose(1, 0, 2, 3), dtype=np.float32)


def by_columns(w, pieces):
    v = w.reshape(w.shape[0] // P, P, w.shape[1]).transpose(1, 0, 2)
    return np.stack([np.concatenate([v[:, :, a:b] for a, b in unit], 2) for unit in pieces])


def kernel(**inputs):
    import concourse.bacc as bacc
    from concourse.bass_utils import run_bass_kernel_spmd as run

    x = {k: np.asarray(v) for k, v in inputs.items()}
    nc = bacc.Bacc("TRN2", target_bir_lowering=False, num_devices=1)
    arrays = {}
    m = Mem()

    def give(name, a):
        a = np.ascontiguousarray(a)
        arrays["in_" + name] = a
        return nc.dram_tensor("in_" + name, a.shape, mybir.dt.from_np(a.dtype), kind="ExternalInput").ap()

    outs = []

    def take(*shape):
        name = f"out_{len(outs)}"
        outs.append(name)
        return nc.dram_tensor(name, shape, F32, kind="ExternalOutput").ap()

    m.x_prompt, m.x_sample = give("x_prompt", x["x_prompt"]), give("x_sample", x["x_sample"])
    m.state_l0_ret, m.state_l3_ret = give("state_l0_ret", x["state_l0_ret"]), give("state_l3_ret", x["state_l3_ret"])
    m.norm = [give(f"l{i}_norm", x[f"l{i}_norm"]) for i in range(4)]
    m.w_out = [give(f"l{i}_w_out", x[f"l{i}_w_out"]) for i in range(4)]
    m.w_in, m.c_ret = {}, {}
    heads = [[(RK * h, RK * (h + 1)), (DM + RK * h, DM + RK * (h + 1)), (2 * DM + RV * h, 2 * DM + RV * (h + 1)),
              (2 * DM + DI + RV * h, 2 * DM + DI + RV * (h + 1))] for h in range(RH)]
    for i in (0, 3):
        m.w_in[i] = give(f"l{i}_w_in", by_columns(x[f"l{i}_w_in"], heads))
        gn = x[f"l{i}_gn"].reshape(RH, 2, P).transpose(0, 2, 1)
        m.c_ret[i] = give(f"c_ret{i}", np.concatenate([retention_constants(), gn], 2))
    m.c_ident = give("c_ident", np.eye(P, dtype=np.float32))
    m.c_rope = give("c_rope", rope_constants(1024))
    e = np.eye(DB, dtype=np.float32)
    m.c_d8 = give("c_d8", np.broadcast_to(e, (P, DB, DB)))
    m.c_e8 = give("c_e8", np.broadcast_to(e[:, :, None], (DB, DB, P)))
    sparse_inputs(m, x, give)
    delta_inputs(m, x, give)
    m.y_prompt, m.y_sample = take(1, SEQ, DM), take(DB, 1, DM)
    m.s0_prompt, m.s0_sample = take(1, RH, RK, RV), take(DB, RH, RK, RV)
    m.cmp_prompt, m.cmp_sample = take(1, SEQ, 2, KVH, HD), take(DB, 1, 2, KVH, HD)
    m.slc_prompt, m.slc_sample = take(1, SEQ, 2, KVH, HD), take(DB, 1, 2, KVH, HD)
    m.win_prompt, m.win_sample = take(1, SEQ, 2, KVH, HD), take(DB, 512, 2, KVH, HD)
    m.conv_prompt, m.conv_sample = take(1, 3, 3 * DI), take(DB, 3, 3 * DI)
    m.gdn_prompt, m.gdn_sample = take(1, GH, 128, 128), take(DB, GH, 128, 128)
    m.s3_prompt, m.s3_sample = take(1, RH, RK, RV), take(DB, RH, RK, RV)
    build(nc, m)
    r = run(nc, [arrays], core_ids=[0])
    return tuple(r.results[0][n] for n in outs)
```
